# Optimizing a Trainium2 kernel written in Bass

```python
import jax, jax.numpy as jnp
from jax import lax
import numpy as np

D_MODEL = 1024
BATCH = 1
SEQ = 512
DEPTH = 2
DEC_BATCH = 1
DEC_SEQ = 32
PAST_LEN = 256

CHUNK = 64
HEAD_DIM = 128
H_SB = 4
H_FOX = 4
H_DSA = 8
KV_DSA = 2
H_IDX = 4
D_IDX = 64
TOPK_MAX = 256
N_GROUPS = 4
EXPERTS_PER_GROUP = 4
N_EXPERTS = N_GROUPS * EXPERTS_PER_GROUP
TOPK_IN_GROUP = 2
D_EXPERT = 256
ROPE_THETA = 10000.0
EPS = 1e-6
Q_BLOCK = 128
DSA_Q_BLOCK = 64
FORGET_BIAS_INIT = 3.0

AB_SPLITS = (H_SB * HEAD_DIM,) * 3 + (H_FOX * HEAD_DIM,) * 3 + (H_FOX,)
DSA_SPLITS = (H_DSA * HEAD_DIM, KV_DSA * HEAD_DIM, KV_DSA * HEAD_DIM, H_IDX * D_IDX, D_IDX, H_IDX)

kernel_name = 'hybrid_stickbreak_fox_dsa_hmoe_stream'

def split_cols(a, sizes):
    cuts = [int(c) for c in np.cumsum(sizes)[:-1]]
    return jnp.split(a, cuts, axis=-1)

def rms_norm(x, g):
    xf = x.astype(jnp.float32)
    y = xf * lax.rsqrt(jnp.mean(xf * xf, axis=-1, keepdims=True) + EPS)
    return (y * g.astype(jnp.float32)).astype(x.dtype)

def rotary(x, pos):
    half = x.shape[-1] // 2
    inv_freq = ROPE_THETA ** (-jnp.arange(half, dtype=jnp.float32) / half)
    ang = pos.astype(jnp.float32)[:, None] * inv_freq[None, :]
    cos = jnp.cos(ang)[None, :, None, :]
    sin = jnp.sin(ang)[None, :, None, :]
    xf = x.astype(jnp.float32)
    x1, x2 = xf[..., :half], xf[..., half:]
    return jnp.concatenate([x1 * cos - x2 * sin, x2 * cos + x1 * sin], axis=-1).astype(x.dtype)

def sweep_queries(fn, q_arrays, q_pos, block):
    T = q_pos.shape[0]
    blk = block if T % block == 0 else T
    nb = T // blk

    def split(a):
        return jnp.moveaxis(a.reshape(a.shape[0], nb, blk, *a.shape[2:]), 1, 0)

    def body(args):
        arrs, qp = args
        return fn(*arrs, qp)

    out = lax.map(body, (tuple(split(a) for a in q_arrays), q_pos.reshape(nb, blk)))
    out = jnp.moveaxis(out, 0, 1)
    return out.reshape(out.shape[0], T, *out.shape[3:])

def stick_breaking_block(q, k, v, q_pos, k_pos):
    z = jnp.einsum('bqhd,bkhd->bhqk', q, k, preferred_element_type=jnp.float32) * HEAD_DIM ** -0.5
    mask = k_pos[None, :] < q_pos[:, None]
    log_1m = jnp.where(mask, jax.nn.log_sigmoid(-z), 0.0)
    between = lax.cumsum(log_1m, axis=3, reverse=True) - log_1m
    log_a = jnp.where(mask, jax.nn.log_sigmoid(z) + between, -jnp.inf)
    a = jnp.exp(log_a)
    return jnp.einsum('bhqk,bkhd->bqhd', a.astype(v.dtype), v)

def forgetting_block(q, fq, k, v, fk, q_pos, k_pos):
    s = jnp.einsum('bqhd,bkhd->bhqk', q, k, preferred_element_type=jnp.float32) * HEAD_DIM ** -0.5
    s = s + jnp.swapaxes(fq, 1, 2)[:, :, :, None] - jnp.swapaxes(fk, 1, 2)[:, :, None, :]
    mask = k_pos[None, :] <= q_pos[:, None]
    p = jax.nn.softmax(jnp.where(mask, s, -jnp.inf), axis=-1)
    return jnp.einsum('bhqk,bkhd->bqhd', p.astype(v.dtype), v)

def mixer_ab(h, past, w_in, b_forget, w_out):
    B, T, _ = h.shape
    proj = jnp.einsum('btd,de->bte', h, w_in)
    q_sb, k_sb, v_sb, q_fx, k_fx, v_fx, f_logit = split_cols(proj, AB_SPLITS)
    q_sb = q_sb.reshape(B, T, H_SB, HEAD_DIM)
    k_sb = k_sb.reshape(B, T, H_SB, HEAD_DIM)
    v_sb = v_sb.reshape(B, T, H_SB, HEAD_DIM)
    q_fx = q_fx.reshape(B, T, H_FOX, HEAD_DIM)
    k_fx = k_fx.reshape(B, T, H_FOX, HEAD_DIM)
    v_fx = v_fx.reshape(B, T, H_FOX, HEAD_DIM)
    logf = jax.nn.log_sigmoid((f_logit + b_forget).astype(jnp.float32))
    rows = (k_sb, v_sb, k_fx, v_fx, logf)
    if past is None:
        keys = rows
    else:
        keys = tuple(jnp.concatenate([c, r], axis=1) for c, r in zip(past, rows))
    K_sb, V_sb, K_fx, V_fx, logf_all = keys
    L = K_sb.shape[1]
    k_pos = jnp.arange(L)
    q_pos = (L - T) + jnp.arange(T)
    F_all = lax.cumsum(logf_all.astype(jnp.float32), axis=1)
    F_q = F_all[:, L - T:]
    o_sb = sweep_queries(lambda q, qp: stick_breaking_block(q, K_sb, V_sb, qp, k_pos), (q_sb,), q_pos, Q_BLOCK)
    o_fx = sweep_queries(lambda q, fq, qp: forgetting_block(q, fq, K_fx, V_fx, F_all, qp, k_pos), (q_fx, F_q), q_pos, Q_BLOCK)
    o = jnp.concatenate([o_sb.reshape(B, T, -1), o_fx.reshape(B, T, -1).astype(o_sb.dtype)], axis=-1)
    return jnp.einsum('bte,ed->btd', o, w_out), rows

def mixer_dsa(h, past, w_in, w_out):
    B, T, _ = h.shape
    proj = jnp.einsum('btd,de->bte', h, w_in)
    q, k, v, q_idx, k_idx, w_idx = split_cols(proj, DSA_SPLITS)
    L = T if past is None else past[0].shape[1] + T
    q_pos = (L - T) + jnp.arange(T)
    q = rotary(q.reshape(B, T, H_DSA, HEAD_DIM), q_pos)
    k = rotary(k.reshape(B, T, KV_DSA, HEAD_DIM), q_pos)
    v = v.reshape(B, T, KV_DSA, HEAD_DIM)
    q_idx = rotary(q_idx.reshape(B, T, H_IDX, D_IDX), q_pos)
    k_idx = rotary(k_idx[:, :, None, :], q_pos)[:, :, 0, :]
    rows = (k, v, k_idx)
    if past is None:
        K, V, KI = rows
    else:
        K, V, KI = tuple(jnp.concatenate([c, r], axis=1) for c, r in zip(past, rows))
    k_chunk = jnp.arange(L) // CHUNK
    k_sel = min(TOPK_MAX, L // 4)

    def block(qb, qib, wib, qp):
        nq = qb.shape[1]
        q_chunk = qp // CHUNK
        logits = jnp.einsum('bqhe,bke->bqhk', qib, KI, preferred_element_type=jnp.float32) * D_IDX ** -0.5
        score = jnp.einsum('bqhk,bqh->bqk', jax.nn.relu(logits), wib.astype(jnp.float32) * H_IDX ** -0.5)
        score = jnp.where(k_chunk[None, None, :] <= q_chunk[None, :, None], score, -jnp.inf)
        _, idx = lax.top_k(score, k_sel)
        valid = (idx // CHUNK) <= q_chunk[None, :, None]
        k_g = jax.vmap(lambda kk, ii: kk[ii])(K, idx)
        v_g = jax.vmap(lambda vv, ii: vv[ii])(V, idx)
        qg = qb.reshape(B, nq, KV_DSA, H_DSA // KV_DSA, HEAD_DIM)
        s = jnp.einsum('bqgrd,bqkgd->bqgrk', qg, k_g, preferred_element_type=jnp.float32) * HEAD_DIM ** -0.5
        p = jax.nn.softmax(jnp.where(valid[:, :, None, None, :], s, -jnp.inf), axis=-1)
        o = jnp.einsum('bqgrk,bqkgd->bqgrd', p.astype(v_g.dtype), v_g)
        return o.reshape(B, nq, H_DSA, HEAD_DIM)

    o = sweep_queries(block, (q, q_idx, w_idx), q_pos, DSA_Q_BLOCK)
    return jnp.einsum('bte,ed->btd', o.reshape(B, T, -1), w_out), rows

def moe_tokens(h, w_group, w_router, w_gate, w_up, w_down):
    g_logits = jnp.einsum('nd,dg->ng', h, w_group, preferred_element_type=jnp.float32)
    g_sel = jnp.argmax(g_logits, axis=-1)
    p_group = jnp.max(jax.nn.softmax(g_logits, axis=-1), axis=-1, keepdims=True)
    e_all = jnp.einsum('nd,dge->nge', h, w_router, preferred_element_type=jnp.float32)
    e_logits = jnp.einsum('nge,ng->ne', e_all, jax.nn.one_hot(g_sel, N_GROUPS, dtype=jnp.float32))
    top_val, top_idx = lax.top_k(e_logits, TOPK_IN_GROUP)
    gates = jax.nn.softmax(top_val, axis=-1) * p_group
    expert = g_sel[:, None] * EXPERTS_PER_GROUP + top_idx
    combine = jnp.einsum('nk,nke->ne', gates, jax.nn.one_hot(expert, N_EXPERTS, dtype=jnp.float32))
    act = jax.nn.silu(jnp.einsum('nd,edf->nef', h, w_gate)) * jnp.einsum('nd,edf->nef', h, w_up)
    return jnp.einsum('nef,efd->nd', act * combine[:, :, None].astype(act.dtype), w_down)

def hier_moe(h, w_group, w_router, w_gate, w_up, w_down):
    return lax.map(lambda hb: moe_tokens(hb, w_group, w_router, w_gate, w_up, w_down), h)

def trunk(x, past_ab, past_dsa, norm_mix, norm_ffn, norm_final, w_in_ab, b_forget, w_out_ab,
          w_in_dsa, w_out_dsa, moe_w_group, moe_w_router, moe_w_gate, moe_w_up, moe_w_down):
    rows_ab, rows_dsa = None, None
    for layer in range(DEPTH):
        h = rms_norm(x, norm_mix[layer])
        if layer % 2 == 0:
            y, rows_ab = mixer_ab(h, past_ab, w_in_ab, b_forget, w_out_ab)
        else:
            y, rows_dsa = mixer_dsa(h, past_dsa, w_in_dsa, w_out_dsa)
        x = x + y.astype(x.dtype)
        h = rms_norm(x, norm_ffn[layer])
        x = x + hier_moe(h, moe_w_group[layer], moe_w_router[layer], moe_w_gate[layer],
                         moe_w_up[layer], moe_w_down[layer]).astype(x.dtype)
    return rms_norm(x, norm_final), rows_ab, rows_dsa

def setup_inputs(seed: int = 0) -> dict:
    key = jax.random.key(seed)
    ks = jax.random.split(key, 24)
    f32 = jnp.float32

    def nrm(k, shape, scale):
        return scale * jax.random.normal(k, shape, f32)

    ab_cols = sum(AB_SPLITS)
    dsa_cols = sum(DSA_SPLITS)
    return {
        'x_prompt': nrm(ks[0], (BATCH, SEQ, D_MODEL), 1.0),
        'x_sample': nrm(ks[1], (DEC_BATCH, DEC_SEQ, D_MODEL), 1.0),
        'cache_sb_k': nrm(ks[2], (DEC_BATCH, PAST_LEN, H_SB, HEAD_DIM), 1.0),
        'cache_sb_v': nrm(ks[3], (DEC_BATCH, PAST_LEN, H_SB, HEAD_DIM), 1.0),
        'cache_fox_k': nrm(ks[4], (DEC_BATCH, PAST_LEN, H_FOX, HEAD_DIM), 1.0),
        'cache_fox_v': nrm(ks[5], (DEC_BATCH, PAST_LEN, H_FOX, HEAD_DIM), 1.0),
        'cache_fox_logf': jax.nn.log_sigmoid(FORGET_BIAS_INIT + nrm(ks[6], (DEC_BATCH, PAST_LEN, H_FOX), 1.0)),
        'cache_dsa_k': nrm(ks[7], (DEC_BATCH, PAST_LEN, KV_DSA, HEAD_DIM), 1.0),
        'cache_dsa_v': nrm(ks[8], (DEC_BATCH, PAST_LEN, KV_DSA, HEAD_DIM), 1.0),
        'cache_dsa_idx_k': nrm(ks[9], (DEC_BATCH, PAST_LEN, D_IDX), 1.0),
        'norm_mix': 1.0 + nrm(ks[10], (DEPTH, D_MODEL), 0.05),
        'norm_ffn': 1.0 + nrm(ks[11], (DEPTH, D_MODEL), 0.05),
        'norm_final': 1.0 + nrm(ks[12], (D_MODEL,), 0.05),
        'w_in_ab': nrm(ks[13], (D_MODEL, ab_cols), D_MODEL ** -0.5),
        'b_forget': FORGET_BIAS_INIT + nrm(ks[14], (H_FOX,), 0.5),
        'w_out_ab': nrm(ks[15], ((H_SB + H_FOX) * HEAD_DIM, D_MODEL), ((H_SB + H_FOX) * HEAD_DIM) ** -0.5),
        'w_in_dsa': nrm(ks[16], (D_MODEL, dsa_cols), D_MODEL ** -0.5),
        'w_out_dsa': nrm(ks[17], (H_DSA * HEAD_DIM, D_MODEL), (H_DSA * HEAD_DIM) ** -0.5),
        'moe_w_group': nrm(ks[18], (DEPTH, D_MODEL, N_GROUPS), D_MODEL ** -0.5),
        'moe_w_router': nrm(ks[19], (DEPTH, D_MODEL, N_GROUPS, EXPERTS_PER_GROUP), D_MODEL ** -0.5),
        'moe_w_gate': nrm(ks[20], (DEPTH, N_EXPERTS, D_MODEL, D_EXPERT), D_MODEL ** -0.5),
        'moe_w_up': nrm(ks[21], (DEPTH, N_EXPERTS, D_MODEL, D_EXPERT), D_MODEL ** -0.5),
        'moe_w_down': nrm(ks[22], (DEPTH, N_EXPERTS, D_EXPERT, D_MODEL), D_EXPERT ** -0.5),
    }

def reference(x_prompt, x_sample, cache_sb_k, cache_sb_v, cache_fox_k, cache_fox_v, cache_fox_logf,
              cache_dsa_k, cache_dsa_v, cache_dsa_idx_k, norm_mix, norm_ffn, norm_final,
              w_in_ab, b_forget, w_out_ab, w_in_dsa, w_out_dsa,
              moe_w_group, moe_w_router, moe_w_gate, moe_w_up, moe_w_down):
    y_prompt, rows_ab_p, rows_dsa_p = trunk(
        x_prompt, None, None, norm_mix, norm_ffn, norm_final, w_in_ab, b_forget, w_out_ab,
        w_in_dsa, w_out_dsa, moe_w_group, moe_w_router, moe_w_gate, moe_w_up, moe_w_down)
    y_sample, rows_ab_s, rows_dsa_s = trunk(
        x_sample, (cache_sb_k, cache_sb_v, cache_fox_k, cache_fox_v, cache_fox_logf),
        (cache_dsa_k, cache_dsa_v, cache_dsa_idx_k), norm_mix, norm_ffn, norm_final,
        w_in_ab, b_forget, w_out_ab, w_in_dsa, w_out_dsa,
        moe_w_group, moe_w_router, moe_w_gate, moe_w_up, moe_w_down)
    p_sb_k, p_sb_v, p_fox_k, p_fox_v, p_fox_logf = rows_ab_p
    p_dsa_k, p_dsa_v, p_dsa_idx_k = rows_dsa_p
    s_sb_k, s_sb_v, s_fox_k, s_fox_v, s_fox_logf = rows_ab_s
    s_dsa_k, s_dsa_v, s_dsa_idx_k = rows_dsa_s
    return (y_prompt, y_sample,
            p_sb_k, p_sb_v, p_fox_k, p_fox_v, p_fox_logf, p_dsa_k, p_dsa_v, p_dsa_idx_k,
            s_sb_k, s_sb_v, s_fox_k, s_fox_v, s_fox_logf, s_dsa_k, s_dsa_v, s_dsa_idx_k)


_drawn_inputs = setup_inputs


def setup_inputs(seed=0):
    import zlib

    import numpy as np

    out = dict(_drawn_inputs(seed))
    spreads = {}
    factors = {}
    for name, (base, spread) in spreads.items():
        noise = np.random.default_rng([zlib.crc32(name.encode()), seed]).standard_normal(out[name].shape)
        drawn = base * np.exp(spread * noise) if base else spread * noise
        out[name] = __import__('jax').numpy.asarray(drawn.astype(out[name].dtype))
    for name, factor in factors.items():
        out[name] = (out[name] * factor).astype(out[name].dtype)
    return out
```

```python
from contextlib import ExitStack

import concourse.bass as bass
from concourse import mybir

ALU = mybir.AluOpType
ACT = mybir.ActivationFunctionType
AX = mybir.AxisListType
F32 = mybir.dt.float32
F32R = mybir.dt.float32r
BF16 = mybir.dt.bfloat16
U32 = mybir.dt.uint32

P = 128
D = 1024
DC = D // P
PROMPT, SAMPLE, PAST = 512, 32, 256
PT = PROMPT // P
NT = PT + 1
T = PROMPT + SAMPLE
LS = PAST + SAMPLE
HEAD = 128
SCALE = HEAD ** -0.5
H_SB = H_FOX = 4
H_DSA, KV_DSA = 8, 2
H_IDX, D_IDX = 4, 64
IDX_COLS = H_IDX * D_IDX + D_IDX + H_IDX
CHUNK = 64
K_PROMPT = min(256, PROMPT // 4)
K_SAMPLE = min(256, LS // 4)
EPS = 1e-6
NG, EPG = 4, 4
NE = NG * EPG
FE = 256
SLOTS = P
PASSES = -(-T // SLOTS)
HALF_T = T // 2
NEG = -1e30
TAKEN = -3.4028234e38
BARRED = -3.2e38
UNTAKEN_FROM = -3.3e38

C_IDENT = 0
C_NEG_SB = P
C_NEG_FOX = 2 * P
C_NEG_CHUNK = 3 * P
C_BEFORE = 4 * P
C_SLOT = 5 * P
C_TOKEN = 6 * P
C_VALID = C_TOKEN + NT
C_FIRST = C_VALID + NT
C_EXPERT = C_FIRST + 4
C_COLS = C_EXPERT + NE
R_COS, R_SIN = 0, NT * HEAD
R_ICOS, R_ISIN = 2 * NT * HEAD, 2 * NT * HEAD + NT * D_IDX
R_COLS = 2 * NT * (HEAD + D_IDX)


def width(t):
    return P if t < PT else SAMPLE


def cols(t):
    return slice(t * P, t * P + width(t))


class Main:
    pass


class Routing:
    pass


class Attention:
    pass


class Chain:

    def __init__(self, eng, sem):
        self.eng, self.sem, self.n = eng, sem, 0

    def __call__(self, instruction):
        instruction.then_inc(self.sem, 1)
        self.n += 1

    def wait(self):
        self.eng.wait_ge(self.sem, self.n)


def tools(nc, ctx, prefix):
    def sb(name, shape, dtype=F32):
        return ctx.enter_context(nc.sbuf_tensor(f"{prefix}_{name}", shape, dtype))

    def ps(name, shape, dtype=F32):
        return ctx.enter_context(nc.psum_tensor(f"{prefix}_{name}", shape, dtype))

    mine = []

    def sem(name, kept=False):
        handle = nc.alloc_semaphore(f"{prefix}_{name}")
        if not kept:
            mine.append(handle)
        return handle

    def clear():
        numbers = sorted(s.num for s in mine)
        runs = [n for n in numbers if n - 1 not in numbers]
        for lo in runs:
            hi = lo
            while hi in numbers:
                hi += 1
            nc.gpsimd.sem_clear(range(lo, hi))
        for s in mine:
            nc.release_semaphore(s)

    ctx.callback(clear)
    return sb, ps, sem


def load_stage(nc, m, io):
    with ExitStack() as ctx:
        _, _, sem = tools(nc, ctx, "load")
        x_cleared, x_loaded, consts_loaded = sem("x_cleared"), sem("x_loaded"), sem("consts_loaded")
        block = ctx.enter_context(nc.Block())

        @block.sync
        def _(sp):
            sp.dma_start(m.x[:, 0:PT, :], io["x_prompt"].rearrange("b (t p) d -> p (b t) d", p=P)).then_inc(x_loaded, 16)
            sp.wait_ge(x_cleared, 1)
            sp.dma_start(m.x[0:SAMPLE, PT, :], io["x_sample"].rearrange("b t d -> (b t) d")).then_inc(x_loaded, 16)
            sp.wait_ge(x_loaded, 32)

        @block.scalar
        def _(act):
            act.dma_start(m.consts[:, :], io["consts"]).then_inc(consts_loaded, 16)
            act.dma_start(m.head_select[:, :], io["head_select"]).then_inc(consts_loaded, 16)

        @block.vector
        def _(dve):
            dve.memset(m.x[:, PT, :], 0.0).then_inc(x_cleared, 1)
            dve.memset(m.ones[:, :], 1.0)
            dve.memset(m.ones16[:, :], 1.0)
            dve.wait_ge(consts_loaded, 32)
            dve.tensor_copy(m.masks[:, :], m.consts[:, 0:4 * P])
            dve.tensor_copy(m.before[:, :], m.consts[:, C_BEFORE:C_BEFORE + P])


def norm_stage(nc, m, name, g_dram, hT=None, h_dram=None, y_dram=None):
    with ExitStack() as ctx:
        sb, ps, sem = tools(nc, ctx, name)
        g = sb("g", [P, D])
        h = sb("h", [P, 2, D])
        squares = sb("squares", [P, D])
        stat = sb("stat", [P, 4, 8])
        turned = ps("turned", [P, 2, 2, 512])
        g_loaded, squared, mean_ready, root_ready = sem("g_loaded"), sem("squared"), sem("mean_ready"), sem("root_ready")
        inverse_ready, h_ready, h_turned = sem("inverse_ready"), sem("h_ready"), sem("h_turned")
        hT_low, hT_high = sem("hT_low"), sem("hT_high")
        stored = [sem("stored0"), sem("stored1")]
        block = ctx.enter_context(nc.Block())

        @block.sync
        def _(sp):
            sp.dma_start(g[:, :], g_dram.partition_broadcast(P)).then_inc(g_loaded, 16)
            for t in range(NT):
                w = width(t)
                sp.wait_ge(h_ready, t + 1)
                if h_dram is not None:
                    sp.dma_start(h_dram[t * P:t * P + w, :], h[0:w, t % 2, :]).then_inc(stored[t % 2], 16)
                if y_dram is not None:
                    dst = y_dram[0][t * P:t * P + w, :] if t < PT else y_dram[1][:, :]
                    sp.dma_start(dst, h[0:w, t % 2, :]).then_inc(stored[t % 2], 16)
            if h_dram is not None or y_dram is not None:
                sp.wait_ge(stored[0], 16 * 3)
                sp.wait_ge(stored[1], 16 * 2)

        @block.scalar
        def _(act):
            for t in range(NT):
                if t:
                    act.wait_ge(squared, t)
                act.activation(squares[:, :], m.x[:, t, :], ACT.Square, accum_out=stat[:, 0, t:t + 1]).then_inc(squared, 1)
            act.wait_ge(mean_ready, 1)
            act.activation(stat[:, 2, 0:NT], stat[:, 1, 0:NT], ACT.Sqrt).then_inc(root_ready, 1)
            if hT is not None:
                for t in range(NT):
                    act.wait_ge(h_turned, t + 1)
                    w = width(t)
                    act.activation(hT[:, 0:4, cols(t)],
                                   turned[:, t % 2, 0, :].rearrange("p (c n) -> p c n", c=4)[:, :, 0:w],
                                   ACT.Copy).then_inc(hT_low, 1)

        @block.vector
        def _(dve):
            dve.wait_ge(squared, NT)
            dve.tensor_scalar(stat[:, 1, 0:NT], stat[:, 0, 0:NT], 1.0 / D, EPS, ALU.mult, ALU.add).then_inc(mean_ready, 1)
            dve.wait_ge(root_ready, 1)
            dve.reciprocal(stat[:, 3, 0:NT], stat[:, 2, 0:NT]).then_inc(inverse_ready, 1)
            dve.wait_ge(inverse_ready, 1)
            dve.wait_ge(g_loaded, 16)

            def high_half(t):
                dve.wait_ge(h_turned, t + 1)
                w = width(t)
                dve.tensor_copy(hT[:, 4:8, cols(t)],
                                turned[:, t % 2, 1, :].rearrange("p (c n) -> p c n", c=4)[:, :, 0:w]).then_inc(hT_high, 1)

            for t in range(NT):
                if t >= 2:
                    if hT is not None:
                        dve.wait_ge(h_turned, t - 1)
                    if h_dram is not None or y_dram is not None:
                        dve.wait_ge(stored[t % 2], 16 * (t // 2))
                dve.scalar_tensor_tensor(out=h[:, t % 2, :], in0=m.x[:, t, :], scalar=stat[:, 3, t:t + 1],
                                         in1=g[:, :], op0=ALU.mult, op1=ALU.mult).then_inc(h_ready, 1)
                if hT is not None and t >= 1:
                    high_half(t - 1)
            if hT is not None:
                high_half(NT - 1)

        @block.tensor
        def _(pe):
            if hT is None:
                return
            for t in range(NT):
                w = width(t)
                pe.wait_ge(h_ready, t + 1)
                if t >= 2:
                    pe.wait_ge(hT_low, t - 1)
                    pe.wait_ge(hT_high, t - 1)
                for c in range(DC):
                    last = pe.transpose(turned[:, t % 2, c // 4, (c % 4) * P:(c % 4) * P + w],
                                        h[0:w, t % 2, c * P:(c + 1) * P], m.ident[0:w, 0:w])
                last.then_inc(h_turned, 1)


def rows_of(dram, t, heads=True):
    pattern = "b t h d -> (b t) (h d)" if heads else "b t d -> (b t) d"
    if t < PT:
        return dram[0].rearrange(pattern)[t * P:(t + 1) * P, :]
    return dram[1].rearrange(pattern)


def project_ab_stage(nc, m, a, io):
    with ExitStack() as ctx:
        sb, ps, sem = tools(nc, ctx, "ab")
        w_forget = sb("w_forget", [P, DC, 4])
        b_col = sb("b_col", [4, 1])
        k_rows = sb("k_rows", [P, 2, 512])
        cache_k = sb("cache_k", [P, 2, 2, 512])
        cache_f = sb("cache_f", [P, 2, 4])
        u = sb("u", [4, T])
        soft = sb("soft", [4, T])
        logf = sb("logf", [4, T])
        logf_s = sb("logf_s", [4, LS])
        logf_rows = sb("logf_rows", [P, NT, 4])
        acc = ps("acc", [P, 4, 512])
        acc_k = ps("acc_k", [P, 2, 512])
        turned = ps("turned", [P, 2, 512])
        ring = sb("ring", [P, 3 * 4096])
        w_slot = [ring[:, s * 4096:(s + 1) * 4096].rearrange("p (c n) -> p c n", c=DC) for s in range(3)]
        w_loaded = [sem(f"w_loaded{s}") for s in range(3)]
        small_loaded, cache_k_loaded = sem("small_loaded", kept=True), sem("cache_k_loaded")
        block_done = sem("block_done")
        group_ready, group_stored = sem("group_ready"), sem("group_stored")
        k_ready, k_rows_ready, k_turned, kT_stored = sem("k_ready"), sem("k_rows_ready"), sem("k_turned"), sem("kT_stored")
        k_saved = [sem("k_saved0", kept=True), sem("k_saved1", kept=True)]
        v_saved, cache_v_loaded, act_chain, dve_chain = sem("v_saved"), sem("cache_v_loaded", kept=True), sem("act_chain"), sem("dve_chain")
        soft_ready, logf_ready, f_turned, f_stored, f_saved = (
            sem("soft_ready"), sem("logf_ready"), sem("f_turned"), sem("f_stored"), sem("f_saved"))
        f_cache_turned = sem("f_cache_turned")
        block = ctx.enter_context(nc.Block())
        COLUMN = [0, 3, 1, 4, 2, 5]
        QG, KG = 16, 10
        out_k, out_v = [io["out_sb_k"], io["out_fox_k"]], [io["out_sb_v"], io["out_fox_v"]]

        @block.sync
        def _(sp):
            w_view = io["w_in_ab"].rearrange("(c p) n -> p c n", p=P)

            def load_block(b):
                sp.dma_start(w_slot[b % 3], w_view[:, :, COLUMN[b] * 512:(COLUMN[b] + 1) * 512]).then_inc(w_loaded[b % 3], 16)

            load_block(0)
            for kind, cache in enumerate((io["cache_sb_k"], io["cache_fox_k"])):
                sp.dma_start(cache_k[:, kind, :, :], cache.rearrange("b (j p) h d -> p (b j) (h d)", p=P)).then_inc(cache_k_loaded, 16)
            load_block(1)
            load_block(2)
            for b in range(3, 6):
                sp.wait_ge(block_done, b - 2)
                load_block(b)
            for kind in range(2):
                for t in range(NT):
                    w = width(t)
                    sp.wait_ge(group_stored, QG + kind * NT + t + 1)
                    sp.dma_start(rows_of(out_v[kind], t), a.v_rows[0:w, t, kind * 512:(kind + 1) * 512]).then_inc(v_saved, 16)
            sp.wait_ge(f_stored, 1)
            sp.dma_start(io["out_fox_logf"][0].rearrange("b (t p) h -> p (b t) h", p=P), logf_rows[:, 0:PT, :]).then_inc(f_saved, 16)
            sp.dma_start(io["out_fox_logf"][1].rearrange("b t h -> (b t) h"), logf_rows[0:SAMPLE, PT, :]).then_inc(f_saved, 16)
            sp.wait_ge(k_saved[0], 16 * KG // 2)
            sp.wait_ge(k_saved[1], 16 * KG // 2)
            sp.wait_ge(v_saved, 16 * 2 * NT)
            sp.wait_ge(f_saved, 32)
            sp.wait_ge(cache_v_loaded, 32)

        @block.gpsimd
        def _(pool):
            pool.dma_start(w_forget[:, :, :], io["w_in_ab"].rearrange("(c p) n -> p c n", p=P)[:, :, 6 * 512:6 * 512 + 4]).then_inc(small_loaded, 16)
            pool.dma_start(b_col[:, :], io["b_forget"].rearrange("(h a) -> h a", a=1)).then_inc(small_loaded, 16)
            pool.dma_start(cache_f[:, :, :], io["cache_fox_logf"].rearrange("b (j p) h -> p (b j) h", p=P)).then_inc(small_loaded, 16)
            for kind, cache in enumerate((io["cache_sb_v"], io["cache_fox_v"])):
                pool.dma_start(a.cache_v[:, :, kind * 512:(kind + 1) * 512], cache.rearrange("b (j p) h d -> p (b j) (h d)", p=P)).then_inc(cache_v_loaded, 16)
            for kind in range(2):
                for t in range(NT):
                    g = kind * NT + t
                    w = width(t)
                    pool.wait_ge(k_rows_ready, g + 1)
                    pool.dma_start(rows_of(out_k[kind], t), k_rows[0:w, g % 2, :]).then_inc(k_saved[g % 2], 16)

        @block.tensor
        def _(pe):
            for j in range(4):
                kind, kb = divmod(j, 2)
                if j == 0:
                    pe.wait_ge(cache_k_loaded, 32)
                if j >= 2:
                    pe.wait_ge(kT_stored, j - 1)
                for h in range(4):
                    last = pe.transpose(turned[:, j % 2, h * P:(h + 1) * P], cache_k[:, kind, kb, h * P:(h + 1) * P], m.ident[:, :])
                last.then_inc(k_turned, 1)
            for h in range(8):
                b = h // 4
                if h % 4 == 0:
                    pe.wait_ge(w_loaded[b], 16)
                for n in range(2):
                    g = 2 * h + n
                    if g >= 4:
                        pe.wait_ge(group_stored, g - 3)
                    for c in range(DC):
                        last = pe.matmul(acc[:, g % 4, 0:HALF_T], w_slot[b][:, c, (h % 4) * P:(h % 4 + 1) * P],
                                         m.hT[:, c, n * HALF_T:(n + 1) * HALF_T], start=(c == 0), stop=(c == DC - 1))
                    last.then_inc(group_ready, 1)
                if h % 4 == 3:
                    pe.drain().then_inc(block_done, 1)

            def turn_k(g):
                kind, t = divmod(g, NT)
                w = width(t)
                pe.wait_ge(k_rows_ready, g + 1)
                pe.wait_ge(kT_stored, g + 3)
                for h in range(4):
                    last = pe.transpose(turned[:, g % 2, h * P:h * P + w], k_rows[0:w, g % 2, h * P:(h + 1) * P], m.ident[0:w, 0:w])
                last.then_inc(k_turned, 1)

            for g in range(KG):
                kind, t = divmod(g, NT)
                w = width(t)
                if t == 0:
                    pe.wait_ge(w_loaded[(2 + kind) % 3], 16 * (1 + kind))
                if g >= 2:
                    pe.wait_ge(k_rows_ready, g - 1)
                for c in range(DC):
                    last = pe.matmul(acc_k[0:w, g % 2, :], m.hT[:, c, cols(t)], w_slot[(2 + kind) % 3][:, c, :],
                                     start=(c == 0), stop=(c == DC - 1))
                last.then_inc(k_ready, 1)
                if t == NT - 1:
                    pe.drain().then_inc(block_done, 1)
                if g >= 1:
                    turn_k(g - 1)
            turn_k(KG - 1)
            for i in range(10):
                kind, t = divmod(i, NT)
                w = width(t)
                g = QG + i
                if t == 0:
                    pe.wait_ge(w_loaded[(4 + kind) % 3], 32)
                pe.wait_ge(group_stored, g - 3)
                for c in range(DC):
                    last = pe.matmul(acc[0:w, g % 4, :], m.hT[:, c, cols(t)], w_slot[(4 + kind) % 3][:, c, :],
                                     start=(c == 0), stop=(c == DC - 1))
                last.then_inc(group_ready, 1)
            pe.wait_ge(small_loaded, 48)
            for n in range(2):
                g = QG + 10 + n
                pe.wait_ge(group_stored, g - 3)
                for c in range(DC):
                    last = pe.matmul(acc[0:4, g % 4, 0:HALF_T], w_forget[:, c, :], m.hT[:, c, n * HALF_T:(n + 1) * HALF_T],
                                     start=(c == 0), stop=(c == DC - 1))
                last.then_inc(group_ready, 1)
            pe.wait_ge(kT_stored, 4 + KG)
            for kb in range(2):
                last = pe.transpose(turned[0:4, 0, kb * P:(kb + 1) * P], cache_f[:, kb, :], m.ident[:, :])
            last.then_inc(f_cache_turned, 1)
            pe.wait_ge(logf_ready, 1)
            for t in range(NT):
                w = width(t)
                last = pe.transpose(turned[0:w, 1, 4 * t:4 * t + 4], logf[:, cols(t)], m.ident[0:4, 0:4])
            last.then_inc(f_turned, 1)

        @block.scalar
        def _(act):
            for g in range(QG):
                h, n = divmod(g, 2)
                act.wait_ge(group_ready, g + 1)
                act.activation(a.qT[:, h, n * HALF_T:(n + 1) * HALF_T], acc[:, g % 4, 0:HALF_T], ACT.Copy, scale=SCALE).then_inc(group_stored, 1)
            for i in range(10):
                kind, t = divmod(i, NT)
                w = width(t)
                g = QG + i
                act.wait_ge(group_ready, g + 1)
                act.activation(a.v_rows[0:w, t, kind * 512:(kind + 1) * 512], acc[0:w, g % 4, :], ACT.Copy).then_inc(group_stored, 1)
            act.wait_ge(small_loaded, 48)
            for n in range(2):
                g = QG + 10 + n
                act.wait_ge(group_ready, g + 1)
                act.activation(u[:, n * HALF_T:(n + 1) * HALF_T], acc[0:4, g % 4, 0:HALF_T], ACT.Identity, bias=b_col[:, 0:1]).then_inc(group_stored, 1)
            act.wait_ge(group_stored, QG + 12)
            act.activation(soft[:, :], u[:, :], ACT.Abs).then_inc(act_chain, 1)
            act.wait_ge(act_chain, 1)
            act.activation(soft[:, :], soft[:, :], ACT.Exp, scale=-1.0).then_inc(act_chain, 1)
            act.wait_ge(act_chain, 2)
            act.activation(soft[:, :], soft[:, :], ACT.Ln, bias=1.0).then_inc(soft_ready, 1)

        @block.vector
        def _(dve):
            for j in range(4):
                kind, kb = divmod(j, 2)
                dve.wait_ge(k_turned, j + 1)
                dve.tensor_copy(a.kT_sample[:, kind * 4:kind * 4 + 4, kb * P:(kb + 1) * P],
                                turned[:, j % 2, :].rearrange("p (h n) -> p h n", h=4)).then_inc(kT_stored, 1)

            def store_kT(g):
                kind, t = divmod(g, NT)
                w = width(t)
                dve.wait_ge(k_turned, 4 + g + 1)
                dst = a.kT[:, kind * 4:kind * 4 + 4, t * P:(t + 1) * P] if t < PT else a.kT_sample[:, kind * 4:kind * 4 + 4, PAST:LS]
                dve.tensor_copy(dst, turned[:, g % 2, :].rearrange("p (h n) -> p h n", h=4)[:, :, 0:w]).then_inc(kT_stored, 1)

            for g in range(KG):
                w = width(g % NT)
                dve.wait_ge(k_ready, g + 1)
                if g >= 2:
                    dve.wait_ge(k_turned, 4 + g - 1)
                    dve.wait_ge(k_saved[g % 2], 16 * (g // 2))
                dve.tensor_copy(k_rows[0:w, g % 2, :], acc_k[0:w, g % 2, :]).then_inc(k_rows_ready, 1)
                if g >= 1:
                    store_kT(g - 1)
            store_kT(KG - 1)
            dve.wait_ge(soft_ready, 1)
            dve.scalar_tensor_tensor(out=logf[:, :], in0=u[:, :], scalar=0.0, in1=soft[:, :], op0=ALU.min, op1=ALU.subtract).then_inc(logf_ready, 1)
            dve.wait_ge(f_cache_turned, 1)
            dve.tensor_copy(logf_s[:, 0:PAST], turned[0:4, 0, 0:PAST]).then_inc(dve_chain, 1)
            dve.wait_ge(logf_ready, 1)
            dve.tensor_copy(logf_s[:, PAST:LS], logf[:, PROMPT:T]).then_inc(dve_chain, 1)
            dve.tensor_tensor_scan(a.forget[:, :], m.ones[0:4, :], logf[:, 0:PROMPT], 0.0, ALU.mult, ALU.add)
            dve.wait_ge(dve_chain, 2)
            dve.tensor_tensor_scan(a.forget_sample[:, :], m.ones[0:4, 0:LS], logf_s[:, :], 0.0, ALU.mult, ALU.add)
            dve.wait_ge(f_turned, 1)
            dve.tensor_copy(logf_rows[:, 0:PT, :], turned[:, 1, 0:4 * PT].rearrange("p (t h) -> p t h", h=4)).then_inc(dve_chain, 1)
            dve.wait_ge(dve_chain, 3)
            dve.tensor_copy(logf_rows[0:SAMPLE, PT, :], turned[0:SAMPLE, 1, 4 * PT:4 * PT + 4]).then_inc(f_stored, 1)


class Unit:

    def __init__(self, heads, t, stick=False):
        self.heads, self.t, self.sample, self.stick = heads, t, t == PT, stick
        self.n = LS if self.sample else (t + 1) * P
        self.blocks = 3 if self.sample else t + 1

    def rows_in(self, kb):
        return SAMPLE if self.sample and kb == 2 else P


def score_products(pe, m, a, unit, out, kv, mask, forget):
    for i, h in enumerate(unit.heads):
        q = a.qT[:, h, cols(unit.t)]
        k = a.kT_sample[:, kv(h), :] if unit.sample else a.kT[:, kv(h), :]
        rows = slice(32 * i, 32 * i + 32) if unit.sample else slice(0, P)
        nq = SAMPLE if unit.sample else P
        edge = PAST if unit.sample else unit.t * P
        spans = [(0, unit.n)] if mask is None else ([(0, edge)] if edge else []) + [(edge, unit.n)]
        for lo, hi in spans:
            masked = mask is None or lo == edge
            products = [(q, k[:, lo:hi])]
            if forget:
                f = a.forget_sample if unit.sample else a.forget
                products.append((m.head_select[:, (h - H_SB) * P:(h - H_SB) * P + nq], f[:, lo:hi]))
            if mask is not None and masked:
                products.append((m.ident16[0:nq, 0:nq], mask[0:nq, 0:hi - lo]))
            if mask is None:
                chosen = a.unchosen[unit.t]
                products.append((m.ident16[0:nq, 0:nq], chosen[0:nq, lo:hi]))
            for j, (left, right) in enumerate(products):
                last = pe.matmul(out[rows, lo:hi], left, right, start=(j == 0), stop=(j == len(products) - 1))
    return last


def value_products(pe, a, unit, out, pT, v_head):
    for i, h in enumerate(unit.heads):
        q = slice(32 * i, 32 * i + 32) if unit.sample else slice(0, P)
        vc = slice(v_head(h) * P, (v_head(h) + 1) * P)
        for kb in range(unit.blocks):
            n = unit.rows_in(kb)
            if unit.sample:
                v = a.cache_v[:, kb, vc] if kb < 2 else a.v_rows[0:SAMPLE, PT, vc]
            else:
                v = a.v_rows[:, kb, vc]
            last = pe.matmul(out[:, q], v, pT[0:n, kb, q], start=(kb == 0), stop=(kb == unit.blocks - 1))
    return last


def mixer_stage(nc, m, a, r, name, steps, kv, v_head, masks, forget, w_dram, g_dram, split):
    with ExitStack() as ctx:
        sb, ps, sem = tools(nc, ctx, name)
        order = [units[0].t for units, last in steps if last]
        last_step = [i for i, (_, last) in enumerate(steps) if last]
        units = [u for us, _ in steps for u in us]
        first_unit = [sum(len(us) for us, _ in steps[:i]) for i in range(len(steps))]
        kind_no = [sum(v.stick == u.stick for v in units[:i]) for i, u in enumerate(units)]
        sticks = any(u.stick for u in units)
        softs = sum(not u.stick for u in units)
        soft_banks = 1 if sticks else 3
        PART = F32R if split else F32
        prob = sb("prob", [P, 4, 512])
        work = sb("work", [P, 2, 512]) if sticks else None
        pT = sb("pT", [P, 3, 4, P])
        row_stat = sb("row_stat", [P, 3, softs])
        oT = sb("oT", [P, 2, DC, P], PART)
        oT_rest = sb("oT_rest", [P, 2, DC, P], PART) if split else None
        g = sb("g", [P, D])
        free = m.hT[:, :, :].rearrange("p c n -> p (c n)")
        h = free[:, 0:2 * D].rearrange("p (b n) -> p b n", b=2)
        squares = free[:, 2 * D:3 * D]
        hT = free[:, 3 * D:4 * D].rearrange("p (c n) -> p c n", c=DC)
        stat = sb("stat", [P, 8, NT])
        w_route = sb("w_route", [P, DC, NG + NE])
        scores_soft = ps("scores_soft", [P, soft_banks, 512])
        scores_stick = ps("scores_stick", [P, 2, 512]) if sticks else None
        turned = ps("turned", [P, 2, 512])
        mixed = ps("mixed", [P, 2, 512])
        acc = ps("acc", [P, 512])
        scores_ready = {True: sem("stick_scores"), False: sem("soft_scores")}
        scores_used = {True: sem("stick_scores_used"), False: sem("soft_scores_used")}
        prob_ready = {True: sem("stick_prob"), False: sem("soft_prob")}
        soft_ready, sum_ready, suffix_ready = sem("soft_ready"), sem("sum_ready"), sem("suffix_ready")
        exponent_ready, act_chain = sem("exponent_ready"), sem("act_chain")
        neg_max_ready, exp_ready, inverse_ready = sem("neg_max_ready"), sem("exp_ready"), sem("inverse_ready")
        turned_ready, turned_stored, mixed_ready, mixed_stored = (
            sem("turned_ready"), sem("turned_stored"), sem("mixed_ready"), sem("mixed_stored"))
        rest_stored, cleared = sem("rest_stored"), sem("cleared")
        w_loaded, small_loaded = [sem("w_loaded0"), sem("w_loaded1")], sem("small_loaded")
        w_rounded, w_split = sem("w_rounded"), sem("w_split")
        group_ready, added, squared, mean_ready, root_ready, newton = (
            sem("group_ready"), sem("added"), sem("squared"), sem("mean_ready"), sem("root_ready"), sem("newton"))
        h_ready, logits_ready, logits_stored = sem("h_ready"), sem("logits_ready"), sem("logits_stored")
        h_saved = [sem("h_saved0"), sem("h_saved1")]
        if split:
            w_raw = sb("w_raw", [P, 2, DC, 256])
            w_high = sb("w_high", [P, 4, DC, 256], F32R)
            w_low = sb("w_low", [P, 4, DC, 256], F32R)
        else:
            w_out = sb("w_out", [P, DC, D])

        turns = {}
        for s in range(last_step[-1] + 9):
            if 1 <= s <= len(steps):
                for i in range(first_unit[s - 1], first_unit[s - 1] + len(steps[s - 1][0])):
                    turns["unit", i] = len(turns)
            for o, end in enumerate(last_step):
                if s == end + 8:
                    turns["norm", o, 0] = len(turns)
                    turns["norm", o, 1] = len(turns)
        END = last_step[-1] + 9
        block = ctx.enter_context(nc.Block())

        def units_of(s):
            return [(first_unit[s] + j, u) for j, u in enumerate(steps[s][0])] if 0 <= s < len(steps) else []

        def scores_of(i):
            u = units[i]
            return scores_stick[:, kind_no[i] % 2] if u.stick else scores_soft[:, kind_no[i] % soft_banks]

        def tiles_at(s, lag):
            return [(o, order[o]) for o, end in enumerate(last_step) if s == end + lag]

        @block.sync
        def _(sp):
            sp.dma_start(w_route[:, :, 0:NG], r.w_group.rearrange("(c p) g -> p c g", p=P)).then_inc(small_loaded, 16)
            sp.dma_start(w_route[:, :, NG:], r.w_router.rearrange("(c p) g e -> p c (g e)", p=P)).then_inc(small_loaded, 16)
            sp.dma_start(g[:, :], g_dram.partition_broadcast(P)).then_inc(small_loaded, 16)
            w_view = w_dram.rearrange("(c p) n -> p c n", p=P)
            if split:
                for q in range(4):
                    if q >= 2:
                        sp.wait_ge(w_split, q - 1)
                    sp.dma_start(w_raw[:, q % 2], w_view[:, :, q * 256:(q + 1) * 256]).then_inc(w_loaded[q % 2], 16)
            else:
                for n in range(2):
                    sp.dma_start(w_out[:, :, n * 512:(n + 1) * 512], w_view[:, :, n * 512:(n + 1) * 512]).then_inc(w_loaded[n], 16)
            for o, t in enumerate(order):
                w = width(t)
                sp.wait_ge(h_ready, o + 1)
                sp.dma_start(r.h_dram[t * P:t * P + w, :], h[0:w, o % 2, :]).then_inc(h_saved[o % 2], 16)
            sp.wait_ge(h_saved[0], 48)
            sp.wait_ge(h_saved[1], 32)

        @block.tensor
        def _(pe):
            def turn(i):
                pos, u = turns["unit", i], units[i]
                pe.wait_ge(prob_ready[u.stick], kind_no[i] + 1)
                if pos >= 2:
                    pe.wait_ge(turned_stored, pos - 1)
                for kb in range(u.blocks):
                    n = u.rows_in(kb)
                    last = pe.transpose(turned[0:n, pos % 2, kb * P:(kb + 1) * P], prob[:, i % 4, kb * P:kb * P + n], m.ident[:, :])
                last.then_inc(turned_ready, 1)

            def mix(i):
                pe.wait_ge(turned_stored, turns["unit", i] + 1)
                if i >= 2:
                    pe.wait_ge(mixed_stored, i - 1)
                    if split:
                        pe.wait_ge(rest_stored, i - 1)
                value_products(pe, a, units[i], mixed[:, i % 2, 0:P], pT[:, i % 3], v_head).then_inc(mixed_ready, 1)

            def output_part(o, q):
                n, first = divmod(q, 2)
                w = P if split else width(order[o])
                if q == 0:
                    done = first_unit[last_step[o]] + len(steps[last_step[o]][0])
                    pe.wait_ge(mixed_stored, done)
                    if split:
                        pe.wait_ge(rest_stored, done)
                        if o == 0:
                            pe.wait_ge(w_split, 4)
                if o == 0 and not split and first == 0:
                    pe.wait_ge(w_loaded[n], 16)
                if first == 0 and 2 * o + n:
                    pe.wait_ge(added, 2 * o + n)
                if first == 0 and routed[0]:
                    pe.wait_ge(logits_stored, routed[0])
                for c in range(4 * first, 4 * first + 4):
                    if not split:
                        last = pe.matmul(acc[0:w, :], oT[:, o % 2, c, 0:w], w_out[:, c, n * 512:(n + 1) * 512], start=(c == 0), stop=(c == DC - 1))
                        continue
                    for half in range(2):
                        out, k = acc[:, half * 256:(half + 1) * 256], 2 * n + half
                        for j, (left, right) in enumerate(((oT, w_high), (oT, w_low), (oT_rest, w_high))):
                            last = pe.matmul(out, left[:, o % 2, c, :], right[:, k, c, :], start=(c == 0 and j == 0 and half == 0),
                                             stop=(c == DC - 1 and j == 2), skip_group_check=True)
                if first:
                    last.then_inc(group_ready, 1)

            def turn_norm(o, t):
                w = width(t)
                pe.wait_ge(h_ready, o + 1)
                for half in range(2):
                    pos = turns["norm", o, half]
                    pe.wait_ge(turned_stored, pos - 1)
                    for c in range(4):
                        last = pe.transpose(turned[:, pos % 2, c * P:c * P + w], h[0:w, o % 2, (4 * half + c) * P:(4 * half + c + 1) * P], m.ident[0:w, 0:w])
                    last.then_inc(turned_ready, 1)

            def route(o, t):
                w = width(t)
                if o == 0:
                    pe.wait_ge(small_loaded, 48)
                pe.wait_ge(added, min(2 * o + 3, 2 * NT))
                pe.wait_ge(turned_stored, turns["norm", o, 1] + 1)
                for c in range(DC):
                    last = pe.matmul(acc[0:w, 0:NG + NE], hT[:, c, 0:w], w_route[:, c, :], start=(c == 0), stop=(c == DC - 1))
                last.then_inc(logits_ready, 1)
                routed[0] = o + 1

            routed = [0]
            for s in range(END):
                for i, u in units_of(s):
                    k, banks = kind_no[i], 2 if u.stick else soft_banks
                    if k >= banks:
                        pe.wait_ge(scores_used[u.stick], k - banks + 1)
                    score_products(pe, m, a, u, scores_of(i), kv, masks[u.stick], forget and not u.stick).then_inc(scores_ready[u.stick], 1)
                for q in range(4):
                    for o, _ in tiles_at(s, 3 + q):
                        output_part(o, q)
                for i, _ in units_of(s - 1):
                    turn(i)
                for i, _ in units_of(s - 2):
                    mix(i)
                for o, t in tiles_at(s, 8):
                    turn_norm(o, t)
                    route(o, t)

        @block.scalar
        def _(act):
            chained = 0
            for s in range(END + 1):
                for i, u in units_of(s):
                    if not u.stick:
                        continue
                    k, buf = kind_no[i], prob[:, i % 4, 0:u.n]
                    act.wait_ge(scores_ready[True], k + 1)
                    if i >= 4:
                        act.wait_ge(turned_ready, turns["unit", i - 4] + 1)
                    act.activation(buf, scores_of(i)[:, 0:u.n], ACT.Abs).then_inc(act_chain, 1)
                    act.wait_ge(act_chain, chained + 1)
                    act.activation(buf, buf, ACT.Exp, scale=-1.0).then_inc(act_chain, 1)
                    act.wait_ge(act_chain, chained + 2)
                    act.activation(buf, buf, ACT.Ln, bias=1.0).then_inc(soft_ready, 1)
                    chained += 2
                for i, u in units_of(s):
                    if u.stick:
                        continue
                    k = kind_no[i]
                    act.wait_ge(neg_max_ready, k + 1)
                    if i >= 4:
                        act.wait_ge(turned_ready, turns["unit", i - 4] + 1)
                    act.activation(prob[:, i % 4, 0:u.n], scores_of(i)[:, 0:u.n], ACT.Exp, bias=row_stat[:, 0, k:k + 1],
                                   accum_out=row_stat[:, 1, k:k + 1]).then_inc(exp_ready, 1)
                for i, u in units_of(s):
                    if u.stick:
                        k = kind_no[i]
                        act.wait_ge(exponent_ready, k + 1)
                        act.activation(prob[:, i % 4, 0:u.n], work[:, k % 2, 0:u.n], ACT.Exp).then_inc(prob_ready[True], 1)
                if split and s < 4:
                    act.wait_ge(w_loaded[s % 2], 16 * (s // 2 + 1))
                    act.activation(w_high[:, s], w_raw[:, s % 2], ACT.Copy).then_inc(w_rounded, 1)
                for i, u in units_of(s - 2):
                    o = sum(end < s - 2 for end in last_step)
                    h0, h1 = u.heads[0], u.heads[-1] + 1
                    act.wait_ge(mixed_ready, i + 1)
                    if i == 0:
                        act.wait_ge(cleared, 1)
                    if o >= 2:
                        act.wait_ge(group_ready, 2 * (o - 1))
                    act.activation(oT[:, o % 2, h0:h1, 0:width(u.t)], mixed[:, i % 2, 0:P].rearrange("p (h n) -> p h n", h=h1 - h0), ACT.Copy).then_inc(mixed_stored, 1)
                for o, t in tiles_at(s, 7):
                    act.wait_ge(added, 2 * o + 2)
                    if o:
                        act.wait_ge(squared, o)
                    act.activation(squares[:, :], m.x[:, t, :], ACT.Square, accum_out=stat[:, 0, o:o + 1]).then_inc(squared, 1)
                    act.wait_ge(mean_ready, o + 1)
                    act.activation(stat[:, 2, o:o + 1], stat[:, 1, o:o + 1], ACT.Ln).then_inc(act_chain, 1)
                    chained += 1
                    act.wait_ge(act_chain, chained)
                    act.activation(stat[:, 3, o:o + 1], stat[:, 2, o:o + 1], ACT.Exp, scale=-0.5).then_inc(root_ready, 1)
                for o, t in tiles_at(s, 8):
                    w = width(t)
                    act.wait_ge(logits_ready, o + 1)
                    act.activation(r.logits[0:w, t, :], acc[0:w, 0:NG + NE], ACT.Copy).then_inc(logits_stored, 1)

        @block.gpsimd
        def _(pool):
            for i, u in enumerate(units):
                if not u.stick:
                    k = kind_no[i]
                    p = prob[:, i % 4, 0:u.n]
                    pool.wait_ge(inverse_ready, k + 1)
                    pool.tensor_scalar(p, p, row_stat[:, 2, k:k + 1], None, ALU.mult).then_inc(prob_ready[False], 1)

        @block.vector
        def _(dve):
            if split:
                dve.memset(oT[:, 0].bitcast(F32), 0.0)
                dve.memset(oT_rest[:, 0].bitcast(F32), 0.0)
            dve.memset(r.logits[:, PT, :], 0.0).then_inc(cleared, 1)
            dve.wait_ge(cleared, 1)

            def store_turned(i):
                pos, u = turns["unit", i], units[i]
                dve.wait_ge(turned_ready, pos + 1)
                if i >= 3:
                    dve.wait_ge(mixed_ready, i - 2)
                full = 2 if u.sample else u.blocks
                done = dve.tensor_copy(pT[:, i % 3, 0:full, :], turned[:, pos % 2, 0:full * P].rearrange("p (k n) -> p k n", k=full))
                if u.sample:
                    done = dve.tensor_copy(pT[0:SAMPLE, i % 3, 2, :], turned[0:SAMPLE, pos % 2, 2 * P:3 * P])
                done.then_inc(turned_stored, 1)

            refined = 0
            for s in range(END):
                for i, u in units_of(s):
                    if not u.stick:
                        k = kind_no[i]
                        dve.wait_ge(scores_ready[False], k + 1)
                        dve.tensor_reduce(row_stat[:, 0, k:k + 1], scores_of(i)[:, 0:u.n], AX.X, ALU.max, negate=True).then_inc(neg_max_ready, 1)
                if split and s < 4:
                    dve.wait_ge(w_rounded, s + 1)
                    dve.tensor_tensor(w_low[:, s], w_raw[:, s % 2], w_high[:, s].bitcast(F32), ALU.subtract).then_inc(w_split, 1)
                for i, u in units_of(s):
                    if not u.stick:
                        continue
                    k = kind_no[i]
                    z, buf, out = scores_of(i)[:, 0:u.n], prob[:, i % 4, 0:u.n], work[:, k % 2, 0:u.n]
                    dve.wait_ge(soft_ready, k + 1)
                    dve.scalar_tensor_tensor(out=buf, in0=z, scalar=0.0, in1=buf, op0=ALU.max, op1=ALU.add).then_inc(sum_ready, 1)
                    dve.wait_ge(sum_ready, k + 1)
                    if k >= 2:
                        dve.wait_ge(prob_ready[True], k - 1)
                    dve.tensor_tensor_scan(out[:, ::-1], m.ones[:, 0:u.n], buf[:, ::-1], 0.0, ALU.mult, ALU.add).then_inc(suffix_ready, 1)
                    dve.wait_ge(suffix_ready, k + 1)
                    dve.tensor_tensor(out, z, out, ALU.subtract).then_inc(exponent_ready, 1)
                    dve.wait_ge(exponent_ready, k + 1)
                    dve.sem_inc(scores_used[True], 1)
                for i, u in units_of(s):
                    if not u.stick:
                        k = kind_no[i]
                        dve.wait_ge(exp_ready, k + 1)
                        dve.sem_inc(scores_used[False], 1)
                        dve.reciprocal(row_stat[:, 2, k:k + 1], row_stat[:, 1, k:k + 1]).then_inc(inverse_ready, 1)
                for q in (1, 3):
                    for o, t in tiles_at(s, 3 + q):
                        n, w = q // 2, width(t)
                        x = m.x[0:w, t, n * 512:(n + 1) * 512]
                        dve.wait_ge(group_ready, 2 * o + n + 1)
                        dve.tensor_tensor(x, acc[0:w, :], x, ALU.add).then_inc(added, 1)
                for i, _ in units_of(s - 1):
                    store_turned(i)
                if split:
                    for i, u in units_of(s - 2):
                        o = sum(end < s - 2 for end in last_step)
                        h0, h1 = u.heads[0], u.heads[-1] + 1
                        w = width(u.t)
                        dve.wait_ge(mixed_stored, i + 1)
                        dve.tensor_tensor(oT_rest[:, o % 2, h0:h1, 0:w], mixed[:, i % 2, 0:P].rearrange("p (h n) -> p h n", h=h1 - h0),
                                          oT[:, o % 2, h0:h1, 0:w].bitcast(F32), ALU.subtract).then_inc(rest_stored, 1)
                for o, t in tiles_at(s, 7):
                    dve.wait_ge(squared, o + 1)
                    v, y, tmp = stat[:, 1, o:o + 1], stat[:, 3, o:o + 1], stat[:, 4, o:o + 1]
                    dve.tensor_scalar(v, stat[:, 0, o:o + 1], 1.0 / D, EPS, ALU.mult, ALU.add).then_inc(mean_ready, 1)
                    dve.wait_ge(root_ready, o + 1)
                    dve.scalar_tensor_tensor(out=tmp, in0=y, scalar=v, in1=y, op0=ALU.mult, op1=ALU.mult).then_inc(newton, 1)
                    dve.wait_ge(newton, refined + 1)
                    dve.tensor_scalar(tmp, tmp, -0.5, 1.5, ALU.mult, ALU.add).then_inc(newton, 1)
                    dve.wait_ge(newton, refined + 2)
                    dve.tensor_tensor(stat[:, 5, o:o + 1], y, tmp, ALU.mult).then_inc(newton, 1)
                    dve.wait_ge(newton, refined + 3)
                    refined += 3
                    if o == 0:
                        dve.wait_ge(small_loaded, 48)
                    if o >= 2:
                        dve.wait_ge(h_saved[o % 2], 16 * (o // 2))
                        dve.wait_ge(turned_ready, turns["norm", o - 2, 1] + 1)
                    dve.scalar_tensor_tensor(out=h[:, o % 2, :], in0=m.x[:, t, :], scalar=stat[:, 5, o:o + 1], in1=g[:, :],
                                             op0=ALU.mult, op1=ALU.mult).then_inc(h_ready, 1)
                for o, t in tiles_at(s, 8):
                    w = width(t)
                    for half in range(2):
                        pos = turns["norm", o, half]
                        dve.wait_ge(turned_ready, pos + 1)
                        if o and half == 0:
                            dve.wait_ge(logits_ready, o)
                        dve.tensor_copy(hT[:, 4 * half:4 * half + 4, 0:w],
                                        turned[:, pos % 2, :].rearrange("p (c n) -> p c n", c=4)[:, :, 0:w]).then_inc(turned_stored, 1)


def router_stage(nc, m, r, name):
    with ExitStack() as ctx:
        sb, ps, sem = tools(nc, ctx, name)
        logits = r.logits
        col = sb("col", [P, 14, NT])
        quad = sb("quad", [P, 10, NT, NG])
        wide = sb("wide", [P, NT, NE])
        chosen = sb("chosen", [P, NT, NE])
        chosen16 = sb("chosen16", [P, NT, NE], BF16)
        place = ps("place", [P, NT + 1, NE])
        chosen_ready, place_ready = sem("chosen_ready"), sem("place_ready")
        chain_sem, for_act, from_act = sem("chain"), sem("for_act"), sem("from_act")
        block = ctx.enter_context(nc.Block())

        @block.tensor
        def _(pe):
            pe.wait_ge(chosen_ready, 1)
            for t in range(NT + 1):
                for s in range(min(t, PT) + 1):
                    left = m.before[:, :] if s == t else m.ones16[:, :]
                    last = pe.matmul(place[:, t, :], left, chosen16[:, s, :], start=(s == 0), stop=(s == min(t, PT)))
            last.then_inc(place_ready, 1)

        @block.scalar
        def _(act):
            act.wait_ge(for_act, 1)
            act.activation(quad[:, 1], quad[:, 0], ACT.Exp).then_inc(from_act, 1)
            act.wait_ge(for_act, 2)
            act.activation(col[:, 5, :], col[:, 4, :], ACT.Exp).then_inc(from_act, 1)

        @block.vector
        def _(dve):
            step = Chain(dve, chain_sem)

            def over(x, n):
                return x.unsqueeze(2).broadcast_to([P, NT, n])

            first = m.consts[:, C_FIRST:C_FIRST + 4].unsqueeze(1).broadcast_to([P, NT, 4])

            def first_max(out, best, values, tmp):
                step(dve.tensor_tensor(tmp, values, over(best, 4), ALU.is_equal))
                step.wait()
                step(dve.tensor_tensor(tmp, tmp, first, ALU.mult))
                step.wait()
                step(dve.tensor_reduce(col[:, 13, :], tmp, AX.X, ALU.max))
                step.wait()
                step(dve.tensor_tensor(out, tmp, over(col[:, 13, :], 4), ALU.is_equal))
                step.wait()

            groups = logits[:, :, 0:NG]
            step(dve.tensor_reduce(col[:, 0, :], groups, AX.X, ALU.max))
            step.wait()
            dve.tensor_tensor(quad[:, 0], groups, over(col[:, 0, :], 4), ALU.subtract).then_inc(for_act, 1)
            first_max(quad[:, 2], col[:, 0, :], groups, quad[:, 3])
            experts = logits[:, :, NG:].rearrange("p t (g e) -> p t g e", g=NG)
            group_of = quad[:, 2].unsqueeze(3).broadcast_to([P, NT, NG, EPG])
            wide4 = wide[:, :, :].rearrange("p t (g e) -> p t g e", g=NG)
            step(dve.tensor_tensor(wide4, experts, group_of, ALU.mult))
            step.wait()
            step(dve.tensor_reduce(quad[:, 4], wide[:, :, :].rearrange("p t (g e) -> p t e g", g=NG), AX.X, ALU.add))
            step.wait()
            step(dve.tensor_reduce(col[:, 1, :], quad[:, 4], AX.X, ALU.max))
            step.wait()
            first_max(quad[:, 5], col[:, 1, :], quad[:, 4], quad[:, 3])
            step(dve.tensor_scalar(quad[:, 7], quad[:, 5], -1.0, 1.0, ALU.mult, ALU.add))
            step.wait()
            step(dve.tensor_tensor(quad[:, 7], quad[:, 7], quad[:, 4], ALU.mult))
            step.wait()
            step(dve.scalar_tensor_tensor(out=quad[:, 6], in0=quad[:, 5], scalar=TAKEN, in1=quad[:, 7], op0=ALU.mult, op1=ALU.add))
            step.wait()
            step(dve.tensor_reduce(col[:, 2, :], quad[:, 6], AX.X, ALU.max))
            step.wait()
            first_max(quad[:, 8], col[:, 2, :], quad[:, 6], quad[:, 3])
            dve.tensor_tensor(col[:, 4, :], col[:, 2, :], col[:, 1, :], ALU.subtract).then_inc(for_act, 1)
            step(dve.tensor_tensor(quad[:, 9], quad[:, 2], over(m.consts[:, C_VALID:C_VALID + NT], NG), ALU.mult))
            step.wait()
            group_of = quad[:, 9].unsqueeze(3).broadcast_to([P, NT, NG, EPG])
            for j, q in enumerate((5, 8)):
                step(dve.tensor_tensor(r.pick[:, j].rearrange("p t (g e) -> p t g e", g=NG), group_of,
                                       quad[:, q].unsqueeze(2).broadcast_to([P, NT, NG, EPG]), ALU.mult))
            step.wait()
            step(dve.tensor_tensor(chosen[:, :, :], r.pick[:, 0], r.pick[:, 1], ALU.add))
            step.wait()
            dve.tensor_copy(chosen16[:, :, :], chosen[:, :, :]).then_inc(chosen_ready, 1)
            dve.wait_ge(from_act, 2)
            step(dve.tensor_reduce(col[:, 3, :], quad[:, 1], AX.X, ALU.add))
            step(dve.tensor_scalar(col[:, 6, :], col[:, 5, :], 1.0, None, ALU.add))
            step.wait()
            step(dve.tensor_tensor(col[:, 7, :], col[:, 3, :], col[:, 6, :], ALU.mult))
            step.wait()
            step(dve.reciprocal(r.gate[:, 0, :], col[:, 7, :]))
            step.wait()
            step(dve.tensor_tensor(r.gate[:, 1, :], r.gate[:, 0, :], col[:, 5, :], ALU.mult))
            dve.wait_ge(place_ready, 1)
            for j in range(2):
                step(dve.tensor_tensor(wide[:, :, :], r.pick[:, j], place[:, 0:NT, :], ALU.mult))
                step.wait()
                step(dve.tensor_reduce(r.place[:, j, :], wide[:, :, :], AX.X, ALU.add))
                step.wait()
                step(dve.tensor_tensor(wide[:, :, :], r.pick[:, j],
                                       m.consts[:, C_EXPERT:C_EXPERT + NE].unsqueeze(1).broadcast_to([P, NT, NE]), ALU.mult))
                step.wait()
                step(dve.tensor_reduce(col[:, 8, :], wide[:, :, :], AX.X, ALU.add))
                step.wait()
                step(dve.tensor_scalar(r.expert_row[:, j, :], col[:, 8, :], float(P), None, ALU.mult))
            step(dve.tensor_reduce(col[:, 10, 0:1], place[:, NT, :], AX.X, ALU.max))
            step.wait()
            step(dve.tensor_copy(r.most[0:1, 0:1], col[0:1, 10, 0:1]))
            step.wait()



def expert_stage(nc, m, r, name, layer, io):
    with ExitStack() as ctx:
        sb, ps, sem = tools(nc, ctx, name)
        take = sb("take", [P, 2, P])
        value = sb("value", [P, 2, NE])
        slots = sb("slots", [P, NE], U32)
        slot_col = sb("slot_col", [P, 2], U32)
        xg = sb("xg", [P, 2, D])
        xT = sb("xT", [P, 2, DC, P])
        silu = sb("silu", [P, 2, FE])
        act_rows = sb("act_rows", [P, 2, FE])
        actT = sb("actT", [P, 2, 2, P])
        y = sb("y", [P, 2, D])
        got = sb("got", [P, 4, D])
        served = sb("served", [P, 2, NT])
        pass_gate = sb("pass_gate", [P, 2, NT])
        row = sb("row", [P, 2, NT])
        result_row = sb("result_row", [P, 2, NT], U32)
        turned = ps("turned", [P, 2, 512])
        hidden = ps("hidden", [P, 2, 2 * FE])
        act_turned_ps = ps("act_turned_ps", [P, 2, 2, P])
        down = ps("down", [P, 2, 512])
        table = ps("table", [P, 512])
        ring = sb("ring", [P, 3 * 4096])
        w_hidden = [ring[:, b * 6144:b * 6144 + 4096].rearrange("p (c n) -> p c n", c=DC) for b in range(2)]
        w_down = [ring[:, b * 6144 + 4096:(b + 1) * 6144].rearrange("p (c n) -> p c n", c=2) for b in range(2)]
        hidden_loaded = [sem("hidden_loaded0"), sem("hidden_loaded1")]
        down_loaded = [sem("down_loaded0"), sem("down_loaded1")]
        gathered = [sem("gathered0", kept=True), sem("gathered1", kept=True)]
        saved = [sem("saved0"), sem("saved1")]
        take_ready, take_used, table_ready, slots_ready = sem("take_ready"), sem("take_used"), sem("table_ready"), sem("slots_ready")
        col_ready, x_turned, xT_low, xT_high = sem("col_ready"), sem("x_turned"), sem("xT_low"), sem("xT_high")
        hidden_ready, silu_ready, act_ready = sem("hidden_ready"), sem("silu_ready"), sem("act_ready")
        act_turned, actT_ready, down_ready, y_low, y_high = sem("act_turned"), sem("actT_ready"), sem("down_ready"), sem("y_low"), sem("y_high")
        moved, passed, prepared, added = sem("moved"), sem("passed"), sem("prepared"), sem("added")
        got_ready = [sem(f"got_ready{b}", kept=True) for b in range(4)]
        block = ctx.enter_context(nc.Block())
        PICKS = 2 * NT
        USES = [len(range(b, PICKS, 4)) for b in range(4)]

        def wait_count(eng, signal, count):
            if not isinstance(count, int) or count > 0:
                eng.wait_ge(signal, count)

        def first_wait(eng, signal, count):
            if not isinstance(count, int) or count > 0:
                eng.wait_ge(signal, count)
                eng.sem_inc(passed, 1)

        def all_passes(eng, one_pass):
            one_pass(0)
            most = eng.value_load(r.most[0:1, 0:1], min_val=0, max_val=T)
            with eng.If(most > SLOTS):
                with eng.Fori(1, PASSES) as c:
                    one_pass(c)

        def steps(eng, c, step):
            with eng.Fori(0, 6) as i:
                for j in range(2):
                    step(i * 2 + 3 + j, c * NE + i * 2 + (3 + j), c * (NE // 2) + i + (1 + j), 1 - j)

        def fixed(c, e, step):
            step(e, c * NE + e, c * (NE // 2) + e // 2, e % 2)

        @block.sync
        def _(sp):
            def load_hidden(e, n, k, b):
                first_wait(sp, hidden_ready, n - 1)
                for j, w in enumerate((io["moe_w_gate"], io["moe_w_up"])):
                    sp.dma_start(w_hidden[b][:, :, j * FE:(j + 1) * FE],
                                 w[layer, bass.ds(e, 1)].rearrange("a (c p) f -> p (a c) f", p=P)).then_inc(hidden_loaded[b], 16)

            def load_down(e, n, k, b):
                first_wait(sp, down_ready, n - 1)
                sp.dma_start(w_down[b], io["moe_w_down"][layer, bass.ds(e, 1)].rearrange("a (c p) d -> p (a c) d", p=P)).then_inc(down_loaded[b], 16)

            def save(c):
                def body(e, n, k, b):
                    sp.wait_ge(y_low, n + 1)
                    first_wait(sp, y_high, n + 1)
                    sp.dma_start(r.y_dram.rearrange("(e p) d -> e p d", p=P)[bass.ds(e, 1)].rearrange("a p d -> (a p) d"),
                                 y[:, b, :]).then_inc(saved[b], 16)
                return body

            def one_pass(c):
                first_wait(sp, added, c * PICKS)
                for e in range(3):
                    fixed(c, e, load_hidden)
                    fixed(c, e, load_down)

                def step(e, n, k, b):
                    load_hidden(e, n, k, b)
                    save(c)(e - 3, n - 3, None, 1 - b)
                    load_down(e, n, k, b)

                steps(sp, c, step)
                fixed(c, NE - 1, step)
                for e in range(NE - 3, NE):
                    fixed(c, e, save(c))

            all_passes(sp, one_pass)

        @block.gpsimd
        def _(pool):
            def gather(e, n, k, b):
                first_wait(pool, x_turned, n - 1)
                pool.tensor_copy(slot_col[:, b:b + 1], slots[:, bass.ds(e, 1)]).then_inc(col_ready, 1)
                first_wait(pool, col_ready, n + 1)
                pool.indirect_dma_start(xg[:, b, :], None, r.h_dram, bass.IndirectOffsetOnAxis(slot_col[:, b:b + 1], 0)).then_inc(gathered[b], 16)

            def one_pass(c):
                pool.wait_ge(slots_ready, c + 1)
                for e in range(3):
                    fixed(c, e, gather)
                steps(pool, c, gather)
                fixed(c, NE - 1, gather)
                for b in range(2):
                    first_wait(pool, saved[b], (c + 1) * (16 * NE // 2))
                for i in range(PICKS):
                    t, j = divmod(i, 2)
                    w = width(t)
                    first_wait(pool, added, c * PICKS + max(i - 3, 0))
                    pool.indirect_dma_start(got[0:w, i % 4, :], None, r.y_dram,
                                            bass.IndirectOffsetOnAxis(result_row[0:w, j, t:t + 1], 0)).then_inc(got_ready[i % 4], 16)

            all_passes(pool, one_pass)

        @block.tensor
        def _(pe):
            def turn_x(e, n, k, b):
                pe.wait_ge(gathered[b], (k + 1) * 16)
                wait_count(pe, xT_low, n)
                wait_count(pe, xT_high, n)
                for c in range(DC):
                    last = pe.transpose(turned[:, c // 4, (c % 4) * P:(c % 4 + 1) * P], xg[:, b, c * P:(c + 1) * P], m.ident[:, :])
                last.then_inc(x_turned, 1)

            def make_hidden(e, n, k, b):
                pe.wait_ge(xT_low, n + 1)
                pe.wait_ge(xT_high, n + 1)
                pe.wait_ge(hidden_loaded[b], (k + 1) * 32)
                wait_count(pe, act_ready, n - 1)
                for c in range(DC):
                    last = pe.matmul(hidden[:, b, :], xT[:, b, c, :], w_hidden[b][:, c, :], start=(c == 0), stop=(c == DC - 1))
                last.then_inc(hidden_ready, 1)

            def turn_act(e, n, k, b):
                pe.wait_ge(act_ready, n + 1)
                for c in range(2):
                    last = pe.transpose(act_turned_ps[:, b, c, :], act_rows[:, b, c * P:(c + 1) * P], m.ident[:, :])
                last.then_inc(act_turned, 1)

            def make_down(e, n, k, b):
                pe.wait_ge(actT_ready, n + 1)
                pe.wait_ge(down_loaded[b], (k + 1) * 16)
                wait_count(pe, y_low, n)
                wait_count(pe, y_high, n)
                for half in range(2):
                    for c in range(2):
                        last = pe.matmul(down[:, half, :], actT[:, b, c, :], w_down[b][:, c, half * 512:(half + 1) * 512], start=(c == 0), stop=(c == 1))
                last.then_inc(down_ready, 1)

            def one_pass(c):
                for i in range(PICKS):
                    pe.wait_ge(take_ready, c * PICKS + i + 1)
                    rows = width(i // 2)
                    pe.matmul(table[:, 0:NE], take[0:rows, i % 2, :], value[0:rows, i % 2, :], start=(i == 0), stop=(i == PICKS - 1)).then_inc(take_used, 1)
                fixed(c, 0, turn_x)
                fixed(c, 0, make_hidden)
                fixed(c, 1, turn_x)

                def step(e, n, k, b, more=True):
                    half = k - 1 + b
                    make_hidden(e, n, k, b)
                    turn_act(e - 1, n - 1, half, 1 - b)
                    if more:
                        turn_x(e + 1, n + 1, k + b, 1 - b)
                    make_down(e - 1, n - 1, half, 1 - b)

                fixed(c, 1, step)
                fixed(c, 2, step)
                steps(pe, c, step)
                fixed(c, NE - 1, lambda e, n, k, b: step(e, n, k, b, more=False))
                fixed(c, NE - 1, turn_act)
                fixed(c, NE - 1, make_down)

            all_passes(pe, one_pass)

        @block.scalar
        def _(act):
            def store_xT(e, n, k, b):
                act.wait_ge(x_turned, n + 1)
                act.activation(xT[:, b, 0:4, :], turned[:, 0, :].rearrange("p (c n) -> p c n", c=4), ACT.Copy).then_inc(xT_low, 1)

            def gate(e, n, k, b):
                act.wait_ge(hidden_ready, n + 1)
                wait_count(act, act_ready, n - 1)
                act.activation(silu[:, b, :], hidden[:, b, 0:FE], ACT.Silu).then_inc(silu_ready, 1)

            def store_y(e, n, k, b):
                act.wait_ge(down_ready, n + 1)
                if not isinstance(k, int) or k > 0:
                    act.wait_ge(saved[b], k * 16)
                act.activation(y[:, b, 0:512], down[:, 0, :], ACT.Copy).then_inc(y_low, 1)

            def one_pass(c):
                fixed(c, 0, store_xT)
                fixed(c, 1, store_xT)

                def step(e, n, k, b, more=True):
                    half = k - 1 + b
                    gate(e - 1, n - 1, half, 1 - b)
                    if more:
                        store_xT(e + 1, n + 1, k + b, 1 - b)
                    store_y(e - 1, n - 1, half, 1 - b)

                fixed(c, 1, step)
                fixed(c, 2, step)
                steps(act, c, step)
                fixed(c, NE - 1, lambda e, n, k, b: step(e, n, k, b, more=False))
                fixed(c, NE - 1, gate)
                fixed(c, NE - 1, store_y)

            all_passes(act, one_pass)

        @block.vector
        def _(dve):
            def store_xT(e, n, k, b):
                dve.wait_ge(x_turned, n + 1)
                dve.tensor_copy(xT[:, b, 4:8, :], turned[:, 1, :].rearrange("p (c n) -> p c n", c=4)).then_inc(xT_high, 1)

            def multiply(e, n, k, b):
                dve.wait_ge(silu_ready, n + 1)
                wait_count(dve, act_turned, n - 1)
                dve.tensor_tensor(act_rows[:, b, :], hidden[:, b, FE:2 * FE], silu[:, b, :], ALU.mult).then_inc(act_ready, 1)

            def store_actT(e, n, k, b):
                dve.wait_ge(act_turned, n + 1)
                wait_count(dve, down_ready, n - 1)
                dve.tensor_copy(actT[:, b, :, :], act_turned_ps[:, b, :, :]).then_inc(actT_ready, 1)

            def store_y(e, n, k, b):
                dve.wait_ge(down_ready, n + 1)
                if not isinstance(k, int) or k > 0:
                    dve.wait_ge(saved[b], k * 16)
                dve.tensor_copy(y[:, b, 512:1024], down[:, 1, :]).then_inc(y_high, 1)

            def one_pass(c):
                if not isinstance(c, int):
                    dve.tensor_scalar(r.place[:, :, :], r.place[:, :, :], float(-SLOTS), None, ALU.add).then_inc(moved, 1)
                    dve.wait_ge(moved, c)
                p0 = c * 4
                dve.tensor_scalar(served[:, :, :], r.place[:, :, :], 0.0, None, ALU.is_ge).then_inc(prepared, 1)
                dve.wait_ge(prepared, p0 + 1)
                dve.scalar_tensor_tensor(out=served[:, :, :], in0=r.place[:, :, :], scalar=float(SLOTS), in1=served[:, :, :], op0=ALU.is_lt, op1=ALU.mult)
                dve.tensor_tensor(row[:, :, :], r.place[:, :, :], r.expert_row[:, :, :], ALU.add).then_inc(prepared, 1)
                dve.wait_ge(prepared, p0 + 2)
                dve.tensor_tensor(pass_gate[:, :, :], r.gate[:, :, :], served[:, :, :], ALU.mult)
                dve.tensor_tensor(row[:, :, :], row[:, :, :], served[:, :, :], ALU.mult).then_inc(prepared, 1)
                dve.wait_ge(prepared, p0 + 3)
                dve.tensor_copy(result_row[:, :, :], row[:, :, :]).then_inc(prepared, 1)
                dve.wait_ge(prepared, p0 + 4)
                for i in range(PICKS):
                    t, j = divmod(i, 2)
                    wait_count(dve, take_used, c * PICKS + (i - 1))
                    dve.tensor_scalar(take[:, i % 2, :], m.consts[:, C_SLOT:C_SLOT + P], r.place[:, j, t:t + 1], None, ALU.is_equal)
                    dve.tensor_scalar(value[:, i % 2, :], r.pick[:, j, t, :], m.consts[:, C_TOKEN + t:C_TOKEN + t + 1], None, ALU.mult).then_inc(take_ready, 1)
                dve.wait_ge(take_used, c * PICKS + PICKS)
                if not isinstance(c, int):
                    dve.wait_ge(x_turned, c * NE)
                dve.tensor_copy(slots[:, :], table[:, 0:NE]).then_inc(slots_ready, 1)
                fixed(c, 0, store_xT)
                fixed(c, 1, store_xT)

                def step(e, n, k, b, more=True):
                    half = k - 1 + b
                    multiply(e - 1, n - 1, half, 1 - b)
                    store_actT(e - 1, n - 1, half, 1 - b)
                    if more:
                        store_xT(e + 1, n + 1, k + b, 1 - b)
                    store_y(e - 1, n - 1, half, 1 - b)

                fixed(c, 1, step)
                fixed(c, 2, step)
                steps(dve, c, step)
                fixed(c, NE - 1, lambda e, n, k, b: step(e, n, k, b, more=False))
                for last in (multiply, store_actT, store_y):
                    fixed(c, NE - 1, last)
                for i in range(PICKS):
                    t, j = divmod(i, 2)
                    w = width(t)
                    x = m.x[0:w, t, :]
                    dve.wait_ge(got_ready[i % 4], (c * USES[i % 4] + (i // 4 + 1)) * 16)
                    if j:
                        dve.wait_ge(added, c * PICKS + i)
                    dve.scalar_tensor_tensor(out=x, in0=got[0:w, i % 4, :], scalar=pass_gate[0:w, j, t:t + 1], in1=x,
                                             op0=ALU.mult, op1=ALU.add).then_inc(added, 1)

            all_passes(dve, one_pass)


def project_dsa_stage(nc, m, a, io):
    with ExitStack() as ctx:
        sb, ps, sem = tools(nc, ctx, "dsa")
        rope = sb("rope", [P, R_COLS])
        idx_rows = sb("idx_rows", [P, 2, IDX_COLS])
        idx_rot = sb("idx_rot", [P, 2, 6, D_IDX])
        idx_tmp = sb("idx_tmp", [P, 2, 5, D_IDX])
        idx_w = sb("idx_w", [P, NT, H_IDX])
        cache_i = sb("cache_i", [P, 2, 2, D_IDX])
        cache_k = sb("cache_k", [P, 2, KV_DSA * HEAD])
        qiT = sb("qiT", [P, 2, T])
        kiT = sb("kiT", [P, PROMPT])
        kiT_sample = sb("kiT_sample", [P, LS])
        relu = sb("relu", [P, 2, 512])
        rows = sb("rows", [P, 2, 512])
        rot = sb("rot", [P, 2, 512])
        tmp = sb("tmp", [P, 2, 512])
        acc = ps("acc", [P, 4, 512])
        turned = ps("turned", [P, 2, 512])
        logit = ps("logit", [P, 2, 512])
        ring = sb("ring", [P, 3 * 4096])
        w_slot = [ring[:, s * 4096:(s + 1) * 4096].rearrange("p (c n) -> p c n", c=DC) for s in range(3)]
        w_loaded = [sem(f"w_loaded{s}") for s in range(3)]
        small_loaded, cache_v_loaded, idx_done = sem("small_loaded"), sem("cache_v_loaded"), sem("idx_done")
        group_ready, group_stored = sem("group_ready"), sem("group_stored")
        idx_chain, idx_rot_ready, pool_chain, rot_ready = sem("idx_chain"), sem("idx_rot_ready"), sem("pool_chain"), sem("rot_ready")
        idx_turned, idx_T_stored = sem("idx_turned"), sem("idx_T_stored")
        logit_ready, relu_ready, score_step = sem("logit_ready"), sem("relu_ready"), sem("score_step")
        rows_turned, rows_T_stored = sem("rows_turned"), sem("rows_T_stored")
        best_found, best_taken, barred = sem("best_found"), sem("best_taken"), sem("barred")
        idx_saved = [sem("idx_saved0"), sem("idx_saved1")]
        k_saved = [sem("k_saved0"), sem("k_saved1")]
        v_saved = sem("v_saved")
        block = ctx.enter_context(nc.Block())

        BLOCKS = [(1536, IDX_COLS), (0, 512), (512, 512), (1024, 512)]
        NI = NT
        NR = 3 * NT
        TILES = [3, PT, 2, 1]
        SCORES = [(t, h) for t in TILES for h in range(H_IDX)]
        SIZE = {t: (LS if t == PT else (t + 1) * P) for t in TILES}
        ROUNDS = {t: (K_SAMPLE if t == PT else K_PROMPT) // 8 for t in TILES}
        best = {t: sb(f"best{t}", [P, 8]) for t in TILES}
        score = {t: sb(f"score{t}", [P, SIZE[t]]) for t in TILES}

        @block.sync
        def _(sp):
            w_view = io["w_in_dsa"].rearrange("(c p) n -> p c n", p=P)

            def load_block(b):
                lo, n = BLOCKS[b]
                sp.dma_start(w_slot[b % 3][:, :, 0:n], w_view[:, :, lo:lo + n]).then_inc(w_loaded[b % 3], 16)

            load_block(0)
            sp.dma_start(rope[:, :], io["rope"]).then_inc(small_loaded, 16)
            for twice in range(2):
                sp.dma_start(cache_i[:, :, twice, :], io["cache_dsa_idx_k"].rearrange("b (j p) e -> p (b j) e", p=P)).then_inc(small_loaded, 16)
            sp.dma_start(cache_k[:, :, :], io["cache_dsa_k"].rearrange("b (j p) h d -> p (b j) (h d)", p=P)).then_inc(small_loaded, 16)
            load_block(1)
            load_block(2)
            sp.dma_start(a.cache_v[:, :, :], io["cache_dsa_v"].rearrange("b (j p) h d -> p (b j) (h d)", p=P)).then_inc(cache_v_loaded, 16)
            for t in range(NT):
                w = width(t)
                sp.wait_ge(idx_rot_ready, t + 1)
                dst = io["out_dsa_idx"][0].rearrange("b t e -> (b t) e")[t * P:(t + 1) * P, :] if t < PT else io["out_dsa_idx"][1].rearrange("b t e -> (b t) e")
                sp.dma_start(dst, idx_rot[0:w, t % 2, 4, :]).then_inc(idx_saved[t % 2], 16)
            sp.wait_ge(idx_done, 1)
            load_block(3)
            for t in range(NT):
                w = width(t)
                g = 2 * NT + t
                sp.wait_ge(rot_ready, g + 1)
                sp.dma_start(rows_of(io["out_dsa_k"], t), rot[0:w, g % 2, 0:256]).then_inc(k_saved[g % 2], 16)
            for t in range(NT):
                w = width(t)
                sp.wait_ge(group_stored, NI + 2 * NT + t + 1)
                sp.dma_start(rows_of(io["out_dsa_v"], t), a.v_rows[0:w, t, :]).then_inc(v_saved, 16)
            sp.wait_ge(idx_saved[0], 48)
            sp.wait_ge(idx_saved[1], 32)
            sp.wait_ge(k_saved[0], 48)
            sp.wait_ge(k_saved[1], 32)
            sp.wait_ge(v_saved, 16 * NT)
            sp.wait_ge(cache_v_loaded, 16)

        @block.tensor
        def _(pe):
            def group(g, block_no, t, n):
                w = width(t)
                if g >= 4:
                    pe.wait_ge(group_stored, g - 3)
                for c in range(DC):
                    last = pe.matmul(acc[0:w, g % 4, 0:n], m.hT[:, c, cols(t)], w_slot[block_no % 3][:, c, 0:n], start=(c == 0), stop=(c == DC - 1))
                last.then_inc(group_ready, 1)

            def turn_idx(t):
                w = width(t)
                pe.wait_ge(idx_rot_ready, t + 1)
                pe.wait_ge(idx_T_stored, t + 1)
                for j in range(3):
                    last = pe.transpose(turned[:, t % 2, j * P:j * P + w], idx_rot[0:w, t % 2, 2 * j:2 * j + 2, :].rearrange("p h e -> p (h e)"), m.ident[0:w, 0:w])
                last.then_inc(idx_turned, 1)

            pe.wait_ge(small_loaded, 64)
            for kb in range(2):
                for h in range(2):
                    last = pe.transpose(turned[:, 0, (2 * h + kb) * P:(2 * h + kb + 1) * P], cache_k[:, kb, h * P:(h + 1) * P], m.ident[:, :])
            last.then_inc(idx_turned, 1)
            for kb in range(2):
                last = pe.transpose(turned[:, 1, kb * P:(kb + 1) * P], cache_i[:, kb, :, :].rearrange("p a e -> p (a e)"), m.ident[:, :])
            last.then_inc(idx_turned, 1)
            pe.wait_ge(w_loaded[0], 16)
            for t in range(NT):
                group(t, 0, t, IDX_COLS)
                if t >= 1:
                    turn_idx(t - 1)
            pe.drain().then_inc(idx_done, 1)
            turn_idx(NT - 1)
            pe.wait_ge(idx_T_stored, 2 + NT)
            for i, (t, h) in enumerate(SCORES):
                half = slice((h % 2) * 64, (h % 2) * 64 + 64)
                w = width(t)
                if i >= 2:
                    pe.wait_ge(relu_ready, i - 1)
                keys = kiT_sample[half, :] if t == PT else kiT[half, 0:SIZE[t]]
                pe.matmul(logit[0:w, i % 2, 0:SIZE[t]], qiT[half, h // 2, cols(t)], keys, start=True, stop=True).then_inc(logit_ready, 1)

            def turn_rows(i):
                b, t = divmod(i, NT)
                w = width(t)
                pe.wait_ge(rot_ready, i + 1)
                if i >= 2:
                    pe.wait_ge(rows_T_stored, i - 1)
                for h in range(4 if b < 2 else 2):
                    last = pe.transpose(turned[:, i % 2, h * P:h * P + w], rot[0:w, i % 2, h * P:(h + 1) * P], m.ident[0:w, 0:w])
                last.then_inc(rows_turned, 1)

            for i in range(NR):
                b, t = divmod(i, NT)
                if t == 0:
                    pe.wait_ge(w_loaded[(b + 1) % 3], 32 if b == 2 else 16)
                group(NI + i, b + 1, t, 512)
                if i >= 2:
                    turn_rows(i - 2)
            turn_rows(NR - 2)
            turn_rows(NR - 1)

        @block.scalar
        def _(act):
            for t in range(NT):
                w = width(t)
                act.wait_ge(group_ready, t + 1)
                if t >= 2:
                    act.wait_ge(idx_rot_ready, t - 1)
                act.activation(idx_rows[0:w, t % 2, :], acc[0:w, t % 4, 0:IDX_COLS], ACT.Copy).then_inc(group_stored, 1)
            for i, (t, h) in enumerate(SCORES):
                w = width(t)
                act.wait_ge(logit_ready, i + 1)
                if i >= 2:
                    act.wait_ge(score_step, i - 1)
                act.activation(relu[0:w, i % 2, 0:SIZE[t]], logit[0:w, i % 2, 0:SIZE[t]], ACT.Relu, scale=D_IDX ** -0.5).then_inc(relu_ready, 1)

            def store_T(i):
                b, t = divmod(i, NT)
                w = width(t)
                act.wait_ge(rows_turned, i + 1)
                src = turned[:, i % 2, :].rearrange("p (h n) -> p h n", h=4)
                if b < 2:
                    dst, n = a.qT[:, 4 * b:4 * b + 4, cols(t)], 4
                else:
                    dst, n = (a.kT[:, :, t * P:(t + 1) * P] if t < PT else a.kT_sample[:, :, PAST:LS]), 2
                act.activation(dst, src[:, 0:n, 0:w], ACT.Copy).then_inc(rows_T_stored, 1)

            for i in range(NR):
                b, t = divmod(i, NT)
                w = width(t)
                g = NI + i
                act.wait_ge(group_ready, g + 1)
                if i >= 2:
                    act.wait_ge(rot_ready, i - 1)
                if b < 2:
                    act.activation(rows[0:w, i % 2, :], acc[0:w, g % 4, :], ACT.Copy, scale=SCALE).then_inc(group_stored, 1)
                else:
                    act.activation(rows[0:w, i % 2, 0:256], acc[0:w, g % 4, 0:256], ACT.Copy)
                    act.activation(a.v_rows[0:w, t, :], acc[0:w, g % 4, 256:512], ACT.Copy).then_inc(group_stored, 1)
                if i >= 2:
                    store_T(i - 2)
            store_T(NR - 2)
            store_T(NR - 1)

        def rotate(eng, chain, out, x, tmp_a, tmp_b, cos, sin, heads):
            w, half = x.shape[0], x.shape[2] // 2
            swapped = x.rearrange("p h (s e) -> p h s e", s=2)[:, :, ::-1, :]
            chain(eng.tensor_tensor(tmp_a, x, cos.unsqueeze(1).broadcast_to([w, heads, 2 * half]), ALU.mult))
            chain(eng.tensor_tensor(tmp_b.rearrange("p h (s e) -> p h s e", s=2), swapped,
                                    sin.rearrange("p (s e) -> p s e", s=2).unsqueeze(1).broadcast_to([w, heads, 2, half]), ALU.mult))
            chain.wait()
            return eng.tensor_tensor(out, tmp_a, tmp_b, ALU.add)

        @block.gpsimd
        def _(pool):
            chain = Chain(pool, pool_chain)
            pool.wait_ge(small_loaded, 64)
            for i in range(NR):
                b, t = divmod(i, NT)
                w = width(t)
                heads = 4 if b < 2 else 2
                pool.wait_ge(group_stored, NI + i + 1)
                if i >= 2:
                    pool.wait_ge(rows_turned, i - 1)
                if i >= 2 * NT + 2:
                    pool.wait_ge(k_saved[i % 2], 16 * ((i - 2 * NT) // 2))

                def view(x):
                    return x.rearrange("p (h d) -> p h d", d=HEAD)

                n = heads * HEAD
                rotate(pool, chain, view(rot[0:w, i % 2, 0:n]), view(rows[0:w, i % 2, 0:n]), view(tmp[0:w, 0, 0:n]), view(tmp[0:w, 1, 0:n]),
                       rope[0:w, R_COS + t * HEAD:R_COS + (t + 1) * HEAD], rope[0:w, R_SIN + t * HEAD:R_SIN + (t + 1) * HEAD], heads).then_inc(rot_ready, 1)
                pool.wait_ge(rot_ready, i + 1)

        @block.vector
        def _(dve):
            chain = Chain(dve, idx_chain)
            dve.wait_ge(idx_turned, 1)
            dve.tensor_copy(a.kT_sample[:, :, 0:PAST], turned[:, 0, :].rearrange("p (h n) -> p h n", h=2)).then_inc(idx_T_stored, 1)
            dve.wait_ge(idx_turned, 2)
            dve.tensor_copy(kiT_sample[:, 0:PAST], turned[:, 1, 0:PAST]).then_inc(idx_T_stored, 1)

            def store_idx_T(t):
                w = width(t)
                dve.wait_ge(idx_turned, 3 + t)
                dve.tensor_copy(qiT[:, :, cols(t)], turned[:, t % 2, 0:2 * P].rearrange("p (h n) -> p h n", h=2)[:, :, 0:w])
                dst = kiT[:, t * P:(t + 1) * P] if t < PT else kiT_sample[:, PAST:LS]
                dve.tensor_copy(dst, turned[:, t % 2, 2 * P:2 * P + w]).then_inc(idx_T_stored, 1)

            dve.wait_ge(small_loaded, 64)
            for t in range(NT):
                w = width(t)
                dve.wait_ge(group_stored, t + 1)
                if t >= 2:
                    dve.wait_ge(idx_turned, 2 + t - 1)
                    dve.wait_ge(idx_saved[t % 2], 16 * (t // 2))
                x = idx_rows[0:w, t % 2, 0:5 * D_IDX].rearrange("p (h e) -> p h e", h=5)
                chain(rotate(dve, chain, idx_rot[0:w, t % 2, 0:5, :], x, idx_tmp[0:w, 0], idx_tmp[0:w, 1],
                             rope[0:w, R_ICOS + t * D_IDX:R_ICOS + (t + 1) * D_IDX], rope[0:w, R_ISIN + t * D_IDX:R_ISIN + (t + 1) * D_IDX], 5))
                chain(dve.tensor_scalar(idx_w[0:w, t, :], idx_rows[0:w, t % 2, 5 * D_IDX:IDX_COLS], H_IDX ** -0.5, None, ALU.mult))
                chain.wait()
                dve.tensor_copy(idx_rot[0:w, t % 2, 5, :], idx_rot[0:w, t % 2, 4, :]).then_inc(idx_rot_ready, 1)
                if t >= 1:
                    store_idx_T(t - 1)
            store_idx_T(NT - 1)
            for i, (t, h) in enumerate(SCORES):
                w = width(t)
                s = score[t][0:w, :]
                dve.wait_ge(relu_ready, i + 1)
                if h == 0:
                    dve.tensor_scalar(s, relu[0:w, i % 2, 0:SIZE[t]], idx_w[0:w, t, 0:1], None, ALU.mult).then_inc(score_step, 1)
                else:
                    dve.wait_ge(score_step, i)
                    dve.scalar_tensor_tensor(out=s, in0=relu[0:w, i % 2, 0:SIZE[t]], scalar=idx_w[0:w, t, h:h + 1], in1=s,
                                             op0=ALU.mult, op1=ALU.add).then_inc(score_step, 1)
            dve.wait_ge(score_step, len(SCORES))
            for t in (3, 2, 1):
                last = dve.memset(score[t][0:CHUNK, SIZE[t] - CHUNK:SIZE[t]], BARRED)
            last.then_inc(barred, 1)
            dve.wait_ge(barred, 1)
            found = taken = 0
            for k in range(max(ROUNDS.values())):
                live = [t for t in TILES if k < ROUNDS[t]]
                if k:
                    dve.wait_ge(best_taken, taken)
                for t in live:
                    dve.max(best[t][0:width(t), :], score[t][0:width(t), :]).then_inc(best_found, 1)
                for j, t in enumerate(live):
                    dve.wait_ge(best_found, found + j + 1)
                    dve.match_replace(score[t][0:width(t), :], best[t][0:width(t), :], score[t][0:width(t), :], TAKEN).then_inc(best_taken, 1)
                found += len(live)
                taken += len(live)
            dve.wait_ge(best_taken, taken)
            for t in TILES:
                dve.tensor_scalar(a.unchosen[t][0:width(t), :], score[t][0:width(t), :], UNTAKEN_FROM, NEG, ALU.is_gt, ALU.mult)


def trunk_program(nc, io):
    with ExitStack() as ctx:
        def sb(name, shape, dtype=F32):
            return ctx.enter_context(nc.sbuf_tensor(name, shape, dtype))

        m = Main()
        m.x = sb("x", [P, NT, D])
        m.hT = sb("hT", [P, DC, T])
        m.consts = sb("consts", [P, C_COLS])
        m.masks = sb("masks", [P, 4 * P], BF16)
        m.before = sb("before", [P, P], BF16)
        m.ones16 = sb("ones16", [P, P], BF16)
        m.ones = sb("ones", [P, 512])
        m.head_select = sb("head_select", [H_FOX, H_FOX * P])
        m.ident = m.consts[:, C_IDENT:C_IDENT + P]
        m.ident16 = m.masks[:, C_IDENT:C_IDENT + P]
        neg_sb, neg_fox, neg_chunk = (m.masks[:, c:c + P] for c in (C_NEG_SB, C_NEG_FOX, C_NEG_CHUNK))
        load_stage(nc, m, io)

        def routing(layer, scope):
            def sb(name, shape, dtype=F32):
                return scope.enter_context(nc.sbuf_tensor(f"moe{layer}_{name}", shape, dtype))

            r = Routing()
            r.w_group, r.w_router = io["moe_w_group"][layer], io["moe_w_router"][layer]
            r.logits = sb("logits", [P, NT, NG + NE])
            r.pick = sb("pick", [P, 2, NT, NE])
            r.place = sb("place", [P, 2, NT])
            r.gate = sb("gate", [P, 2, NT])
            r.expert_row = sb("expert_row", [P, 2, NT])
            r.most = sb("most", [P, 1], U32)
            r.h_dram = nc.dram_tensor(f"h_dram{layer}", (T, D), F32, kind="Internal").ap()
            r.y_dram = nc.dram_tensor(f"y_dram{layer}", (NE * P, D), F32, kind="Internal").ap()
            return r

        def tile_steps(pairs, sample):
            steps = [(sample, True)]
            for t in range(PT):
                steps += [([Unit([h], t, stick) for h, stick in pair], j == len(pairs) - 1) for j, pair in enumerate(pairs)]
            return steps

        r0, r1 = routing(0, ctx), routing(1, ctx)
        norm_stage(nc, m, "mix0", io["norm_mix"][0], m.hT)
        with ExitStack() as inner:
            def sb(name, shape, dtype=F32):
                return inner.enter_context(nc.sbuf_tensor(f"ab_{name}", shape, dtype))

            a = Attention()
            a.qT = sb("qT", [P, 8, T])
            a.kT = sb("kT", [P, 8, PROMPT])
            a.kT_sample = sb("kT_sample", [P, 8, LS])
            a.v_rows = sb("v_rows", [P, NT, D])
            a.cache_v = sb("cache_v", [P, 2, D])
            a.forget = sb("forget", [4, PROMPT])
            a.forget_sample = sb("forget_sample", [4, LS])
            project_ab_stage(nc, m, a, io)
            pairs = [((h, True), (h + H_SB, False)) for h in range(H_SB)]
            sample = [Unit(list(range(h0, h0 + 4)), PT, h0 == 0) for h0 in (0, H_SB)]
            mixer_stage(nc, m, a, r0, "mixer0", tile_steps(pairs, sample), lambda h: h, lambda h: h, {True: neg_sb, False: neg_fox}, True,
                        io["w_out_ab"], io["norm_ffn"][0], split=False)
        router_stage(nc, m, r0, "route0")
        expert_stage(nc, m, r0, "experts0", 0, io)

        norm_stage(nc, m, "mix1", io["norm_mix"][1], m.hT)
        with ExitStack() as inner:
            def sb(name, shape, dtype=F32):
                return inner.enter_context(nc.sbuf_tensor(f"dsa_{name}", shape, dtype))

            a = Attention()
            a.qT = sb("qT", [P, H_DSA, T])
            a.kT = sb("kT", [P, KV_DSA, PROMPT])
            a.kT_sample = sb("kT_sample", [P, KV_DSA, LS])
            a.v_rows = sb("v_rows", [P, NT, KV_DSA * HEAD])
            a.cache_v = sb("cache_v", [P, 2, KV_DSA * HEAD])
            a.unchosen = {t: sb(f"unchosen{t}", [P, LS if t == PT else (t + 1) * P], BF16) for t in range(1, NT)}
            a.unchosen[0] = neg_chunk
            project_dsa_stage(nc, m, a, io)
            kv = lambda h: h // (H_DSA // KV_DSA)
            pairs = [((h, False), (h + 1, False)) for h in range(0, H_DSA, 2)]
            sample = [Unit(list(range(h0, h0 + 4)), PT) for h0 in (0, 4)]
            mixer_stage(nc, m, a, r1, "mixer1", tile_steps(pairs, sample), kv, kv, {False: None}, False,
                        io["w_out_dsa"], io["norm_ffn"][1], split=True)
        router_stage(nc, m, r1, "route1")
        expert_stage(nc, m, r1, "experts1", 1, io)
        y = [io["y_prompt"].rearrange("b t d -> (b t) d"), io["y_sample"].rearrange("b t d -> (b t) d")]
        norm_stage(nc, m, "final", io["norm_final"], y_dram=y)


_INS = ["x_prompt", "x_sample", "cache_sb_k", "cache_sb_v", "cache_fox_k", "cache_fox_v", "cache_fox_logf",
        "cache_dsa_k", "cache_dsa_v", "cache_dsa_idx_k", "norm_mix", "norm_ffn", "norm_final",
        "w_in_ab", "b_forget", "w_out_ab", "w_in_dsa", "w_out_dsa",
        "moe_w_group", "moe_w_router", "moe_w_gate", "moe_w_up", "moe_w_down"]


def _row_shapes(n):
    return [(1, n, H_SB, HEAD), (1, n, H_SB, HEAD), (1, n, H_FOX, HEAD), (1, n, H_FOX, HEAD), (1, n, H_FOX),
            (1, n, KV_DSA, HEAD), (1, n, KV_DSA, HEAD), (1, n, D_IDX)]


def _constants():
    import numpy as np

    p, j = np.arange(P)[:, None], np.arange(P)[None, :]
    consts = np.zeros((P, C_COLS), np.float32)
    consts[:, C_IDENT:C_IDENT + P] = p == j
    consts[:, C_NEG_SB:C_NEG_SB + P] = np.where(j >= p, NEG, 0)
    consts[:, C_NEG_FOX:C_NEG_FOX + P] = np.where(j > p, NEG, 0)
    consts[:, C_NEG_CHUNK:C_NEG_CHUNK + P] = np.where(j // CHUNK > p // CHUNK, NEG, 0)
    consts[:, C_BEFORE:C_BEFORE + P] = p < j
    consts[:, C_SLOT:C_SLOT + P] = j
    tile = np.arange(NT)[None, :]
    consts[:, C_TOKEN:C_TOKEN + NT] = np.minimum(tile * P + p, T - 1)
    consts[:, C_VALID:C_VALID + NT] = tile * P + p < T
    consts[:, C_FIRST:C_FIRST + 4] = 4 - np.arange(4)
    consts[:, C_EXPERT:C_EXPERT + NE] = np.arange(NE)
    select = np.zeros((H_FOX, H_FOX, P), np.float32)
    for h in range(H_FOX):
        select[h, h] = -1.0
    pos = np.where(tile < PT, tile * P + p, PAST + p).astype(np.float32)
    tables = []
    for size in (HEAD, D_IDX):
        half = size // 2
        inv = (10000.0 ** (-np.arange(half, dtype=np.float32) / np.float32(half)).astype(np.float64)).astype(np.float32)
        ang = (pos[:, :, None] * inv[None, None, :]).astype(np.float32).astype(np.float64)
        cos, sin = np.cos(ang).astype(np.float32), np.sin(ang).astype(np.float32)
        tables += [np.concatenate([cos, cos], 2).reshape(P, -1), np.concatenate([-sin, sin], 2).reshape(P, -1)]
    return {"consts": consts, "head_select": select.reshape(H_FOX, -1), "rope": np.concatenate(tables, 1).astype(np.float32)}


def kernel(**inputs):
    import numpy as np
    import concourse.bacc as bacc
    from concourse.bass_utils import run_bass_kernel_spmd

    nc = bacc.Bacc("TRN2", target_bir_lowering=False, num_devices=1)
    arrays = {name: np.ascontiguousarray(inputs[name]) for name in _INS}
    arrays.update(_constants())
    io = {}
    feed = {}
    for name, value in arrays.items():
        feed[f"in_{name}"] = value
        io[name] = nc.dram_tensor(f"in_{name}", value.shape, F32, kind="ExternalInput").ap()
    shapes = [(1, PROMPT, D), (1, SAMPLE, D)] + _row_shapes(PROMPT) + _row_shapes(SAMPLE)
    outs = [nc.dram_tensor(f"out_{i}", shape, F32, kind="ExternalOutput").ap() for i, shape in enumerate(shapes)]
    io["y_prompt"], io["y_sample"] = outs[0:2]
    (io["out_sb_k"], io["out_sb_v"], io["out_fox_k"], io["out_fox_v"], io["out_fox_logf"],
     io["out_dsa_k"], io["out_dsa_v"], io["out_dsa_idx"]) = [(outs[2 + i], outs[10 + i]) for i in range(8)]
    trunk_program(nc, io)
    r = run_bass_kernel_spmd(nc, [feed], core_ids=[0])
    return tuple(r.results[0][f"out_{i}"] for i in range(len(outs)))
```

```python
from contextlib import ExitStack

import concourse.bass as bass
from concourse import mybir

ALU = mybir.AluOpType
ACT = mybir.ActivationFunctionType
AX = mybir.AxisListType
F32 = mybir.dt.float32
F32R = mybir.dt.float32r
BF16 = mybir.dt.bfloat16
U32 = mybir.dt.uint32

P = 128
D = 1024
DC = D // P
PROMPT, SAMPLE, PAST = 512, 32, 256
PT = PROMPT // P
NT = PT + 1
T = PROMPT + SAMPLE
LS = PAST + SAMPLE
HEAD = 128
SCALE = HEAD ** -0.5
H_SB = H_FOX = 4
H_DSA, KV_DSA = 8, 2
H_IDX, D_IDX = 4, 64
IDX_COLS = H_IDX * D_IDX + D_IDX + H_IDX
CHUNK = 64
K_PROMPT = min(256, PROMPT // 4)
K_SAMPLE = min(256, LS // 4)
EPS = 1e-6
NG, EPG = 4, 4
NE = NG * EPG
FE = 256
SLOTS = P
PASSES = -(-T // SLOTS)
HALF_T = T // 2
NEG = -1e30
TAKEN = -3.4028234e38
BARRED = -3.2e38
UNTAKEN_FROM = -3.3e38

C_IDENT = 0
C_NEG_SB = P
C_NEG_FOX = 2 * P
C_NEG_CHUNK = 3 * P
C_BEFORE = 4 * P
C_SLOT = 5 * P
C_TOKEN = 6 * P
C_VALID = C_TOKEN + NT
C_FIRST = C_VALID + NT
C_EXPERT = C_FIRST + 4
C_COLS = C_EXPERT + NE
R_COS, R_SIN = 0, NT * HEAD
R_ICOS, R_ISIN = 2 * NT * HEAD, 2 * NT * HEAD + NT * D_IDX
R_COLS = 2 * NT * (HEAD + D_IDX)


def width(t):
    return P if t < PT else SAMPLE


def cols(t):
    return slice(t * P, t * P + width(t))


class Main:
    pass


class Routing:
    pass


class Attention:
    pass


class Chain:

    def __init__(self, eng, sem):
        self.eng, self.sem, self.n = eng, sem, 0

    def __call__(self, instruction):
        instruction.then_inc(self.sem, 1)
        self.n += 1

    def wait(self):
        self.eng.wait_ge(self.sem, self.n)


def tools(nc, ctx, prefix):
    def sb(name, shape, dtype=F32):
        return ctx.enter_context(nc.sbuf_tensor(f"{prefix}_{name}", shape, dtype))

    def ps(name, shape, dtype=F32):
        return ctx.enter_context(nc.psum_tensor(f"{prefix}_{name}", shape, dtype))

    mine = []

    def sem(name, kept=False):
        handle = nc.alloc_semaphore(f"{prefix}_{name}")
        if not kept:
            mine.append(handle)
        return handle

    def clear():
        numbers = sorted(s.num for s in mine)
        runs = [n for n in numbers if n - 1 not in numbers]
        for lo in runs:
            hi = lo
            while hi in numbers:
                hi += 1
            nc.gpsimd.sem_clear(range(lo, hi))
        for s in mine:
            nc.release_semaphore(s)

    ctx.callback(clear)
    return sb, ps, sem


def norm_stage(nc, m, name, g_dram, hT=None, h_dram=None, y_dram=None):
    with ExitStack() as ctx:
        sb, ps, sem = tools(nc, ctx, name)
        g = sb("g", [P, D])
        h = sb("h", [P, 2, D])
        squares = sb("squares", [P, D])
        stat = sb("stat", [P, 4, 8])
        turned = ps("turned", [P, 2, 2, 512])
        g_loaded, squared, mean_ready, root_ready = sem("g_loaded"), sem("squared"), sem("mean_ready"), sem("root_ready")
        inverse_ready, h_ready, h_turned = sem("inverse_ready"), sem("h_ready"), sem("h_turned")
        hT_low, hT_high = sem("hT_low"), sem("hT_high")
        stored = [sem("stored0"), sem("stored1")]
        block = ctx.enter_context(nc.Block())

        @block.sync
        def _(sp):
            sp.dma_start(g[:, :], g_dram.partition_broadcast(P)).then_inc(g_loaded, 16)
            for t in range(NT):
                w = width(t)
                sp.wait_ge(h_ready, t + 1)
                if h_dram is not None:
                    sp.dma_start(h_dram[t * P:t * P + w, :], h[0:w, t % 2, :]).then_inc(stored[t % 2], 16)
                if y_dram is not None:
                    dst = y_dram[0][t * P:t * P + w, :] if t < PT else y_dram[1][:, :]
                    sp.dma_start(dst, h[0:w, t % 2, :]).then_inc(stored[t % 2], 16)
            if h_dram is not None or y_dram is not None:
                sp.wait_ge(stored[0], 16 * 3)
                sp.wait_ge(stored[1], 16 * 2)

        @block.scalar
        def _(act):
            for t in range(NT):
                if t:
                    act.wait_ge(squared, t)
                act.activation(squares[:, :], m.x[:, t, :], ACT.Square, accum_out=stat[:, 0, t:t + 1]).then_inc(squared, 1)
            act.wait_ge(mean_ready, 1)
            act.activation(stat[:, 2, 0:NT], stat[:, 1, 0:NT], ACT.Sqrt).then_inc(root_ready, 1)
            if hT is not None:
                for t in range(NT):
                    act.wait_ge(h_turned, t + 1)
                    w = width(t)
                    act.activation(hT[:, 0:4, cols(t)],
                                   turned[:, t % 2, 0, :].rearrange("p (c n) -> p c n", c=4)[:, :, 0:w],
                                   ACT.Copy).then_inc(hT_low, 1)

        @block.vector
        def _(dve):
            dve.wait_ge(squared, NT)
            dve.tensor_scalar(stat[:, 1, 0:NT], stat[:, 0, 0:NT], 1.0 / D, EPS, ALU.mult, ALU.add).then_inc(mean_ready, 1)
            dve.wait_ge(root_ready, 1)
            dve.reciprocal(stat[:, 3, 0:NT], stat[:, 2, 0:NT]).then_inc(inverse_ready, 1)
            dve.wait_ge(inverse_ready, 1)
            dve.wait_ge(g_loaded, 16)

            def high_half(t):
                dve.wait_ge(h_turned, t + 1)
                w = width(t)
                dve.tensor_copy(hT[:, 4:8, cols(t)],
                                turned[:, t % 2, 1, :].rearrange("p (c n) -> p c n", c=4)[:, :, 0:w]).then_inc(hT_high, 1)

            for t in range(NT):
                if t >= 2:
                    if hT is not None:
                        dve.wait_ge(h_turned, t - 1)
                    if h_dram is not None or y_dram is not None:
                        dve.wait_ge(stored[t % 2], 16 * (t // 2))
                dve.scalar_tensor_tensor(out=h[:, t % 2, :], in0=m.x[:, t, :], scalar=stat[:, 3, t:t + 1],
                                         in1=g[:, :], op0=ALU.mult, op1=ALU.mult).then_inc(h_ready, 1)
                if hT is not None and t >= 1:
                    high_half(t - 1)
            if hT is not None:
                high_half(NT - 1)

        @block.tensor
        def _(pe):
            if hT is None:
                return
            for t in range(NT):
                w = width(t)
                pe.wait_ge(h_ready, t + 1)
                if t >= 2:
                    pe.wait_ge(hT_low, t - 1)
                    pe.wait_ge(hT_high, t - 1)
                for c in range(DC):
                    last = pe.transpose(turned[:, t % 2, c // 4, (c % 4) * P:(c % 4) * P + w],
                                        h[0:w, t % 2, c * P:(c + 1) * P], m.ident[0:w, 0:w])
                last.then_inc(h_turned, 1)


class Norm:

    def __init__(self, m, sem, g_dram, g, h, squares, stat, turned, high, low):
        self.m, self.g_dram, self.g, self.h, self.squares, self.stat = m, g_dram, g, h, squares, stat
        self.turned, self.high, self.low = turned, high, low
        self.g_loaded, self.squared, self.mean_ready, self.root_ready = sem("g_loaded"), sem("squared"), sem("mean_ready"), sem("root_ready")
        self.newton, self.h_ready, self.h_turned = sem("newton"), sem("h_ready"), sem("h_turned")
        self.high_ready, self.low_ready = sem("h_high_ready"), sem("h_low_ready")

    def load(self, sp):
        sp.dma_start(self.g, self.g_dram.partition_broadcast(P)).then_inc(self.g_loaded, 16)

    def square(self, act, t):
        if t:
            act.wait_ge(self.squared, t)
        act.activation(self.squares, self.m.x[:, t, :], ACT.Square, accum_out=self.stat[:, 0, t:t + 1]).then_inc(self.squared, 1)

    def root(self, act):
        act.wait_ge(self.mean_ready, 1)
        act.activation(self.stat[:, 2, 0:NT], self.stat[:, 1, 0:NT], ACT.Sqrt).then_inc(self.root_ready, 1)

    def inverse_root(self, dve):
        total, v, root, y, tmp, scale = (self.stat[:, k, 0:NT] for k in range(6))
        dve.wait_ge(self.squared, NT)
        dve.tensor_scalar(v, total, 1.0 / D, EPS, ALU.mult, ALU.add).then_inc(self.mean_ready, 1)
        dve.wait_ge(self.root_ready, 1)
        dve.reciprocal(y, root).then_inc(self.newton, 1)
        dve.wait_ge(self.newton, 1)
        dve.tensor_tensor(tmp, y, y, ALU.mult).then_inc(self.newton, 1)
        dve.wait_ge(self.newton, 2)
        dve.tensor_tensor(tmp, tmp, v, ALU.mult).then_inc(self.newton, 1)
        dve.wait_ge(self.newton, 3)
        dve.tensor_scalar(tmp, tmp, -0.5, 1.5, ALU.mult, ALU.add).then_inc(self.newton, 1)
        dve.wait_ge(self.newton, 4)
        dve.tensor_tensor(scale, y, tmp, ALU.mult).then_inc(self.newton, 1)
        dve.wait_ge(self.newton, 5)
        dve.wait_ge(self.g_loaded, 16)

    def scale(self, dve, t):
        if t >= 2:
            dve.wait_ge(self.h_turned, t - 1)
        dve.scalar_tensor_tensor(out=self.h[:, t % 2, :], in0=self.m.x[:, t, :], scalar=self.stat[:, 5, t:t + 1],
                                 in1=self.g, op0=ALU.mult, op1=ALU.mult).then_inc(self.h_ready, 1)

    def turn(self, pe, t):
        w = width(t)
        pe.wait_ge(self.h_ready, t + 1)
        if t >= 2:
            pe.wait_ge(self.low_ready, t - 1)
        for c in range(DC):
            last = pe.transpose(self.turned[:, 2 * (t % 2) + c // 4, (c % 4) * P:(c % 4) * P + w],
                                self.h[0:w, t % 2, c * P:(c + 1) * P], self.m.ident[0:w, 0:w])
        last.then_inc(self.h_turned, 1)

    def parts(self, t, half):
        w = width(t)
        source = self.turned[:, 2 * (t % 2) + half, :].rearrange("p (c n) -> p c n", c=4)[:, :, 0:w]
        high, low = (x[:, 0:DC * T].rearrange("p (c n) -> p c n", c=DC)[:, 4 * half:4 * half + 4, cols(t)] for x in (self.high, self.low))
        return source, high, low

    def store_high(self, act, t):
        act.wait_ge(self.h_turned, t + 1)
        for half in range(2):
            source, high, _ = self.parts(t, half)
            act.activation(high, source, ACT.Copy).then_inc(self.high_ready, 1)

    def store_low(self, dve, t):
        for half in range(2):
            source, high, low = self.parts(t, half)
            dve.wait_ge(self.high_ready, 2 * t + half + 1)
            last = dve.tensor_tensor(low, source, high.bitcast(F32), ALU.subtract)
        last.then_inc(self.low_ready, 1)

    def clear_pad(self, dve):
        dve.memset(self.high[:, DC * T:].bitcast(F32), 0.0)
        dve.memset(self.low[:, DC * T:].bitcast(F32), 0.0)

    def product(self, pe, out, t, w_high, w_low):
        for c in range(DC):
            for high, weights in ((self.high, w_high), (self.high, w_low), (self.low, w_high)):
                last = pe.matmul(out, high[:, c * T + t * P:c * T + (t + 1) * P], weights[:, c, :],
                                 start=(c == 0 and weights is w_high and high is self.high), stop=(c == DC - 1 and high is self.low))
        return last


def rows_of(dram, t, heads=True):
    pattern = "b t h d -> (b t) (h d)" if heads else "b t d -> (b t) d"
    if t < PT:
        return dram[0].rearrange(pattern)[t * P:(t + 1) * P, :]
    return dram[1].rearrange(pattern)


def project_ab_stage(nc, m, a, high, low, io):
    with ExitStack() as ctx:
        sb, ps, sem = tools(nc, ctx, "ab")
        COLS = 2 * HEAD
        UNITS = [(part * 512 + kind * 1536 + pair * COLS, what, kind, pair) for what, part in (("k", 1), ("v", 2), ("q", 0))
                 for kind in range(2) for pair in range(2)]
        KG, VG, QG = 4 * NT, 4 * NT, 16
        w_raw = sb("w_raw", [P, 2, DC, COLS])
        w_high = sb("w_high", [P, 2, DC, COLS], F32R)
        w_low = sb("w_low", [P, 2, DC, COLS], F32R)
        w_forget = sb("w_forget", [P, DC, H_FOX])
        w_forget_high = sb("w_forget_high", [P, DC, H_FOX], F32R)
        w_forget_low = sb("w_forget_low", [P, DC, H_FOX], F32R)
        b_rows = sb("b_rows", [P, H_FOX])
        k_rows = sb("k_rows", [P, 4, COLS])
        cache_k = sb("cache_k", [P, 2, 2, 512])
        cache_f = sb("cache_f", [P, 2, H_FOX])
        u = sb("u", [P, NT, H_FOX])
        soft = sb("soft", [P, NT, H_FOX])
        logf = sb("logf", [P, NT, H_FOX])
        stat = sb("stat", [P, 6, NT])
        acc = ps("acc", [P, 4, 512])
        acc_k = ps("acc_k", [P, 2, 512])
        turned = ps("turned", [P, 2, 512])
        norm = Norm(m, sem, io["norm_mix"][0], a.v_rows[:, 3, :], a.v_rows[:, 0:2, :], a.v_rows[:, 2, :], stat, acc, high, low)
        x_cleared, x_loaded, consts_loaded = sem("x_cleared"), [sem(f"x_loaded{t}") for t in range(NT)], sem("consts_loaded")
        w_loaded = [sem("w_loaded0"), sem("w_loaded1")]
        w_high_ready, w_low_ready = sem("w_high_ready"), sem("w_low_ready")
        small_loaded, cache_k_loaded = sem("small_loaded", kept=True), sem("cache_k_loaded", kept=True)
        small_high, small_low, rest_set = sem("small_high"), sem("small_low"), sem("rest_set")
        group_ready, group_stored = sem("group_ready"), sem("group_stored")
        k_ready, k_rows_ready, k_turned, kT_stored = sem("k_ready"), sem("k_rows_ready"), sem("k_turned"), sem("kT_stored")
        k_saved = [sem(f"k_saved{b}", kept=True) for b in range(4)]
        v_saved, cache_v_loaded, act_chain = sem("v_saved"), sem("cache_v_loaded", kept=True), sem("act_chain")
        f_ready, u_ready, soft_ready, logf_ready, f_turned, f_used, f_saved = (
            sem("f_ready"), sem("u_ready"), sem("soft_ready"), sem("logf_ready"), sem("f_turned"), sem("f_used"), sem("f_saved"))
        block = ctx.enter_context(nc.Block())
        out_k, out_v = [io["out_sb_k"], io["out_fox_k"]], [io["out_sb_v"], io["out_fox_v"]]
        w_view = io["w_in_ab"].rearrange("(c p) n -> p c n", p=P)

        def unit_done(eng, i):
            if i < 4:
                eng.wait_ge(k_ready, (i + 1) * NT)
            else:
                eng.wait_ge(group_ready, (i - 3) * NT if i < 8 else VG + (i - 7) * 4)

        @block.sync
        def _(sp):
            x_view = io["x_prompt"].rearrange("b (t p) d -> p (b t) d", p=P)
            for t in range(PT):
                sp.dma_start(m.x[:, t, :], x_view[:, t, :]).then_inc(x_loaded[t], 16)
            sp.wait_ge(x_cleared, 1)
            sp.dma_start(m.x[0:SAMPLE, PT, :], io["x_sample"].rearrange("b t d -> (b t) d")).then_inc(x_loaded[PT], 16)
            norm.load(sp)
            for i, (lo, what, kind, pair) in enumerate(UNITS):
                if i >= 2:
                    sp.wait_ge(w_low_ready, i - 1)
                sp.dma_start(w_raw[:, i % 2], w_view[:, :, lo:lo + COLS]).then_inc(w_loaded[i % 2], 16)
                if i == 4:
                    sp.wait_ge(logf_ready, 1)
                    sp.dma_start(io["out_fox_logf"][0].rearrange("b (t p) h -> p (b t) h", p=P), logf[:, 0:PT, :]).then_inc(f_saved, 16)
                    sp.dma_start(io["out_fox_logf"][1].rearrange("b t h -> (b t) h"), logf[0:SAMPLE, PT, :]).then_inc(f_saved, 16)
            for kind in range(2):
                for t in range(NT):
                    sp.wait_ge(group_stored, (2 * kind + 1) * NT + t + 1)
                    sp.dma_start(rows_of(out_v[kind], t), a.v_rows[0:width(t), t, kind * 512:(kind + 1) * 512]).then_inc(v_saved, 16)
            for b in range(4):
                sp.wait_ge(k_saved[b], 16 * KG // 4)
            sp.wait_ge(v_saved, 16 * 2 * NT)
            sp.wait_ge(f_saved, 32)
            sp.wait_ge(cache_v_loaded, 32)

        @block.gpsimd
        def _(pool):
            pool.dma_start(w_forget[:, :, :], w_view[:, :, 6 * 512:6 * 512 + H_FOX]).then_inc(small_loaded, 16)
            pool.dma_start(b_rows[:, :], io["b_forget"].partition_broadcast(P)).then_inc(small_loaded, 16)
            pool.dma_start(cache_f[:, :, :], io["cache_fox_logf"].rearrange("b (j p) h -> p (b j) h", p=P)).then_inc(small_loaded, 16)
            pool.wait_ge(norm.h_turned, 1)
            for kind, cache in enumerate((io["cache_sb_k"], io["cache_fox_k"])):
                pool.dma_start(cache_k[:, kind, :, :], cache.rearrange("b (j p) h d -> p (b j) (h d)", p=P)).then_inc(cache_k_loaded, 16)
            for kind, cache in enumerate((io["cache_sb_v"], io["cache_fox_v"])):
                pool.dma_start(a.cache_v[:, :, kind * 512:(kind + 1) * 512], cache.rearrange("b (j p) h d -> p (b j) (h d)", p=P)).then_inc(cache_v_loaded, 16)
            for g in range(KG):
                i, t = divmod(g, NT)
                _, _, kind, pair = UNITS[i]
                pool.wait_ge(k_rows_ready, g + 1)
                pool.dma_start(rows_of(out_k[kind], t)[:, pair * COLS:(pair + 1) * COLS], k_rows[0:width(t), g % 4, :]).then_inc(k_saved[g % 4], 16)

        @block.tensor
        def _(pe):
            def k_group(g):
                i, t = divmod(g, NT)
                if t == 0:
                    pe.wait_ge(w_low_ready, i + 1)
                if g < NT:
                    pe.wait_ge(norm.low_ready, t + 1)
                if g == NT - 1:
                    pe.wait_ge(rest_set, 1)
                if g >= 2:
                    pe.wait_ge(k_rows_ready, g - 1)
                norm.product(pe, acc_k[:, g % 2, 0:COLS], t, w_high[:, i % 2], w_low[:, i % 2]).then_inc(k_ready, 1)

            def turn_k(g):
                w = width(g % NT)
                pe.wait_ge(k_rows_ready, g + 1)
                if g >= 2:
                    pe.wait_ge(kT_stored, g - 1)
                for h in range(2):
                    last = pe.transpose(turned[:, g % 2, h * P:h * P + w], k_rows[0:w, g % 4, h * P:(h + 1) * P], m.ident[0:w, 0:w])
                last.then_inc(k_turned, 1)

            pe.wait_ge(consts_loaded, 32)
            norm.turn(pe, 0)
            for t in range(1, NT):
                norm.turn(pe, t)
                k_group(t - 1)
                if t >= 3:
                    turn_k(t - 3)
            for g in range(NT - 1, KG):
                k_group(g)
                turn_k(g - 2)
                if g == NT - 1:
                    pe.wait_ge(small_low, 1)
                    for t in range(NT):
                        last = norm.product(pe, acc[:, 0, t * H_FOX:(t + 1) * H_FOX], t, w_forget_high, w_forget_low)
                    last.then_inc(f_ready, 1)
            turn_k(KG - 2)
            turn_k(KG - 1)
            pe.wait_ge(cache_k_loaded, 32)
            for j in range(4):
                kind, kb = divmod(j, 2)
                pe.wait_ge(kT_stored, KG + j - 1)
                for h in range(4):
                    last = pe.transpose(turned[:, j % 2, h * P:(h + 1) * P], cache_k[:, kind, kb, h * P:(h + 1) * P], m.ident[:, :])
                last.then_inc(k_turned, 1)
            pe.wait_ge(kT_stored, KG + 4)
            pe.wait_ge(logf_ready, 1)
            for t in range(PT):
                pe.transpose(turned[0:H_FOX, 0, t * P:(t + 1) * P], logf[:, t, :], m.ident[:, :])
            for kb in range(2):
                pe.transpose(turned[0:H_FOX, 1, kb * P:(kb + 1) * P], cache_f[:, kb, :], m.ident[:, :])
            pe.transpose(turned[0:H_FOX, 1, PAST:LS], logf[0:SAMPLE, PT, :], m.ident[0:SAMPLE, 0:SAMPLE]).then_inc(f_turned, 1)
            for g in range(VG):
                i, t = divmod(g, NT)
                if t == 0:
                    pe.wait_ge(w_low_ready, 4 + i + 1)
                if g == 0:
                    pe.wait_ge(u_ready, 1)
                if g >= 4:
                    pe.wait_ge(group_stored, g - 3)
                norm.product(pe, acc[:, g % 4, 0:COLS], t, w_high[:, i % 2], w_low[:, i % 2]).then_inc(group_ready, 1)
            for j in range(QG):
                i, h, n = 8 + j // 4, (j // 2) % 2, j % 2
                g = VG + j
                if j % 4 == 0:
                    pe.wait_ge(w_low_ready, i + 1)
                pe.wait_ge(group_stored, g - 3)
                for c in range(DC):
                    for k, (w, x) in enumerate(((w_high, high), (w_low, high), (w_high, low))):
                        last = pe.matmul(acc[:, g % 4, 0:HALF_T], w[:, i % 2, c, h * P:(h + 1) * P],
                                         x[:, c * T + n * HALF_T:c * T + (n + 1) * HALF_T], start=(c == 0 and k == 0), stop=(c == DC - 1 and k == 2))
                last.then_inc(group_ready, 1)

        @block.scalar
        def _(act):
            act.dma_start(m.consts[:, :], io["consts"]).then_inc(consts_loaded, 16)
            act.dma_start(m.head_select[:, :], io["head_select"]).then_inc(consts_loaded, 16)
            for t in range(NT):
                act.wait_ge(x_loaded[t], 16)
                norm.square(act, t)
            norm.root(act)

            def cut_high(i):
                act.wait_ge(w_loaded[i % 2], 16 * (i // 2 + 1))
                if i >= 2:
                    unit_done(act, i - 2)
                act.activation(w_high[:, i % 2], w_raw[:, i % 2], ACT.Copy).then_inc(w_high_ready, 1)

            cut_high(0)
            for t in range(NT):
                norm.store_high(act, t)
            cut_high(1)
            act.wait_ge(small_loaded, 48)
            act.activation(w_forget_high[:, :, :], w_forget[:, :, :], ACT.Copy).then_inc(small_high, 1)
            cut_high(2)
            act.wait_ge(u_ready, 1)
            act.activation(soft[:, :, :], u[:, :, :], ACT.Abs).then_inc(act_chain, 1)
            act.wait_ge(act_chain, 1)
            act.activation(soft[:, :, :], soft[:, :, :], ACT.Exp, scale=-1.0).then_inc(act_chain, 1)
            act.wait_ge(act_chain, 2)
            act.activation(soft[:, :, :], soft[:, :, :], ACT.Ln, bias=1.0).then_inc(soft_ready, 1)
            cut_high(3)
            cut_high(4)
            for g in range(VG):
                i, t = divmod(g, NT)
                w = width(t)
                if t == 0:
                    cut_high(5 + i)
                lo = UNITS[4 + i][2] * 512 + UNITS[4 + i][3] * COLS
                act.wait_ge(group_ready, g + 1)
                act.activation(a.v_rows[0:w, t, lo:lo + COLS], acc[0:w, g % 4, 0:COLS], ACT.Copy).then_inc(group_stored, 1)
            for j in range(QG):
                g, n = VG + j, j % 2
                _, _, kind, pair = UNITS[8 + j // 4]
                if j % 4 == 0 and j < 12:
                    cut_high(9 + j // 4)
                head = kind * 4 + pair * 2 + (j // 2) % 2
                act.wait_ge(group_ready, g + 1)
                act.activation(a.qT[:, head, n * HALF_T:(n + 1) * HALF_T], acc[:, g % 4, 0:HALF_T], ACT.Copy, scale=SCALE).then_inc(group_stored, 1)

        @block.vector
        def _(dve):
            dve.memset(m.x[:, PT, :], 0.0).then_inc(x_cleared, 1)
            dve.memset(m.ones[:, :], 1.0)
            dve.memset(m.ones16[:, :], 1.0)
            norm.clear_pad(dve)
            dve.wait_ge(consts_loaded, 32)
            dve.tensor_copy(m.masks[:, :], m.consts[:, 0:4 * P])
            dve.tensor_copy(m.before[:, :], m.consts[:, C_BEFORE:C_BEFORE + P]).then_inc(rest_set, 1)

            def cut_low(i):
                dve.wait_ge(w_high_ready, i + 1)
                dve.tensor_tensor(w_low[:, i % 2], w_raw[:, i % 2], w_high[:, i % 2].bitcast(F32), ALU.subtract).then_inc(w_low_ready, 1)

            def store_k(g):
                w = width(g % NT)
                dve.wait_ge(k_ready, g + 1)
                if g >= 4:
                    dve.wait_ge(k_turned, g - 3)
                    dve.wait_ge(k_saved[g % 4], 16 * (g // 4))
                dve.tensor_copy(k_rows[0:w, g % 4, :], acc_k[0:w, g % 2, 0:COLS]).then_inc(k_rows_ready, 1)

            def store_kT(g):
                i, t = divmod(g, NT)
                _, _, kind, pair = UNITS[i]
                heads = slice(kind * 4 + pair * 2, kind * 4 + pair * 2 + 2)
                dve.wait_ge(k_turned, g + 1)
                dst = a.kT[:, heads, t * P:(t + 1) * P] if t < PT else a.kT_sample[:, heads, PAST:LS]
                dve.tensor_copy(dst, turned[:, g % 2, 0:COLS].rearrange("p (h n) -> p h n", h=2)[:, :, 0:width(t)]).then_inc(kT_stored, 1)

            norm.inverse_root(dve)
            norm.scale(dve, 0)
            cut_low(0)
            for t in range(1, NT):
                norm.scale(dve, t)
                norm.store_low(dve, t - 1)
                if t >= 2:
                    store_k(t - 2)
            norm.store_low(dve, NT - 1)
            cut_low(1)
            dve.wait_ge(small_high, 1)
            dve.tensor_tensor(w_forget_low[:, :, :], w_forget[:, :, :], w_forget_high[:, :, :].bitcast(F32), ALU.subtract).then_inc(small_low, 1)
            for g in range(NT - 2, KG):
                store_k(g)
                store_kT(g - 3)
                if g == NT:
                    dve.wait_ge(f_ready, 1)
                    dve.tensor_tensor(u[:, :, :], acc[:, 0, 0:NT * H_FOX].rearrange("p (t h) -> p t h", t=NT),
                                      b_rows[:, :].unsqueeze(1).broadcast_to([P, NT, H_FOX]), ALU.add).then_inc(u_ready, 1)
                if g == NT + 1:
                    dve.wait_ge(soft_ready, 1)
                    dve.scalar_tensor_tensor(out=logf[:, :, :], in0=u[:, :, :], scalar=0.0, in1=soft[:, :, :], op0=ALU.min, op1=ALU.subtract).then_inc(logf_ready, 1)
                if g % NT == 0:
                    cut_low(g // NT + 1)
            for g in range(KG - 3, KG):
                store_kT(g)
            for j in range(4):
                kind, kb = divmod(j, 2)
                dve.wait_ge(k_turned, KG + j + 1)
                dve.tensor_copy(a.kT_sample[:, kind * 4:kind * 4 + 4, kb * P:(kb + 1) * P],
                                turned[:, j % 2, :].rearrange("p (h n) -> p h n", h=4)).then_inc(kT_stored, 1)
            dve.wait_ge(f_turned, 1)
            dve.tensor_tensor_scan(a.forget[:, :], m.ones[0:4, :], turned[0:4, 0, :], 0.0, ALU.mult, ALU.add)
            dve.tensor_tensor_scan(a.forget_sample[:, :], m.ones[0:4, 0:LS], turned[0:4, 1, 0:LS], 0.0, ALU.mult, ALU.add)
            for i in range(5, 12):
                cut_low(i)


class Unit:

    def __init__(self, heads, t, stick=False):
        self.heads, self.t, self.sample, self.stick = heads, t, t == PT, stick
        self.n = LS if self.sample else (t + 1) * P
        self.blocks = 3 if self.sample else t + 1

    def rows_in(self, kb):
        return SAMPLE if self.sample and kb == 2 else P


def score_products(pe, m, a, unit, out, kv, mask, forget):
    for i, h in enumerate(unit.heads):
        q = a.qT[:, h, cols(unit.t)]
        k = a.kT_sample[:, kv(h), :] if unit.sample else a.kT[:, kv(h), :]
        rows = slice(32 * i, 32 * i + 32) if unit.sample else slice(0, P)
        nq = SAMPLE if unit.sample else P
        edge = PAST if unit.sample else unit.t * P
        spans = [(0, unit.n)] if mask is None else ([(0, edge)] if edge else []) + [(edge, unit.n)]
        for lo, hi in spans:
            masked = mask is None or lo == edge
            products = [(q, k[:, lo:hi])]
            if forget:
                f = a.forget_sample if unit.sample else a.forget
                products.append((m.head_select[:, (h - H_SB) * P:(h - H_SB) * P + nq], f[:, lo:hi]))
            if mask is not None and masked:
                products.append((m.ident16[0:nq, 0:nq], mask[0:nq, 0:hi - lo]))
            if mask is None:
                chosen = a.unchosen[unit.t]
                products.append((m.ident16[0:nq, 0:nq], chosen[0:nq, lo:hi]))
            for j, (left, right) in enumerate(products):
                last = pe.matmul(out[rows, lo:hi], left, right, start=(j == 0), stop=(j == len(products) - 1))
    return last


def value_products(pe, a, unit, out, pT, v_head):
    for i, h in enumerate(unit.heads):
        q = slice(32 * i, 32 * i + 32) if unit.sample else slice(0, P)
        vc = slice(v_head(h) * P, (v_head(h) + 1) * P)
        for kb in range(unit.blocks):
            n = unit.rows_in(kb)
            if unit.sample:
                v = a.cache_v[:, kb, vc] if kb < 2 else a.v_rows[0:SAMPLE, PT, vc]
            else:
                v = a.v_rows[:, kb, vc]
            last = pe.matmul(out[:, q], v, pT[0:n, kb, q], start=(kb == 0), stop=(kb == unit.blocks - 1))
    return last


def mixer_stage(nc, m, a, r, name, steps, kv, v_head, masks, forget, w_dram, g_dram, split):
    with ExitStack() as ctx:
        sb, ps, sem = tools(nc, ctx, name)
        order = [units[0].t for units, last in steps if last]
        last_step = [i for i, (_, last) in enumerate(steps) if last]
        units = [u for us, _ in steps for u in us]
        first_unit = [sum(len(us) for us, _ in steps[:i]) for i in range(len(steps))]
        kind_no = [sum(v.stick == u.stick for v in units[:i]) for i, u in enumerate(units)]
        sticks = any(u.stick for u in units)
        softs = sum(not u.stick for u in units)
        soft_banks = 1 if sticks else 3
        PART = F32R if split else F32
        prob = sb("prob", [P, 4, 512])
        work = sb("work", [P, 2, 512]) if sticks else None
        pT = sb("pT", [P, 3, 4, P])
        row_stat = sb("row_stat", [P, 3, softs])
        oT = sb("oT", [P, 2, DC, P], PART)
        oT_rest = sb("oT_rest", [P, 2, DC, P], PART) if split else None
        g = sb("g", [P, D])
        h = sb("h", [P, 2, D])
        squares = sb("squares", [P, D])
        hT = sb("hT", [P, DC, P])
        stat = sb("stat", [P, 8, NT])
        w_route = sb("w_route", [P, DC, NG + NE])
        scores_soft = ps("scores_soft", [P, soft_banks, 512])
        scores_stick = ps("scores_stick", [P, 2, 512]) if sticks else None
        turned = ps("turned", [P, 2, 512])
        mixed = ps("mixed", [P, 2, 512])
        acc = ps("acc", [P, 512])
        scores_ready = {True: sem("stick_scores"), False: sem("soft_scores")}
        scores_used = {True: sem("stick_scores_used"), False: sem("soft_scores_used")}
        prob_ready = {True: sem("stick_prob"), False: sem("soft_prob")}
        soft_ready, sum_ready, suffix_ready = sem("soft_ready"), sem("sum_ready"), sem("suffix_ready")
        exponent_ready, act_chain = sem("exponent_ready"), sem("act_chain")
        neg_max_ready, exp_ready, inverse_ready = sem("neg_max_ready"), sem("exp_ready"), sem("inverse_ready")
        turned_ready, turned_stored, mixed_ready, mixed_stored = (
            sem("turned_ready"), sem("turned_stored"), sem("mixed_ready"), sem("mixed_stored"))
        rest_stored, cleared = sem("rest_stored"), sem("cleared")
        w_loaded, small_loaded = [sem("w_loaded0"), sem("w_loaded1")], sem("small_loaded")
        w_rounded, w_split = sem("w_rounded"), sem("w_split")
        group_ready, added, squared, mean_ready, root_ready, newton = (
            sem("group_ready"), sem("added"), sem("squared"), sem("mean_ready"), sem("root_ready"), sem("newton"))
        h_ready, logits_ready, logits_stored = sem("h_ready"), sem("logits_ready"), sem("logits_stored")
        h_saved = [sem("h_saved0"), sem("h_saved1")]
        if split:
            w_raw = sb("w_raw", [P, 2, DC, 256])
            w_high = sb("w_high", [P, 4, DC, 256], F32R)
            w_low = sb("w_low", [P, 4, DC, 256], F32R)
        else:
            w_out = sb("w_out", [P, DC, D])

        turns = {}
        for s in range(last_step[-1] + 9):
            if 1 <= s <= len(steps):
                for i in range(first_unit[s - 1], first_unit[s - 1] + len(steps[s - 1][0])):
                    turns["unit", i] = len(turns)
            for o, end in enumerate(last_step):
                if s == end + 8:
                    turns["norm", o, 0] = len(turns)
                    turns["norm", o, 1] = len(turns)
        END = last_step[-1] + 9
        block = ctx.enter_context(nc.Block())

        def units_of(s):
            return [(first_unit[s] + j, u) for j, u in enumerate(steps[s][0])] if 0 <= s < len(steps) else []

        def scores_of(i):
            u = units[i]
            return scores_stick[:, kind_no[i] % 2] if u.stick else scores_soft[:, kind_no[i] % soft_banks]

        def tiles_at(s, lag):
            return [(o, order[o]) for o, end in enumerate(last_step) if s == end + lag]

        @block.sync
        def _(sp):
            sp.dma_start(w_route[:, :, 0:NG], r.w_group.rearrange("(c p) g -> p c g", p=P)).then_inc(small_loaded, 16)
            sp.dma_start(w_route[:, :, NG:], r.w_router.rearrange("(c p) g e -> p c (g e)", p=P)).then_inc(small_loaded, 16)
            sp.dma_start(g[:, :], g_dram.partition_broadcast(P)).then_inc(small_loaded, 16)
            w_view = w_dram.rearrange("(c p) n -> p c n", p=P)
            if split:
                for q in range(4):
                    if q >= 2:
                        sp.wait_ge(w_split, q - 1)
                    sp.dma_start(w_raw[:, q % 2], w_view[:, :, q * 256:(q + 1) * 256]).then_inc(w_loaded[q % 2], 16)
            else:
                for n in range(2):
                    sp.dma_start(w_out[:, :, n * 512:(n + 1) * 512], w_view[:, :, n * 512:(n + 1) * 512]).then_inc(w_loaded[n], 16)
            for o, t in enumerate(order):
                w = width(t)
                sp.wait_ge(h_ready, o + 1)
                sp.dma_start(r.h_dram[t * P:t * P + w, :], h[0:w, o % 2, :]).then_inc(h_saved[o % 2], 16)
            sp.wait_ge(h_saved[0], 48)
            sp.wait_ge(h_saved[1], 32)

        @block.tensor
        def _(pe):
            def turn(i):
                pos, u = turns["unit", i], units[i]
                pe.wait_ge(prob_ready[u.stick], kind_no[i] + 1)
                if pos >= 2:
                    pe.wait_ge(turned_stored, pos - 1)
                for kb in range(u.blocks):
                    n = u.rows_in(kb)
                    last = pe.transpose(turned[0:n, pos % 2, kb * P:(kb + 1) * P], prob[:, i % 4, kb * P:kb * P + n], m.ident[:, :])
                last.then_inc(turned_ready, 1)

            def mix(i):
                pe.wait_ge(turned_stored, turns["unit", i] + 1)
                if i >= 2:
                    pe.wait_ge(mixed_stored, i - 1)
                    if split:
                        pe.wait_ge(rest_stored, i - 1)
                value_products(pe, a, units[i], mixed[:, i % 2, 0:P], pT[:, i % 3], v_head).then_inc(mixed_ready, 1)

            def output_part(o, q):
                n, first = divmod(q, 2)
                w = P if split else width(order[o])
                if q == 0:
                    done = first_unit[last_step[o]] + len(steps[last_step[o]][0])
                    pe.wait_ge(mixed_stored, done)
                    if split:
                        pe.wait_ge(rest_stored, done)
                        if o == 0:
                            pe.wait_ge(w_split, 4)
                if o == 0 and not split and first == 0:
                    pe.wait_ge(w_loaded[n], 16)
                if first == 0 and 2 * o + n:
                    pe.wait_ge(added, 2 * o + n)
                if first == 0 and routed[0]:
                    pe.wait_ge(logits_stored, routed[0])
                for c in range(4 * first, 4 * first + 4):
                    if not split:
                        last = pe.matmul(acc[0:w, :], oT[:, o % 2, c, 0:w], w_out[:, c, n * 512:(n + 1) * 512], start=(c == 0), stop=(c == DC - 1))
                        continue
                    for half in range(2):
                        out, k = acc[:, half * 256:(half + 1) * 256], 2 * n + half
                        for j, (left, right) in enumerate(((oT, w_high), (oT, w_low), (oT_rest, w_high))):
                            last = pe.matmul(out, left[:, o % 2, c, :], right[:, k, c, :], start=(c == 0 and j == 0 and half == 0),
                                             stop=(c == DC - 1 and j == 2), skip_group_check=True)
                if first:
                    last.then_inc(group_ready, 1)

            def turn_norm(o, t):
                w = width(t)
                pe.wait_ge(h_ready, o + 1)
                for half in range(2):
                    pos = turns["norm", o, half]
                    pe.wait_ge(turned_stored, pos - 1)
                    for c in range(4):
                        last = pe.transpose(turned[:, pos % 2, c * P:c * P + w], h[0:w, o % 2, (4 * half + c) * P:(4 * half + c + 1) * P], m.ident[0:w, 0:w])
                    last.then_inc(turned_ready, 1)

            def route(o, t):
                w = width(t)
                if o == 0:
                    pe.wait_ge(small_loaded, 48)
                pe.wait_ge(added, min(2 * o + 3, 2 * NT))
                pe.wait_ge(turned_stored, turns["norm", o, 1] + 1)
                for c in range(DC):
                    last = pe.matmul(acc[0:w, 0:NG + NE], hT[:, c, 0:w], w_route[:, c, :], start=(c == 0), stop=(c == DC - 1))
                last.then_inc(logits_ready, 1)
                routed[0] = o + 1

            routed = [0]
            for s in range(END):
                for i, u in units_of(s):
                    k, banks = kind_no[i], 2 if u.stick else soft_banks
                    if k >= banks:
                        pe.wait_ge(scores_used[u.stick], k - banks + 1)
                    score_products(pe, m, a, u, scores_of(i), kv, masks[u.stick], forget and not u.stick).then_inc(scores_ready[u.stick], 1)
                for q in range(4):
                    for o, _ in tiles_at(s, 3 + q):
                        output_part(o, q)
                for i, _ in units_of(s - 1):
                    turn(i)
                for i, _ in units_of(s - 2):
                    mix(i)
                for o, t in tiles_at(s, 8):
                    turn_norm(o, t)
                    route(o, t)

        @block.scalar
        def _(act):
            chained = 0
            for s in range(END + 1):
                for i, u in units_of(s):
                    if not u.stick:
                        continue
                    k, buf = kind_no[i], prob[:, i % 4, 0:u.n]
                    act.wait_ge(scores_ready[True], k + 1)
                    if i >= 4:
                        act.wait_ge(turned_ready, turns["unit", i - 4] + 1)
                    act.activation(buf, scores_of(i)[:, 0:u.n], ACT.Abs).then_inc(act_chain, 1)
                    act.wait_ge(act_chain, chained + 1)
                    act.activation(buf, buf, ACT.Exp, scale=-1.0).then_inc(act_chain, 1)
                    act.wait_ge(act_chain, chained + 2)
                    act.activation(buf, buf, ACT.Ln, bias=1.0).then_inc(soft_ready, 1)
                    chained += 2
                for i, u in units_of(s):
                    if u.stick:
                        continue
                    k = kind_no[i]
                    act.wait_ge(neg_max_ready, k + 1)
                    if i >= 4:
                        act.wait_ge(turned_ready, turns["unit", i - 4] + 1)
                    act.activation(prob[:, i % 4, 0:u.n], scores_of(i)[:, 0:u.n], ACT.Exp, bias=row_stat[:, 0, k:k + 1],
                                   accum_out=row_stat[:, 1, k:k + 1]).then_inc(exp_ready, 1)
                for i, u in units_of(s):
                    if u.stick:
                        k = kind_no[i]
                        act.wait_ge(exponent_ready, k + 1)
                        act.activation(prob[:, i % 4, 0:u.n], work[:, k % 2, 0:u.n], ACT.Exp).then_inc(prob_ready[True], 1)
                if split and s < 4:
                    act.wait_ge(w_loaded[s % 2], 16 * (s // 2 + 1))
                    act.activation(w_high[:, s], w_raw[:, s % 2], ACT.Copy).then_inc(w_rounded, 1)
                for i, u in units_of(s - 2):
                    o = sum(end < s - 2 for end in last_step)
                    h0, h1 = u.heads[0], u.heads[-1] + 1
                    act.wait_ge(mixed_ready, i + 1)
                    if i == 0:
                        act.wait_ge(cleared, 1)
                    if o >= 2:
                        act.wait_ge(group_ready, 2 * (o - 1))
                    act.activation(oT[:, o % 2, h0:h1, 0:width(u.t)], mixed[:, i % 2, 0:P].rearrange("p (h n) -> p h n", h=h1 - h0), ACT.Copy).then_inc(mixed_stored, 1)
                for o, t in tiles_at(s, 7):
                    act.wait_ge(added, 2 * o + 2)
                    if o:
                        act.wait_ge(squared, o)
                    act.activation(squares[:, :], m.x[:, t, :], ACT.Square, accum_out=stat[:, 0, o:o + 1]).then_inc(squared, 1)
                    act.wait_ge(mean_ready, o + 1)
                    act.activation(stat[:, 2, o:o + 1], stat[:, 1, o:o + 1], ACT.Ln).then_inc(act_chain, 1)
                    chained += 1
                    act.wait_ge(act_chain, chained)
                    act.activation(stat[:, 3, o:o + 1], stat[:, 2, o:o + 1], ACT.Exp, scale=-0.5).then_inc(root_ready, 1)
                for o, t in tiles_at(s, 8):
                    w = width(t)
                    act.wait_ge(logits_ready, o + 1)
                    act.activation(r.logits[0:w, t, :], acc[0:w, 0:NG + NE], ACT.Copy).then_inc(logits_stored, 1)

        @block.gpsimd
        def _(pool):
            for i, u in enumerate(units):
                if not u.stick:
                    k = kind_no[i]
                    p = prob[:, i % 4, 0:u.n]
                    pool.wait_ge(inverse_ready, k + 1)
                    pool.tensor_scalar(p, p, row_stat[:, 2, k:k + 1], None, ALU.mult).then_inc(prob_ready[False], 1)

        @block.vector
        def _(dve):
            if split:
                dve.memset(oT[:, 0].bitcast(F32), 0.0)
                dve.memset(oT_rest[:, 0].bitcast(F32), 0.0)
            dve.memset(r.logits[:, PT, :], 0.0).then_inc(cleared, 1)
            dve.wait_ge(cleared, 1)

            def store_turned(i):
                pos, u = turns["unit", i], units[i]
                dve.wait_ge(turned_ready, pos + 1)
                if i >= 3:
                    dve.wait_ge(mixed_ready, i - 2)
                full = 2 if u.sample else u.blocks
                done = dve.tensor_copy(pT[:, i % 3, 0:full, :], turned[:, pos % 2, 0:full * P].rearrange("p (k n) -> p k n", k=full))
                if u.sample:
                    done = dve.tensor_copy(pT[0:SAMPLE, i % 3, 2, :], turned[0:SAMPLE, pos % 2, 2 * P:3 * P])
                done.then_inc(turned_stored, 1)

            refined = 0
            for s in range(END):
                for i, u in units_of(s):
                    if not u.stick:
                        k = kind_no[i]
                        dve.wait_ge(scores_ready[False], k + 1)
                        dve.tensor_reduce(row_stat[:, 0, k:k + 1], scores_of(i)[:, 0:u.n], AX.X, ALU.max, negate=True).then_inc(neg_max_ready, 1)
                if split and s < 4:
                    dve.wait_ge(w_rounded, s + 1)
                    dve.tensor_tensor(w_low[:, s], w_raw[:, s % 2], w_high[:, s].bitcast(F32), ALU.subtract).then_inc(w_split, 1)
                for i, u in units_of(s):
                    if not u.stick:
                        continue
                    k = kind_no[i]
                    z, buf, out = scores_of(i)[:, 0:u.n], prob[:, i % 4, 0:u.n], work[:, k % 2, 0:u.n]
                    dve.wait_ge(soft_ready, k + 1)
                    dve.scalar_tensor_tensor(out=buf, in0=z, scalar=0.0, in1=buf, op0=ALU.max, op1=ALU.add).then_inc(sum_ready, 1)
                    dve.wait_ge(sum_ready, k + 1)
                    if k >= 2:
                        dve.wait_ge(prob_ready[True], k - 1)
                    dve.tensor_tensor_scan(out[:, ::-1], m.ones[:, 0:u.n], buf[:, ::-1], 0.0, ALU.mult, ALU.add).then_inc(suffix_ready, 1)
                    dve.wait_ge(suffix_ready, k + 1)
                    dve.tensor_tensor(out, z, out, ALU.subtract).then_inc(exponent_ready, 1)
                    dve.wait_ge(exponent_ready, k + 1)
                    dve.sem_inc(scores_used[True], 1)
                for i, u in units_of(s):
                    if not u.stick:
                        k = kind_no[i]
                        dve.wait_ge(exp_ready, k + 1)
                        dve.sem_inc(scores_used[False], 1)
                        dve.reciprocal(row_stat[:, 2, k:k + 1], row_stat[:, 1, k:k + 1]).then_inc(inverse_ready, 1)
                for q in (1, 3):
                    for o, t in tiles_at(s, 3 + q):
                        n, w = q // 2, width(t)
                        x = m.x[0:w, t, n * 512:(n + 1) * 512]
                        dve.wait_ge(group_ready, 2 * o + n + 1)
                        dve.tensor_tensor(x, acc[0:w, :], x, ALU.add).then_inc(added, 1)
                for i, _ in units_of(s - 1):
                    store_turned(i)
                if split:
                    for i, u in units_of(s - 2):
                        o = sum(end < s - 2 for end in last_step)
                        h0, h1 = u.heads[0], u.heads[-1] + 1
                        w = width(u.t)
                        dve.wait_ge(mixed_stored, i + 1)
                        dve.tensor_tensor(oT_rest[:, o % 2, h0:h1, 0:w], mixed[:, i % 2, 0:P].rearrange("p (h n) -> p h n", h=h1 - h0),
                                          oT[:, o % 2, h0:h1, 0:w].bitcast(F32), ALU.subtract).then_inc(rest_stored, 1)
                for o, t in tiles_at(s, 7):
                    dve.wait_ge(squared, o + 1)
                    v, y, tmp = stat[:, 1, o:o + 1], stat[:, 3, o:o + 1], stat[:, 4, o:o + 1]
                    dve.tensor_scalar(v, stat[:, 0, o:o + 1], 1.0 / D, EPS, ALU.mult, ALU.add).then_inc(mean_ready, 1)
                    dve.wait_ge(root_ready, o + 1)
                    dve.scalar_tensor_tensor(out=tmp, in0=y, scalar=v, in1=y, op0=ALU.mult, op1=ALU.mult).then_inc(newton, 1)
                    dve.wait_ge(newton, refined + 1)
                    dve.tensor_scalar(tmp, tmp, -0.5, 1.5, ALU.mult, ALU.add).then_inc(newton, 1)
                    dve.wait_ge(newton, refined + 2)
                    dve.tensor_tensor(stat[:, 5, o:o + 1], y, tmp, ALU.mult).then_inc(newton, 1)
                    dve.wait_ge(newton, refined + 3)
                    refined += 3
                    if o == 0:
                        dve.wait_ge(small_loaded, 48)
                    if o >= 2:
                        dve.wait_ge(h_saved[o % 2], 16 * (o // 2))
                        dve.wait_ge(turned_ready, turns["norm", o - 2, 1] + 1)
                    dve.scalar_tensor_tensor(out=h[:, o % 2, :], in0=m.x[:, t, :], scalar=stat[:, 5, o:o + 1], in1=g[:, :],
                                             op0=ALU.mult, op1=ALU.mult).then_inc(h_ready, 1)
                for o, t in tiles_at(s, 8):
                    w = width(t)
                    for half in range(2):
                        pos = turns["norm", o, half]
                        dve.wait_ge(turned_ready, pos + 1)
                        if o and half == 0:
                            dve.wait_ge(logits_ready, o)
                        dve.tensor_copy(hT[:, 4 * half:4 * half + 4, 0:w],
                                        turned[:, pos % 2, :].rearrange("p (c n) -> p c n", c=4)[:, :, 0:w]).then_inc(turned_stored, 1)


def router_stage(nc, m, r, name):
    with ExitStack() as ctx:
        sb, ps, sem = tools(nc, ctx, name)
        logits = r.logits
        col = sb("col", [P, 14, NT])
        quad = sb("quad", [P, 10, NT, NG])
        wide = sb("wide", [P, NT, NE])
        chosen = sb("chosen", [P, NT, NE])
        chosen16 = sb("chosen16", [P, NT, NE], BF16)
        place = ps("place", [P, NT + 1, NE])
        chosen_ready, place_ready = sem("chosen_ready"), sem("place_ready")
        chain_sem, for_act, from_act = sem("chain"), sem("for_act"), sem("from_act")
        block = ctx.enter_context(nc.Block())

        @block.tensor
        def _(pe):
            pe.wait_ge(chosen_ready, 1)
            for t in range(NT + 1):
                for s in range(min(t, PT) + 1):
                    left = m.before[:, :] if s == t else m.ones16[:, :]
                    last = pe.matmul(place[:, t, :], left, chosen16[:, s, :], start=(s == 0), stop=(s == min(t, PT)))
            last.then_inc(place_ready, 1)

        @block.scalar
        def _(act):
            act.wait_ge(for_act, 1)
            act.activation(quad[:, 1], quad[:, 0], ACT.Exp).then_inc(from_act, 1)
            act.wait_ge(for_act, 2)
            act.activation(col[:, 5, :], col[:, 4, :], ACT.Exp).then_inc(from_act, 1)

        @block.vector
        def _(dve):
            step = Chain(dve, chain_sem)

            def over(x, n):
                return x.unsqueeze(2).broadcast_to([P, NT, n])

            first = m.consts[:, C_FIRST:C_FIRST + 4].unsqueeze(1).broadcast_to([P, NT, 4])

            def first_max(out, best, values, tmp):
                step(dve.tensor_tensor(tmp, values, over(best, 4), ALU.is_equal))
                step.wait()
                step(dve.tensor_tensor(tmp, tmp, first, ALU.mult))
                step.wait()
                step(dve.tensor_reduce(col[:, 13, :], tmp, AX.X, ALU.max))
                step.wait()
                step(dve.tensor_tensor(out, tmp, over(col[:, 13, :], 4), ALU.is_equal))
                step.wait()

            groups = logits[:, :, 0:NG]
            step(dve.tensor_reduce(col[:, 0, :], groups, AX.X, ALU.max))
            step.wait()
            dve.tensor_tensor(quad[:, 0], groups, over(col[:, 0, :], 4), ALU.subtract).then_inc(for_act, 1)
            first_max(quad[:, 2], col[:, 0, :], groups, quad[:, 3])
            experts = logits[:, :, NG:].rearrange("p t (g e) -> p t g e", g=NG)
            group_of = quad[:, 2].unsqueeze(3).broadcast_to([P, NT, NG, EPG])
            wide4 = wide[:, :, :].rearrange("p t (g e) -> p t g e", g=NG)
            step(dve.tensor_tensor(wide4, experts, group_of, ALU.mult))
            step.wait()
            step(dve.tensor_reduce(quad[:, 4], wide[:, :, :].rearrange("p t (g e) -> p t e g", g=NG), AX.X, ALU.add))
            step.wait()
            step(dve.tensor_reduce(col[:, 1, :], quad[:, 4], AX.X, ALU.max))
            step.wait()
            first_max(quad[:, 5], col[:, 1, :], quad[:, 4], quad[:, 3])
            step(dve.tensor_scalar(quad[:, 7], quad[:, 5], -1.0, 1.0, ALU.mult, ALU.add))
            step.wait()
            step(dve.tensor_tensor(quad[:, 7], quad[:, 7], quad[:, 4], ALU.mult))
            step.wait()
            step(dve.scalar_tensor_tensor(out=quad[:, 6], in0=quad[:, 5], scalar=TAKEN, in1=quad[:, 7], op0=ALU.mult, op1=ALU.add))
            step.wait()
            step(dve.tensor_reduce(col[:, 2, :], quad[:, 6], AX.X, ALU.max))
            step.wait()
            first_max(quad[:, 8], col[:, 2, :], quad[:, 6], quad[:, 3])
            dve.tensor_tensor(col[:, 4, :], col[:, 2, :], col[:, 1, :], ALU.subtract).then_inc(for_act, 1)
            step(dve.tensor_tensor(quad[:, 9], quad[:, 2], over(m.consts[:, C_VALID:C_VALID + NT], NG), ALU.mult))
            step.wait()
            group_of = quad[:, 9].unsqueeze(3).broadcast_to([P, NT, NG, EPG])
            for j, q in enumerate((5, 8)):
                step(dve.tensor_tensor(r.pick[:, j].rearrange("p t (g e) -> p t g e", g=NG), group_of,
                                       quad[:, q].unsqueeze(2).broadcast_to([P, NT, NG, EPG]), ALU.mult))
            step.wait()
            step(dve.tensor_tensor(chosen[:, :, :], r.pick[:, 0], r.pick[:, 1], ALU.add))
            step.wait()
            dve.tensor_copy(chosen16[:, :, :], chosen[:, :, :]).then_inc(chosen_ready, 1)
            dve.wait_ge(from_act, 2)
            step(dve.tensor_reduce(col[:, 3, :], quad[:, 1], AX.X, ALU.add))
            step(dve.tensor_scalar(col[:, 6, :], col[:, 5, :], 1.0, None, ALU.add))
            step.wait()
            step(dve.tensor_tensor(col[:, 7, :], col[:, 3, :], col[:, 6, :], ALU.mult))
            step.wait()
            step(dve.reciprocal(r.gate[:, 0, :], col[:, 7, :]))
            step.wait()
            step(dve.tensor_tensor(r.gate[:, 1, :], r.gate[:, 0, :], col[:, 5, :], ALU.mult))
            dve.wait_ge(place_ready, 1)
            for j in range(2):
                step(dve.tensor_tensor(wide[:, :, :], r.pick[:, j], place[:, 0:NT, :], ALU.mult))
                step.wait()
                step(dve.tensor_reduce(r.place[:, j, :], wide[:, :, :], AX.X, ALU.add))
                step.wait()
                step(dve.tensor_tensor(wide[:, :, :], r.pick[:, j],
                                       m.consts[:, C_EXPERT:C_EXPERT + NE].unsqueeze(1).broadcast_to([P, NT, NE]), ALU.mult))
                step.wait()
                step(dve.tensor_reduce(col[:, 8, :], wide[:, :, :], AX.X, ALU.add))
                step.wait()
                step(dve.tensor_scalar(r.expert_row[:, j, :], col[:, 8, :], float(P), None, ALU.mult))
            step(dve.tensor_reduce(col[:, 10, 0:1], place[:, NT, :], AX.X, ALU.max))
            step.wait()
            step(dve.tensor_copy(r.most[0:1, 0:1], col[0:1, 10, 0:1]))
            step.wait()



def expert_stage(nc, m, r, name, layer, io):
    with ExitStack() as ctx:
        sb, ps, sem = tools(nc, ctx, name)
        take = sb("take", [P, 2, P])
        value = sb("value", [P, 2, NE])
        slots = sb("slots", [P, NE], U32)
        slot_col = sb("slot_col", [P, 2], U32)
        xg = sb("xg", [P, 2, D])
        xT = sb("xT", [P, 2, DC, P])
        silu = sb("silu", [P, 2, FE])
        act_rows = sb("act_rows", [P, 2, FE])
        actT = sb("actT", [P, 2, 2, P])
        y = sb("y", [P, 2, D])
        got = sb("got", [P, 4, D])
        served = sb("served", [P, 2, NT])
        pass_gate = sb("pass_gate", [P, 2, NT])
        row = sb("row", [P, 2, NT])
        result_row = sb("result_row", [P, 2, NT], U32)
        turned = ps("turned", [P, 2, 512])
        hidden = ps("hidden", [P, 2, 2 * FE])
        act_turned_ps = ps("act_turned_ps", [P, 2, 2, P])
        down = ps("down", [P, 2, 512])
        table = ps("table", [P, 512])
        ring = sb("ring", [P, 3 * 4096])
        w_hidden = [ring[:, b * 6144:b * 6144 + 4096].rearrange("p (c n) -> p c n", c=DC) for b in range(2)]
        w_down = [ring[:, b * 6144 + 4096:(b + 1) * 6144].rearrange("p (c n) -> p c n", c=2) for b in range(2)]
        hidden_loaded = [sem("hidden_loaded0"), sem("hidden_loaded1")]
        down_loaded = [sem("down_loaded0"), sem("down_loaded1")]
        gathered = [sem("gathered0", kept=True), sem("gathered1", kept=True)]
        saved = [sem("saved0"), sem("saved1")]
        take_ready, take_used, table_ready, slots_ready = sem("take_ready"), sem("take_used"), sem("table_ready"), sem("slots_ready")
        col_ready, x_turned, xT_low, xT_high = sem("col_ready"), sem("x_turned"), sem("xT_low"), sem("xT_high")
        hidden_ready, silu_ready, act_ready = sem("hidden_ready"), sem("silu_ready"), sem("act_ready")
        act_turned, actT_ready, down_ready, y_low, y_high = sem("act_turned"), sem("actT_ready"), sem("down_ready"), sem("y_low"), sem("y_high")
        moved, passed, prepared, added = sem("moved"), sem("passed"), sem("prepared"), sem("added")
        got_ready = [sem(f"got_ready{b}", kept=True) for b in range(4)]
        block = ctx.enter_context(nc.Block())
        PICKS = 2 * NT
        USES = [len(range(b, PICKS, 4)) for b in range(4)]

        def wait_count(eng, signal, count):
            if not isinstance(count, int) or count > 0:
                eng.wait_ge(signal, count)

        def first_wait(eng, signal, count):
            if not isinstance(count, int) or count > 0:
                eng.wait_ge(signal, count)
                eng.sem_inc(passed, 1)

        def all_passes(eng, one_pass):
            one_pass(0)
            most = eng.value_load(r.most[0:1, 0:1], min_val=0, max_val=T)
            with eng.If(most > SLOTS):
                with eng.Fori(1, PASSES) as c:
                    one_pass(c)

        def steps(eng, c, step):
            with eng.Fori(0, 6) as i:
                for j in range(2):
                    step(i * 2 + 3 + j, c * NE + i * 2 + (3 + j), c * (NE // 2) + i + (1 + j), 1 - j)

        def fixed(c, e, step):
            step(e, c * NE + e, c * (NE // 2) + e // 2, e % 2)

        @block.sync
        def _(sp):
            def load_hidden(e, n, k, b):
                first_wait(sp, hidden_ready, n - 1)
                for j, w in enumerate((io["moe_w_gate"], io["moe_w_up"])):
                    sp.dma_start(w_hidden[b][:, :, j * FE:(j + 1) * FE],
                                 w[layer, bass.ds(e, 1)].rearrange("a (c p) f -> p (a c) f", p=P)).then_inc(hidden_loaded[b], 16)

            def load_down(e, n, k, b):
                first_wait(sp, down_ready, n - 1)
                sp.dma_start(w_down[b], io["moe_w_down"][layer, bass.ds(e, 1)].rearrange("a (c p) d -> p (a c) d", p=P)).then_inc(down_loaded[b], 16)

            def save(c):
                def body(e, n, k, b):
                    sp.wait_ge(y_low, n + 1)
                    first_wait(sp, y_high, n + 1)
                    sp.dma_start(r.y_dram.rearrange("(e p) d -> e p d", p=P)[bass.ds(e, 1)].rearrange("a p d -> (a p) d"),
                                 y[:, b, :]).then_inc(saved[b], 16)
                return body

            def one_pass(c):
                first_wait(sp, added, c * PICKS)
                for e in range(3):
                    fixed(c, e, load_hidden)
                    fixed(c, e, load_down)

                def step(e, n, k, b):
                    load_hidden(e, n, k, b)
                    save(c)(e - 3, n - 3, None, 1 - b)
                    load_down(e, n, k, b)

                steps(sp, c, step)
                fixed(c, NE - 1, step)
                for e in range(NE - 3, NE):
                    fixed(c, e, save(c))

            all_passes(sp, one_pass)

        @block.gpsimd
        def _(pool):
            def gather(e, n, k, b):
                first_wait(pool, x_turned, n - 1)
                pool.tensor_copy(slot_col[:, b:b + 1], slots[:, bass.ds(e, 1)]).then_inc(col_ready, 1)
                first_wait(pool, col_ready, n + 1)
                pool.indirect_dma_start(xg[:, b, :], None, r.h_dram, bass.IndirectOffsetOnAxis(slot_col[:, b:b + 1], 0)).then_inc(gathered[b], 16)

            def one_pass(c):
                pool.wait_ge(slots_ready, c + 1)
                for e in range(3):
                    fixed(c, e, gather)
                steps(pool, c, gather)
                fixed(c, NE - 1, gather)
                for b in range(2):
                    first_wait(pool, saved[b], (c + 1) * (16 * NE // 2))
                for i in range(PICKS):
                    t, j = divmod(i, 2)
                    w = width(t)
                    first_wait(pool, added, c * PICKS + max(i - 3, 0))
                    pool.indirect_dma_start(got[0:w, i % 4, :], None, r.y_dram,
                                            bass.IndirectOffsetOnAxis(result_row[0:w, j, t:t + 1], 0)).then_inc(got_ready[i % 4], 16)

            all_passes(pool, one_pass)

        @block.tensor
        def _(pe):
            def turn_x(e, n, k, b):
                pe.wait_ge(gathered[b], (k + 1) * 16)
                wait_count(pe, xT_low, n)
                wait_count(pe, xT_high, n)
                for c in range(DC):
                    last = pe.transpose(turned[:, c // 4, (c % 4) * P:(c % 4 + 1) * P], xg[:, b, c * P:(c + 1) * P], m.ident[:, :])
                last.then_inc(x_turned, 1)

            def make_hidden(e, n, k, b):
                pe.wait_ge(xT_low, n + 1)
                pe.wait_ge(xT_high, n + 1)
                pe.wait_ge(hidden_loaded[b], (k + 1) * 32)
                wait_count(pe, act_ready, n - 1)
                for c in range(DC):
                    last = pe.matmul(hidden[:, b, :], xT[:, b, c, :], w_hidden[b][:, c, :], start=(c == 0), stop=(c == DC - 1))
                last.then_inc(hidden_ready, 1)

            def turn_act(e, n, k, b):
                pe.wait_ge(act_ready, n + 1)
                for c in range(2):
                    last = pe.transpose(act_turned_ps[:, b, c, :], act_rows[:, b, c * P:(c + 1) * P], m.ident[:, :])
                last.then_inc(act_turned, 1)

            def make_down(e, n, k, b):
                pe.wait_ge(actT_ready, n + 1)
                pe.wait_ge(down_loaded[b], (k + 1) * 16)
                wait_count(pe, y_low, n)
                wait_count(pe, y_high, n)
                for half in range(2):
                    for c in range(2):
                        last = pe.matmul(down[:, half, :], actT[:, b, c, :], w_down[b][:, c, half * 512:(half + 1) * 512], start=(c == 0), stop=(c == 1))
                last.then_inc(down_ready, 1)

            def one_pass(c):
                for i in range(PICKS):
                    pe.wait_ge(take_ready, c * PICKS + i + 1)
                    rows = width(i // 2)
                    pe.matmul(table[:, 0:NE], take[0:rows, i % 2, :], value[0:rows, i % 2, :], start=(i == 0), stop=(i == PICKS - 1)).then_inc(take_used, 1)
                fixed(c, 0, turn_x)
                fixed(c, 0, make_hidden)
                fixed(c, 1, turn_x)

                def step(e, n, k, b, more=True):
                    half = k - 1 + b
                    make_hidden(e, n, k, b)
                    turn_act(e - 1, n - 1, half, 1 - b)
                    if more:
                        turn_x(e + 1, n + 1, k + b, 1 - b)
                    make_down(e - 1, n - 1, half, 1 - b)

                fixed(c, 1, step)
                fixed(c, 2, step)
                steps(pe, c, step)
                fixed(c, NE - 1, lambda e, n, k, b: step(e, n, k, b, more=False))
                fixed(c, NE - 1, turn_act)
                fixed(c, NE - 1, make_down)

            all_passes(pe, one_pass)

        @block.scalar
        def _(act):
            def store_xT(e, n, k, b):
                act.wait_ge(x_turned, n + 1)
                act.activation(xT[:, b, 0:4, :], turned[:, 0, :].rearrange("p (c n) -> p c n", c=4), ACT.Copy).then_inc(xT_low, 1)

            def gate(e, n, k, b):
                act.wait_ge(hidden_ready, n + 1)
                wait_count(act, act_ready, n - 1)
                act.activation(silu[:, b, :], hidden[:, b, 0:FE], ACT.Silu).then_inc(silu_ready, 1)

            def store_y(e, n, k, b):
                act.wait_ge(down_ready, n + 1)
                if not isinstance(k, int) or k > 0:
                    act.wait_ge(saved[b], k * 16)
                act.activation(y[:, b, 0:512], down[:, 0, :], ACT.Copy).then_inc(y_low, 1)

            def one_pass(c):
                fixed(c, 0, store_xT)
                fixed(c, 1, store_xT)

                def step(e, n, k, b, more=True):
                    half = k - 1 + b
                    gate(e - 1, n - 1, half, 1 - b)
                    if more:
                        store_xT(e + 1, n + 1, k + b, 1 - b)
                    store_y(e - 1, n - 1, half, 1 - b)

                fixed(c, 1, step)
                fixed(c, 2, step)
                steps(act, c, step)
                fixed(c, NE - 1, lambda e, n, k, b: step(e, n, k, b, more=False))
                fixed(c, NE - 1, gate)
                fixed(c, NE - 1, store_y)

            all_passes(act, one_pass)

        @block.vector
        def _(dve):
            def store_xT(e, n, k, b):
                dve.wait_ge(x_turned, n + 1)
                dve.tensor_copy(xT[:, b, 4:8, :], turned[:, 1, :].rearrange("p (c n) -> p c n", c=4)).then_inc(xT_high, 1)

            def multiply(e, n, k, b):
                dve.wait_ge(silu_ready, n + 1)
                wait_count(dve, act_turned, n - 1)
                dve.tensor_tensor(act_rows[:, b, :], hidden[:, b, FE:2 * FE], silu[:, b, :], ALU.mult).then_inc(act_ready, 1)

            def store_actT(e, n, k, b):
                dve.wait_ge(act_turned, n + 1)
                wait_count(dve, down_ready, n - 1)
                dve.tensor_copy(actT[:, b, :, :], act_turned_ps[:, b, :, :]).then_inc(actT_ready, 1)

            def store_y(e, n, k, b):
                dve.wait_ge(down_ready, n + 1)
                if not isinstance(k, int) or k > 0:
                    dve.wait_ge(saved[b], k * 16)
                dve.tensor_copy(y[:, b, 512:1024], down[:, 1, :]).then_inc(y_high, 1)

            def one_pass(c):
                if not isinstance(c, int):
                    dve.tensor_scalar(r.place[:, :, :], r.place[:, :, :], float(-SLOTS), None, ALU.add).then_inc(moved, 1)
                    dve.wait_ge(moved, c)
                p0 = c * 4
                dve.tensor_scalar(served[:, :, :], r.place[:, :, :], 0.0, None, ALU.is_ge).then_inc(prepared, 1)
                dve.wait_ge(prepared, p0 + 1)
                dve.scalar_tensor_tensor(out=served[:, :, :], in0=r.place[:, :, :], scalar=float(SLOTS), in1=served[:, :, :], op0=ALU.is_lt, op1=ALU.mult)
                dve.tensor_tensor(row[:, :, :], r.place[:, :, :], r.expert_row[:, :, :], ALU.add).then_inc(prepared, 1)
                dve.wait_ge(prepared, p0 + 2)
                dve.tensor_tensor(pass_gate[:, :, :], r.gate[:, :, :], served[:, :, :], ALU.mult)
                dve.tensor_tensor(row[:, :, :], row[:, :, :], served[:, :, :], ALU.mult).then_inc(prepared, 1)
                dve.wait_ge(prepared, p0 + 3)
                dve.tensor_copy(result_row[:, :, :], row[:, :, :]).then_inc(prepared, 1)
                dve.wait_ge(prepared, p0 + 4)
                for i in range(PICKS):
                    t, j = divmod(i, 2)
                    wait_count(dve, take_used, c * PICKS + (i - 1))
                    dve.tensor_scalar(take[:, i % 2, :], m.consts[:, C_SLOT:C_SLOT + P], r.place[:, j, t:t + 1], None, ALU.is_equal)
                    dve.tensor_scalar(value[:, i % 2, :], r.pick[:, j, t, :], m.consts[:, C_TOKEN + t:C_TOKEN + t + 1], None, ALU.mult).then_inc(take_ready, 1)
                dve.wait_ge(take_used, c * PICKS + PICKS)
                if not isinstance(c, int):
                    dve.wait_ge(x_turned, c * NE)
                dve.tensor_copy(slots[:, :], table[:, 0:NE]).then_inc(slots_ready, 1)
                fixed(c, 0, store_xT)
                fixed(c, 1, store_xT)

                def step(e, n, k, b, more=True):
                    half = k - 1 + b
                    multiply(e - 1, n - 1, half, 1 - b)
                    store_actT(e - 1, n - 1, half, 1 - b)
                    if more:
                        store_xT(e + 1, n + 1, k + b, 1 - b)
                    store_y(e - 1, n - 1, half, 1 - b)

                fixed(c, 1, step)
                fixed(c, 2, step)
                steps(dve, c, step)
                fixed(c, NE - 1, lambda e, n, k, b: step(e, n, k, b, more=False))
                for last in (multiply, store_actT, store_y):
                    fixed(c, NE - 1, last)
                for i in range(PICKS):
                    t, j = divmod(i, 2)
                    w = width(t)
                    x = m.x[0:w, t, :]
                    dve.wait_ge(got_ready[i % 4], (c * USES[i % 4] + (i // 4 + 1)) * 16)
                    if j:
                        dve.wait_ge(added, c * PICKS + i)
                    dve.scalar_tensor_tensor(out=x, in0=got[0:w, i % 4, :], scalar=pass_gate[0:w, j, t:t + 1], in1=x,
                                             op0=ALU.mult, op1=ALU.add).then_inc(added, 1)

            all_passes(dve, one_pass)


def project_dsa_stage(nc, m, a, high, low, io):
    with ExitStack() as ctx:
        sb, ps, sem = tools(nc, ctx, "dsa")
        rope = sb("rope", [P, R_COLS])
        idx_rows = sb("idx_rows", [P, 2, IDX_COLS])
        idx_rot = sb("idx_rot", [P, 2, 6, D_IDX])
        idx_tmp = sb("idx_tmp", [P, 2, 5, D_IDX])
        idx_w = sb("idx_w", [P, NT, H_IDX])
        cache_i = sb("cache_i", [P, 2, 2, D_IDX])
        cache_k = sb("cache_k", [P, 2, KV_DSA * HEAD])
        qiT = sb("qiT", [P, 2, T])
        kiT = sb("kiT", [P, PROMPT])
        kiT_sample = sb("kiT_sample", [P, LS])
        relu = sb("relu", [P, 2, 512])
        COLS = 2 * HEAD
        rows = sb("rows", [P, 2, COLS])
        rot = sb("rot", [P, 2, COLS])
        tmp = sb("tmp", [P, 2, COLS])
        stat = sb("stat", [P, 6, NT])
        w_raw = sb("w_raw", [P, 2, DC, IDX_COLS])
        w_high = sb("w_high", [P, 2, DC, IDX_COLS], F32R)
        w_low = sb("w_low", [P, 2, DC, IDX_COLS], F32R)
        acc = ps("acc", [P, 4, 512])
        turned = ps("turned", [P, 2, 512])
        logit = ps("logit", [P, 2, 512])
        w_loaded = [sem("w_loaded0"), sem("w_loaded1")]
        w_high_ready, w_low_ready = sem("w_high_ready"), sem("w_low_ready")
        small_loaded, cache_v_loaded = sem("small_loaded"), sem("cache_v_loaded")
        group_ready, group_stored = sem("group_ready"), sem("group_stored")
        idx_chain, idx_rot_ready, pool_chain, rot_ready = sem("idx_chain"), sem("idx_rot_ready"), sem("pool_chain"), sem("rot_ready")
        idx_turned, idx_T_stored = sem("idx_turned"), sem("idx_T_stored")
        logit_ready, relu_ready, score_step = sem("logit_ready"), sem("relu_ready"), sem("score_step")
        rows_turned, rows_T_stored = sem("rows_turned"), sem("rows_T_stored")
        best_found, best_taken, barred = sem("best_found"), sem("best_taken"), sem("barred")
        idx_saved = [sem("idx_saved0"), sem("idx_saved1")]
        k_saved = [sem("k_saved0"), sem("k_saved1")]
        v_saved = sem("v_saved")
        free = a.qT[:, :, :].rearrange("p h n -> p (h n)")
        norm = Norm(m, sem, io["norm_mix"][1], free[:, 3 * D:4 * D], free[:, 0:2 * D].rearrange("p (b n) -> p b n", b=2),
                    free[:, 2 * D:3 * D], stat, acc, high, low)
        block = ctx.enter_context(nc.Block())

        UNITS = [(1536, IDX_COLS), (1024, COLS)] + [(pair * COLS, COLS) for pair in range(4)] + [(1280, COLS)]
        NI = NT
        NR = 5 * NT
        TILES = [3, PT, 2, 1]
        SCORES = [(t, h) for t in TILES for h in range(H_IDX)]
        SIZE = {t: (LS if t == PT else (t + 1) * P) for t in TILES}
        ROUNDS = {t: (K_SAMPLE if t == PT else K_PROMPT) // 8 for t in TILES}
        best = {t: sb(f"best{t}", [P, 8]) for t in TILES}
        score = {t: sb(f"score{t}", [P, SIZE[t]]) for t in TILES}

        @block.sync
        def _(sp):
            w_view = io["w_in_dsa"].rearrange("(c p) n -> p c n", p=P)

            def load_unit(i):
                lo, n = UNITS[i]
                if i >= 2:
                    sp.wait_ge(w_low_ready, i - 1)
                sp.dma_start(w_raw[:, i % 2, :, 0:n], w_view[:, :, lo:lo + n]).then_inc(w_loaded[i % 2], 16)

            norm.load(sp)
            load_unit(0)
            sp.dma_start(rope[:, :], io["rope"]).then_inc(small_loaded, 16)
            for twice in range(2):
                sp.dma_start(cache_i[:, :, twice, :], io["cache_dsa_idx_k"].rearrange("b (j p) e -> p (b j) e", p=P)).then_inc(small_loaded, 16)
            sp.dma_start(cache_k[:, :, :], io["cache_dsa_k"].rearrange("b (j p) h d -> p (b j) (h d)", p=P)).then_inc(small_loaded, 16)
            load_unit(1)
            sp.dma_start(a.cache_v[:, :, :], io["cache_dsa_v"].rearrange("b (j p) h d -> p (b j) (h d)", p=P)).then_inc(cache_v_loaded, 16)
            load_unit(2)
            for t in range(NT):
                w = width(t)
                sp.wait_ge(idx_rot_ready, t + 1)
                dst = io["out_dsa_idx"][0].rearrange("b t e -> (b t) e")[t * P:(t + 1) * P, :] if t < PT else io["out_dsa_idx"][1].rearrange("b t e -> (b t) e")
                sp.dma_start(dst, idx_rot[0:w, t % 2, 4, :]).then_inc(idx_saved[t % 2], 16)
            load_unit(3)
            for t in range(NT):
                sp.wait_ge(rot_ready, t + 1)
                sp.dma_start(rows_of(io["out_dsa_k"], t), rot[0:width(t), t % 2, :]).then_inc(k_saved[t % 2], 16)
            for i in range(4, len(UNITS)):
                load_unit(i)
            for t in range(NT):
                sp.wait_ge(group_stored, NI + NR + t + 1)
                sp.dma_start(rows_of(io["out_dsa_v"], t), a.v_rows[0:width(t), t, :]).then_inc(v_saved, 16)
            sp.wait_ge(idx_saved[0], 48)
            sp.wait_ge(idx_saved[1], 32)
            sp.wait_ge(k_saved[0], 48)
            sp.wait_ge(k_saved[1], 32)
            sp.wait_ge(v_saved, 16 * NT)
            sp.wait_ge(cache_v_loaded, 16)

        @block.tensor
        def _(pe):
            def group(g):
                i, t = divmod(g, NT)
                n = UNITS[i][1]
                if t == 0:
                    pe.wait_ge(w_low_ready, i + 1)
                if g >= 4:
                    pe.wait_ge(group_stored, g - 3)
                norm.product(pe, acc[:, g % 4, 0:n], t, w_high[:, i % 2, :, 0:n], w_low[:, i % 2, :, 0:n]).then_inc(group_ready, 1)

            def turn_idx(t):
                w = width(t)
                pe.wait_ge(idx_rot_ready, t + 1)
                pe.wait_ge(idx_T_stored, t + 1)
                for j in range(3):
                    last = pe.transpose(turned[:, t % 2, j * P:j * P + w], idx_rot[0:w, t % 2, 2 * j:2 * j + 2, :].rearrange("p h e -> p (h e)"), m.ident[0:w, 0:w])
                last.then_inc(idx_turned, 1)

            for t in range(NT):
                norm.turn(pe, t)
            pe.wait_ge(small_loaded, 64)
            for kb in range(2):
                for h in range(2):
                    last = pe.transpose(turned[:, 0, (2 * h + kb) * P:(2 * h + kb + 1) * P], cache_k[:, kb, h * P:(h + 1) * P], m.ident[:, :])
            last.then_inc(idx_turned, 1)
            for kb in range(2):
                last = pe.transpose(turned[:, 1, kb * P:(kb + 1) * P], cache_i[:, kb, :, :].rearrange("p a e -> p (a e)"), m.ident[:, :])
            last.then_inc(idx_turned, 1)
            pe.wait_ge(norm.low_ready, NT)
            for t in range(NT):
                group(t)
                if t >= 1:
                    turn_idx(t - 1)
            turn_idx(NT - 1)
            pe.wait_ge(idx_T_stored, 2 + NT)
            for i, (t, h) in enumerate(SCORES):
                half = slice((h % 2) * 64, (h % 2) * 64 + 64)
                w = width(t)
                if i >= 2:
                    pe.wait_ge(relu_ready, i - 1)
                keys = kiT_sample[half, :] if t == PT else kiT[half, 0:SIZE[t]]
                pe.matmul(logit[0:w, i % 2, 0:SIZE[t]], qiT[half, h // 2, cols(t)], keys, start=True, stop=True).then_inc(logit_ready, 1)

            def turn_rows(i):
                w = width(i % NT)
                pe.wait_ge(rot_ready, i + 1)
                if i >= 2:
                    pe.wait_ge(rows_T_stored, i - 1)
                for h in range(2):
                    last = pe.transpose(turned[:, i % 2, h * P:h * P + w], rot[0:w, i % 2, h * P:(h + 1) * P], m.ident[0:w, 0:w])
                last.then_inc(rows_turned, 1)

            for i in range(NR + NT):
                group(NI + i)
                if 2 <= i < NR + 2:
                    turn_rows(i - 2)

        @block.scalar
        def _(act):
            def cut_high(i):
                n = UNITS[i][1]
                act.wait_ge(w_loaded[i % 2], 16 * (i // 2 + 1))
                if i >= 2:
                    act.wait_ge(group_ready, (i - 1) * NT)
                act.activation(w_high[:, i % 2, :, 0:n], w_raw[:, i % 2, :, 0:n], ACT.Copy).then_inc(w_high_ready, 1)

            for t in range(NT):
                norm.square(act, t)
            norm.root(act)
            cut_high(0)
            for t in range(NT):
                norm.store_high(act, t)
            cut_high(1)
            for t in range(NT):
                w = width(t)
                act.wait_ge(group_ready, t + 1)
                if t >= 2:
                    act.wait_ge(idx_rot_ready, t - 1)
                act.activation(idx_rows[0:w, t % 2, :], acc[0:w, t % 4, 0:IDX_COLS], ACT.Copy).then_inc(group_stored, 1)
            cut_high(2)
            for i, (t, h) in enumerate(SCORES):
                w = width(t)
                act.wait_ge(logit_ready, i + 1)
                if i >= 2:
                    act.wait_ge(score_step, i - 1)
                act.activation(relu[0:w, i % 2, 0:SIZE[t]], logit[0:w, i % 2, 0:SIZE[t]], ACT.Relu, scale=D_IDX ** -0.5).then_inc(relu_ready, 1)

            def store_T(i):
                unit, t = divmod(i, NT)
                w = width(t)
                act.wait_ge(rows_turned, i + 1)
                if unit:
                    dst = a.qT[:, 2 * unit - 2:2 * unit, cols(t)]
                else:
                    dst = a.kT[:, :, t * P:(t + 1) * P] if t < PT else a.kT_sample[:, :, PAST:LS]
                act.activation(dst, turned[:, i % 2, 0:COLS].rearrange("p (h n) -> p h n", h=2)[:, :, 0:w], ACT.Copy).then_inc(rows_T_stored, 1)

            for i in range(NR + NT):
                unit, t = divmod(i, NT)
                w = width(t)
                g = NI + i
                act.wait_ge(group_ready, g + 1)
                if i < NR:
                    if i >= 2:
                        act.wait_ge(rot_ready, i - 1)
                    act.activation(rows[0:w, i % 2, :], acc[0:w, g % 4, 0:COLS], ACT.Copy, scale=SCALE if unit else 1.0).then_inc(group_stored, 1)
                else:
                    act.activation(a.v_rows[0:w, t, :], acc[0:w, g % 4, 0:COLS], ACT.Copy).then_inc(group_stored, 1)
                if 2 <= i < NR + 2:
                    store_T(i - 2)
                if t == NT - 1 and unit + 3 < len(UNITS):
                    cut_high(unit + 3)

        def rotate(eng, chain, out, x, tmp_a, tmp_b, cos, sin, heads):
            w, half = x.shape[0], x.shape[2] // 2
            swapped = x.rearrange("p h (s e) -> p h s e", s=2)[:, :, ::-1, :]
            chain(eng.tensor_tensor(tmp_a, x, cos.unsqueeze(1).broadcast_to([w, heads, 2 * half]), ALU.mult))
            chain(eng.tensor_tensor(tmp_b.rearrange("p h (s e) -> p h s e", s=2), swapped,
                                    sin.rearrange("p (s e) -> p s e", s=2).unsqueeze(1).broadcast_to([w, heads, 2, half]), ALU.mult))
            chain.wait()
            return eng.tensor_tensor(out, tmp_a, tmp_b, ALU.add)

        @block.gpsimd
        def _(pool):
            chain = Chain(pool, pool_chain)
            pool.wait_ge(small_loaded, 64)
            for i in range(NR):
                t = i % NT
                w = width(t)
                pool.wait_ge(group_stored, NI + i + 1)
                if i >= 2:
                    pool.wait_ge(rows_turned, i - 1)
                    if i < NT + 2:
                        pool.wait_ge(k_saved[i % 2], 16 * (i // 2))

                def view(x):
                    return x.rearrange("p (h d) -> p h d", d=HEAD)

                rotate(pool, chain, view(rot[0:w, i % 2, :]), view(rows[0:w, i % 2, :]), view(tmp[0:w, 0, :]), view(tmp[0:w, 1, :]),
                       rope[0:w, R_COS + t * HEAD:R_COS + (t + 1) * HEAD], rope[0:w, R_SIN + t * HEAD:R_SIN + (t + 1) * HEAD], 2).then_inc(rot_ready, 1)
                pool.wait_ge(rot_ready, i + 1)

        @block.vector
        def _(dve):
            chain = Chain(dve, idx_chain)

            def cut_low(i):
                n = UNITS[i][1]
                dve.wait_ge(w_high_ready, i + 1)
                dve.tensor_tensor(w_low[:, i % 2, :, 0:n], w_raw[:, i % 2, :, 0:n], w_high[:, i % 2, :, 0:n].bitcast(F32),
                                  ALU.subtract).then_inc(w_low_ready, 1)

            norm.clear_pad(dve)
            norm.inverse_root(dve)
            norm.scale(dve, 0)
            for t in range(1, NT):
                norm.scale(dve, t)
                if t == 1:
                    cut_low(0)
                norm.store_low(dve, t - 1)
            norm.store_low(dve, NT - 1)
            cut_low(1)
            dve.wait_ge(idx_turned, 1)
            dve.tensor_copy(a.kT_sample[:, :, 0:PAST], turned[:, 0, :].rearrange("p (h n) -> p h n", h=2)).then_inc(idx_T_stored, 1)
            dve.wait_ge(idx_turned, 2)
            dve.tensor_copy(kiT_sample[:, 0:PAST], turned[:, 1, 0:PAST]).then_inc(idx_T_stored, 1)

            def store_idx_T(t):
                w = width(t)
                dve.wait_ge(idx_turned, 3 + t)
                dve.tensor_copy(qiT[:, :, cols(t)], turned[:, t % 2, 0:2 * P].rearrange("p (h n) -> p h n", h=2)[:, :, 0:w])
                dst = kiT[:, t * P:(t + 1) * P] if t < PT else kiT_sample[:, PAST:LS]
                dve.tensor_copy(dst, turned[:, t % 2, 2 * P:2 * P + w]).then_inc(idx_T_stored, 1)

            dve.wait_ge(small_loaded, 64)
            for t in range(NT):
                w = width(t)
                dve.wait_ge(group_stored, t + 1)
                if t >= 2:
                    dve.wait_ge(idx_turned, 2 + t - 1)
                    dve.wait_ge(idx_saved[t % 2], 16 * (t // 2))
                x = idx_rows[0:w, t % 2, 0:5 * D_IDX].rearrange("p (h e) -> p h e", h=5)
                chain(rotate(dve, chain, idx_rot[0:w, t % 2, 0:5, :], x, idx_tmp[0:w, 0], idx_tmp[0:w, 1],
                             rope[0:w, R_ICOS + t * D_IDX:R_ICOS + (t + 1) * D_IDX], rope[0:w, R_ISIN + t * D_IDX:R_ISIN + (t + 1) * D_IDX], 5))
                chain(dve.tensor_scalar(idx_w[0:w, t, :], idx_rows[0:w, t % 2, 5 * D_IDX:IDX_COLS], H_IDX ** -0.5, None, ALU.mult))
                chain.wait()
                dve.tensor_copy(idx_rot[0:w, t % 2, 5, :], idx_rot[0:w, t % 2, 4, :]).then_inc(idx_rot_ready, 1)
                if t >= 1:
                    store_idx_T(t - 1)
            store_idx_T(NT - 1)
            cut_low(2)
            for i, (t, h) in enumerate(SCORES):
                w = width(t)
                s = score[t][0:w, :]
                dve.wait_ge(relu_ready, i + 1)
                if h == 0:
                    dve.tensor_scalar(s, relu[0:w, i % 2, 0:SIZE[t]], idx_w[0:w, t, 0:1], None, ALU.mult).then_inc(score_step, 1)
                else:
                    dve.wait_ge(score_step, i)
                    dve.scalar_tensor_tensor(out=s, in0=relu[0:w, i % 2, 0:SIZE[t]], scalar=idx_w[0:w, t, h:h + 1], in1=s,
                                             op0=ALU.mult, op1=ALU.add).then_inc(score_step, 1)
            dve.wait_ge(score_step, len(SCORES))
            for t in (3, 2, 1):
                last = dve.memset(score[t][0:CHUNK, SIZE[t] - CHUNK:SIZE[t]], BARRED)
            last.then_inc(barred, 1)
            dve.wait_ge(barred, 1)
            found = taken = 0
            for k in range(max(ROUNDS.values())):
                live = [t for t in TILES if k < ROUNDS[t]]
                if k:
                    dve.wait_ge(best_taken, taken)
                for t in live:
                    dve.max(best[t][0:width(t), :], score[t][0:width(t), :]).then_inc(best_found, 1)
                for j, t in enumerate(live):
                    dve.wait_ge(best_found, found + j + 1)
                    dve.match_replace(score[t][0:width(t), :], best[t][0:width(t), :], score[t][0:width(t), :], TAKEN).then_inc(best_taken, 1)
                found += len(live)
                taken += len(live)
                if k % 4 == 3 and 3 + k // 4 < len(UNITS):
                    cut_low(3 + k // 4)
            dve.wait_ge(best_taken, taken)
            for t in TILES:
                dve.tensor_scalar(a.unchosen[t][0:width(t), :], score[t][0:width(t), :], UNTAKEN_FROM, NEG, ALU.is_gt, ALU.mult)


def trunk_program(nc, io):
    with ExitStack() as ctx:
        def sb(name, shape, dtype=F32):
            return ctx.enter_context(nc.sbuf_tensor(name, shape, dtype))

        m = Main()
        m.x = sb("x", [P, NT, D])
        m.consts = sb("consts", [P, C_COLS])
        m.masks = sb("masks", [P, 4 * P], BF16)
        m.before = sb("before", [P, P], BF16)
        m.ones16 = sb("ones16", [P, P], BF16)
        m.ones = sb("ones", [P, 512])
        m.head_select = sb("head_select", [H_FOX, H_FOX * P])
        m.ident = m.consts[:, C_IDENT:C_IDENT + P]
        m.ident16 = m.masks[:, C_IDENT:C_IDENT + P]
        neg_sb, neg_fox, neg_chunk = (m.masks[:, c:c + P] for c in (C_NEG_SB, C_NEG_FOX, C_NEG_CHUNK))

        def routing(layer, scope):
            def sb(name, shape, dtype=F32):
                return scope.enter_context(nc.sbuf_tensor(f"moe{layer}_{name}", shape, dtype))

            r = Routing()
            r.w_group, r.w_router = io["moe_w_group"][layer], io["moe_w_router"][layer]
            r.logits = sb("logits", [P, NT, NG + NE])
            r.pick = sb("pick", [P, 2, NT, NE])
            r.place = sb("place", [P, 2, NT])
            r.gate = sb("gate", [P, 2, NT])
            r.expert_row = sb("expert_row", [P, 2, NT])
            r.most = sb("most", [P, 1], U32)
            r.h_dram = nc.dram_tensor(f"h_dram{layer}", (T, D), F32, kind="Internal").ap()
            r.y_dram = nc.dram_tensor(f"y_dram{layer}", (NE * P, D), F32, kind="Internal").ap()
            return r

        def tile_steps(pairs, sample):
            steps = [(sample, True)]
            for t in range(PT):
                steps += [([Unit([h], t, stick) for h, stick in pair], j == len(pairs) - 1) for j, pair in enumerate(pairs)]
            return steps

        r0, r1 = routing(0, ctx), routing(1, ctx)
        with ExitStack() as inner:
            def sb(name, shape, dtype=F32):
                return inner.enter_context(nc.sbuf_tensor(f"ab_{name}", shape, dtype))

            a = Attention()
            a.qT = sb("qT", [P, 8, T])
            a.kT = sb("kT", [P, 8, PROMPT])
            a.kT_sample = sb("kT_sample", [P, 8, LS])
            a.v_rows = sb("v_rows", [P, NT, D])
            a.cache_v = sb("cache_v", [P, 2, D])
            a.forget = sb("forget", [4, PROMPT])
            a.forget_sample = sb("forget_sample", [4, LS])
            with ExitStack() as parts:
                high, low = (parts.enter_context(nc.sbuf_tensor(f"ab_hT_{part}", [P, DC * T + P - SAMPLE], F32R)) for part in ("high", "low"))
                project_ab_stage(nc, m, a, high, low, io)
            pairs = [((h, True), (h + H_SB, False)) for h in range(H_SB)]
            sample = [Unit(list(range(h0, h0 + 4)), PT, h0 == 0) for h0 in (0, H_SB)]
            mixer_stage(nc, m, a, r0, "mixer0", tile_steps(pairs, sample), lambda h: h, lambda h: h, {True: neg_sb, False: neg_fox}, True,
                        io["w_out_ab"], io["norm_ffn"][0], split=False)
        router_stage(nc, m, r0, "route0")
        expert_stage(nc, m, r0, "experts0", 0, io)

        with ExitStack() as inner:
            def sb(name, shape, dtype=F32):
                return inner.enter_context(nc.sbuf_tensor(f"dsa_{name}", shape, dtype))

            a = Attention()
            a.qT = sb("qT", [P, H_DSA, T])
            a.kT = sb("kT", [P, KV_DSA, PROMPT])
            a.kT_sample = sb("kT_sample", [P, KV_DSA, LS])
            a.v_rows = sb("v_rows", [P, NT, KV_DSA * HEAD])
            a.cache_v = sb("cache_v", [P, 2, KV_DSA * HEAD])
            a.unchosen = {t: sb(f"unchosen{t}", [P, LS if t == PT else (t + 1) * P], BF16) for t in range(1, NT)}
            a.unchosen[0] = neg_chunk
            with ExitStack() as parts:
                high, low = (parts.enter_context(nc.sbuf_tensor(f"dsa_hT_{part}", [P, DC * T + P - SAMPLE], F32R)) for part in ("high", "low"))
                project_dsa_stage(nc, m, a, high, low, io)
            kv = lambda h: h // (H_DSA // KV_DSA)
            pairs = [((h, False), (h + 1, False)) for h in range(0, H_DSA, 2)]
            sample = [Unit(list(range(h0, h0 + 4)), PT) for h0 in (0, 4)]
            mixer_stage(nc, m, a, r1, "mixer1", tile_steps(pairs, sample), kv, kv, {False: None}, False,
                        io["w_out_dsa"], io["norm_ffn"][1], split=True)
        router_stage(nc, m, r1, "route1")
        expert_stage(nc, m, r1, "experts1", 1, io)
        y = [io["y_prompt"].rearrange("b t d -> (b t) d"), io["y_sample"].rearrange("b t d -> (b t) d")]
        norm_stage(nc, m, "final", io["norm_final"], y_dram=y)


_INS = ["x_prompt", "x_sample", "cache_sb_k", "cache_sb_v", "cache_fox_k", "cache_fox_v", "cache_fox_logf",
        "cache_dsa_k", "cache_dsa_v", "cache_dsa_idx_k", "norm_mix", "norm_ffn", "norm_final",
        "w_in_ab", "b_forget", "w_out_ab", "w_in_dsa", "w_out_dsa",
        "moe_w_group", "moe_w_router", "moe_w_gate", "moe_w_up", "moe_w_down"]


def _row_shapes(n):
    return [(1, n, H_SB, HEAD), (1, n, H_SB, HEAD), (1, n, H_FOX, HEAD), (1, n, H_FOX, HEAD), (1, n, H_FOX),
            (1, n, KV_DSA, HEAD), (1, n, KV_DSA, HEAD), (1, n, D_IDX)]


def _constants():
    import numpy as np

    p, j = np.arange(P)[:, None], np.arange(P)[None, :]
    consts = np.zeros((P, C_COLS), np.float32)
    consts[:, C_IDENT:C_IDENT + P] = p == j
    consts[:, C_NEG_SB:C_NEG_SB + P] = np.where(j >= p, NEG, 0)
    consts[:, C_NEG_FOX:C_NEG_FOX + P] = np.where(j > p, NEG, 0)
    consts[:, C_NEG_CHUNK:C_NEG_CHUNK + P] = np.where(j // CHUNK > p // CHUNK, NEG, 0)
    consts[:, C_BEFORE:C_BEFORE + P] = p < j
    consts[:, C_SLOT:C_SLOT + P] = j
    tile = np.arange(NT)[None, :]
    consts[:, C_TOKEN:C_TOKEN + NT] = np.minimum(tile * P + p, T - 1)
    consts[:, C_VALID:C_VALID + NT] = tile * P + p < T
    consts[:, C_FIRST:C_FIRST + 4] = 4 - np.arange(4)
    consts[:, C_EXPERT:C_EXPERT + NE] = np.arange(NE)
    select = np.zeros((H_FOX, H_FOX, P), np.float32)
    for h in range(H_FOX):
        select[h, h] = -1.0
    pos = np.where(tile < PT, tile * P + p, PAST + p).astype(np.float32)
    tables = []
    for size in (HEAD, D_IDX):
        half = size // 2
        inv = (10000.0 ** (-np.arange(half, dtype=np.float32) / np.float32(half)).astype(np.float64)).astype(np.float32)
        ang = (pos[:, :, None] * inv[None, None, :]).astype(np.float32).astype(np.float64)
        cos, sin = np.cos(ang).astype(np.float32), np.sin(ang).astype(np.float32)
        tables += [np.concatenate([cos, cos], 2).reshape(P, -1), np.concatenate([-sin, sin], 2).reshape(P, -1)]
    return {"consts": consts, "head_select": select.reshape(H_FOX, -1), "rope": np.concatenate(tables, 1).astype(np.float32)}


def kernel(**inputs):
    import numpy as np
    import concourse.bacc as bacc
    from concourse.bass_utils import run_bass_kernel_spmd

    nc = bacc.Bacc("TRN2", target_bir_lowering=False, num_devices=1)
    arrays = {name: np.ascontiguousarray(inputs[name]) for name in _INS}
    arrays.update(_constants())
    io = {}
    feed = {}
    for name, value in arrays.items():
        feed[f"in_{name}"] = value
        io[name] = nc.dram_tensor(f"in_{name}", value.shape, F32, kind="ExternalInput").ap()
    shapes = [(1, PROMPT, D), (1, SAMPLE, D)] + _row_shapes(PROMPT) + _row_shapes(SAMPLE)
    outs = [nc.dram_tensor(f"out_{i}", shape, F32, kind="ExternalOutput").ap() for i, shape in enumerate(shapes)]
    io["y_prompt"], io["y_sample"] = outs[0:2]
    (io["out_sb_k"], io["out_sb_v"], io["out_fox_k"], io["out_fox_v"], io["out_fox_logf"],
     io["out_dsa_k"], io["out_dsa_v"], io["out_dsa_idx"]) = [(outs[2 + i], outs[10 + i]) for i in range(8)]
    trunk_program(nc, io)
    r = run_bass_kernel_spmd(nc, [feed], core_ids=[0])
    return tuple(r.results[0][f"out_{i}"] for i in range(len(outs)))
```

```python
from contextlib import ExitStack

import concourse.bass as bass
from concourse import mybir

ALU = mybir.AluOpType
ACT = mybir.ActivationFunctionType
AX = mybir.AxisListType
F32 = mybir.dt.float32
F32R = mybir.dt.float32r
BF16 = mybir.dt.bfloat16
U32 = mybir.dt.uint32

P = 128
D = 1024
DC = D // P
PROMPT, SAMPLE, PAST = 512, 32, 256
PT = PROMPT // P
NT = PT + 1
T = PROMPT + SAMPLE
LS = PAST + SAMPLE
HEAD = 128
SCALE = HEAD ** -0.5
H_SB = H_FOX = 4
H_DSA, KV_DSA = 8, 2
H_IDX, D_IDX = 4, 64
IDX_COLS = H_IDX * D_IDX + D_IDX + H_IDX
CHUNK = 64
K_PROMPT = min(256, PROMPT // 4)
K_SAMPLE = min(256, LS // 4)
EPS = 1e-6
NG, EPG = 4, 4
NE = NG * EPG
FE = 256
SLOTS = P
PASSES = -(-T // SLOTS)
HALF_T = T // 2
NEG = -1e30
TAKEN = -3.4028234e38
BARRED = -3.2e38
UNTAKEN_FROM = -3.3e38

C_IDENT = 0
C_NEG_SB = P
C_NEG_FOX = 2 * P
C_NEG_CHUNK = 3 * P
C_BEFORE = 4 * P
C_SLOT = 5 * P
C_TOKEN = 6 * P
C_VALID = C_TOKEN + NT
C_FIRST = C_VALID + NT
C_EXPERT = C_FIRST + 4
C_COLS = C_EXPERT + NE
R_COS, R_SIN = 0, NT * HEAD
R_ICOS, R_ISIN = 2 * NT * HEAD, 2 * NT * HEAD + NT * D_IDX
R_COLS = 2 * NT * (HEAD + D_IDX)


def width(t):
    return P if t < PT else SAMPLE


def cols(t):
    return slice(t * P, t * P + width(t))


class Main:
    pass


class Routing:
    pass


class Attention:
    pass


class Chain:

    def __init__(self, eng, sem):
        self.eng, self.sem, self.n = eng, sem, 0

    def __call__(self, instruction):
        instruction.then_inc(self.sem, 1)
        self.n += 1

    def wait(self):
        self.eng.wait_ge(self.sem, self.n)


def tools(nc, ctx, prefix):
    def sb(name, shape, dtype=F32):
        return ctx.enter_context(nc.sbuf_tensor(f"{prefix}_{name}", shape, dtype))

    def ps(name, shape, dtype=F32):
        return ctx.enter_context(nc.psum_tensor(f"{prefix}_{name}", shape, dtype))

    mine = []

    def sem(name, kept=False):
        handle = nc.alloc_semaphore(f"{prefix}_{name}")
        if not kept:
            mine.append(handle)
        return handle

    def clear():
        numbers = sorted(s.num for s in mine)
        runs = [n for n in numbers if n - 1 not in numbers]
        for lo in runs:
            hi = lo
            while hi in numbers:
                hi += 1
            nc.gpsimd.sem_clear(range(lo, hi))
        for s in mine:
            nc.release_semaphore(s)

    ctx.callback(clear)
    return sb, ps, sem


class Norm:

    def __init__(self, m, sem, g_dram, g, h, squares, stat, turned=None, high=None, low=None, groups=((0, NT),)):
        self.groups = groups
        self.m, self.g_dram, self.g, self.h, self.squares, self.stat = m, g_dram, g, h, squares, stat
        self.turned, self.high, self.low = turned, high, low
        self.g_loaded, self.squared, self.mean_ready, self.root_ready = sem("g_loaded"), sem("squared"), sem("mean_ready"), sem("root_ready")
        self.newton, self.h_ready, self.h_turned = sem("newton"), sem("h_ready"), sem("h_turned")
        self.high_ready, self.low_ready = sem("h_high_ready"), sem("h_low_ready")

    def load(self, sp):
        sp.dma_start(self.g, self.g_dram.partition_broadcast(P)).then_inc(self.g_loaded, 16)

    def square(self, act, t):
        if t:
            act.wait_ge(self.squared, t)
        act.activation(self.squares, self.m.x[:, t, :], ACT.Square, accum_out=self.stat[:, 0, t:t + 1]).then_inc(self.squared, 1)

    def root(self, act, group):
        lo, hi = self.groups[group]
        act.wait_ge(self.mean_ready, group + 1)
        act.activation(self.stat[:, 2, lo:hi], self.stat[:, 1, lo:hi], ACT.Sqrt).then_inc(self.root_ready, 1)

    def inverse_root(self, dve, group):
        lo, hi = self.groups[group]
        total, v, root, y, tmp, scale = (self.stat[:, k, lo:hi] for k in range(6))
        dve.wait_ge(self.squared, hi)
        dve.tensor_scalar(v, total, 1.0 / D, EPS, ALU.mult, ALU.add).then_inc(self.mean_ready, 1)
        dve.wait_ge(self.root_ready, group + 1)
        dve.reciprocal(y, root).then_inc(self.newton, 1)
        dve.wait_ge(self.newton, 5 * group + 1)
        dve.tensor_tensor(tmp, y, y, ALU.mult).then_inc(self.newton, 1)
        dve.wait_ge(self.newton, 5 * group + 2)
        dve.tensor_tensor(tmp, tmp, v, ALU.mult).then_inc(self.newton, 1)
        dve.wait_ge(self.newton, 5 * group + 3)
        dve.tensor_scalar(tmp, tmp, -0.5, 1.5, ALU.mult, ALU.add).then_inc(self.newton, 1)
        dve.wait_ge(self.newton, 5 * group + 4)
        dve.tensor_tensor(scale, y, tmp, ALU.mult).then_inc(self.newton, 1)
        dve.wait_ge(self.newton, 5 * group + 5)
        if group == 0:
            dve.wait_ge(self.g_loaded, 16)

    def scale(self, dve, t, buffers=2):
        if t >= buffers:
            dve.wait_ge(self.h_turned, t - buffers + 1)
        dve.scalar_tensor_tensor(out=self.h[:, t % buffers, :], in0=self.m.x[:, t, :], scalar=self.stat[:, 5, t:t + 1],
                                 in1=self.g, op0=ALU.mult, op1=ALU.mult).then_inc(self.h_ready, 1)

    def turn(self, pe, t):
        w = width(t)
        pe.wait_ge(self.h_ready, t + 1)
        if t >= 2:
            pe.wait_ge(self.low_ready, t - 1)
        for c in range(DC):
            last = pe.transpose(self.turned[:, 2 * (t % 2) + c // 4, (c % 4) * P:(c % 4) * P + w],
                                self.h[0:w, t % 2, c * P:(c + 1) * P], self.m.ident[0:w, 0:w])
        last.then_inc(self.h_turned, 1)

    def parts(self, t, half):
        w = width(t)
        source = self.turned[:, 2 * (t % 2) + half, :].rearrange("p (c n) -> p c n", c=4)[:, :, 0:w]
        high, low = (x[:, 0:DC * T].rearrange("p (c n) -> p c n", c=DC)[:, 4 * half:4 * half + 4, cols(t)] for x in (self.high, self.low))
        return source, high, low

    def store_high(self, act, t):
        act.wait_ge(self.h_turned, t + 1)
        for half in range(2):
            source, high, _ = self.parts(t, half)
            act.activation(high, source, ACT.Copy).then_inc(self.high_ready, 1)

    def store_low(self, dve, t):
        for half in range(2):
            source, high, low = self.parts(t, half)
            dve.wait_ge(self.high_ready, 2 * t + half + 1)
            last = dve.tensor_tensor(low, source, high.bitcast(F32), ALU.subtract)
        last.then_inc(self.low_ready, 1)

    def clear_pad(self, dve):
        dve.memset(self.high[:, DC * T:].bitcast(F32), 0.0)
        dve.memset(self.low[:, DC * T:].bitcast(F32), 0.0)

    def product(self, pe, out, t, w_high, w_low):
        for c in range(DC):
            for high, weights in ((self.high, w_high), (self.high, w_low), (self.low, w_high)):
                last = pe.matmul(out, high[:, c * T + t * P:c * T + (t + 1) * P], weights[:, c, :],
                                 start=(c == 0 and weights is w_high and high is self.high), stop=(c == DC - 1 and high is self.low))
        return last


class Combine:

    def __init__(self, m, r, sem, got):
        self.m, self.r, self.got = m, r, got
        self.got_ready = [sem(f"got_ready{b}", kept=True) for b in range(len(got))]
        self.added = sem("results_added")

    def gather(self, pool, t):
        w = width(t)
        for j in range(2):
            i = 2 * t + j
            buf, first = i % len(self.got), i - len(self.got) + 1
            if first > 0:
                pool.wait_ge(self.added, first)
            pool.indirect_dma_start(self.got[buf][0:w, :], None, self.r.y_dram,
                                    bass.IndirectOffsetOnAxis(self.r.result_row[0:w, j, t:t + 1], 0)).then_inc(self.got_ready[buf], 16)

    def add(self, dve, t):
        w = width(t)
        x = self.m.x[0:w, t, :]
        for j in range(2):
            i = 2 * t + j
            buf, use = i % len(self.got), i // len(self.got)
            dve.wait_ge(self.got_ready[buf], 16 * (use + 1))
            if j:
                dve.wait_ge(self.added, i)
            dve.scalar_tensor_tensor(out=x, in0=self.got[buf][0:w, :], scalar=self.r.pass_gate[0:w, j, t:t + 1], in1=x,
                                     op0=ALU.mult, op1=ALU.add).then_inc(self.added, 1)


def final_stage(nc, m, r, g_dram, y_dram):
    with ExitStack() as ctx:
        sb, ps, sem = tools(nc, ctx, "final")
        g, h, squares, stat, got = sb("g", [P, D]), sb("h", [P, NT, D]), sb("squares", [P, D]), sb("stat", [P, 6, NT]), sb("got", [P, 2 * NT, D])
        groups = ((0, PT), (PT, NT))
        norm = Norm(m, sem, g_dram, g[:, :], h, squares[:, :], stat, groups=groups)
        combine = Combine(m, r, sem, [got[:, b, :] for b in range(2 * NT)])
        stored = sem("stored")
        block = ctx.enter_context(nc.Block())

        @block.sync
        def _(sp):
            norm.load(sp)
            for t in range(NT):
                sp.wait_ge(norm.h_ready, t + 1)
                dst = y_dram[0][t * P:(t + 1) * P, :] if t < PT else y_dram[1]
                sp.dma_start(dst, h[0:width(t), t, :]).then_inc(stored, 16)
            sp.wait_ge(stored, 16 * NT)

        @block.gpsimd
        def _(pool):
            for t in range(NT):
                combine.gather(pool, t)

        @block.scalar
        def _(act):
            act.preload_act_table_set("sqrt_and_others")
            for group, (lo, hi) in enumerate(groups):
                for t in range(lo, hi):
                    act.wait_ge(combine.added, 2 * t + 2)
                    norm.square(act, t)
                norm.root(act, group)

        @block.vector
        def _(dve):
            for t in range(NT):
                combine.add(dve, t)
            for group, (lo, hi) in enumerate(groups):
                norm.inverse_root(dve, group)
                for t in range(lo, hi):
                    norm.scale(dve, t, buffers=NT)


def rows_of(dram, t, heads=True):
    pattern = "b t h d -> (b t) (h d)" if heads else "b t d -> (b t) d"
    if t < PT:
        return dram[0].rearrange(pattern)[t * P:(t + 1) * P, :]
    return dram[1].rearrange(pattern)


def project_ab_stage(nc, m, a, high, low, io):
    with ExitStack() as ctx:
        sb, ps, sem = tools(nc, ctx, "ab")
        COLS = 2 * HEAD
        UNITS = [(part * 512 + kind * 1536 + pair * COLS, what, kind, pair) for what, part in (("k", 1), ("v", 2), ("q", 0))
                 for kind in range(2) for pair in range(2)]
        KG, VG, QG = 4 * NT, 4 * NT, 16
        w_raw = m.spare[:, 0:2 * DC * COLS].rearrange("p (b c n) -> p b c n", b=2, c=DC)
        w_high = sb("w_high", [P, 2, DC, COLS], F32R)
        w_low = sb("w_low", [P, 2, DC, COLS], F32R)
        w_forget = sb("w_forget", [P, DC, H_FOX])
        w_forget_high = sb("w_forget_high", [P, DC, H_FOX], F32R)
        w_forget_low = sb("w_forget_low", [P, DC, H_FOX], F32R)
        b_rows = sb("b_rows", [P, H_FOX])
        k_rows = sb("k_rows", [P, 4, COLS])
        cache_k = m.spare[:, 2 * DC * COLS:].rearrange("p (k b n) -> p k b n", k=2, b=2)
        cache_f = sb("cache_f", [P, 2, H_FOX])
        u = sb("u", [P, NT, H_FOX])
        soft = sb("soft", [P, NT, H_FOX])
        logf = sb("logf", [P, NT, H_FOX])
        stat = sb("stat", [P, 6, NT])
        acc = ps("acc", [P, 4, 512])
        acc_k = ps("acc_k", [P, 2, 512])
        turned = ps("turned", [P, 2, 512])
        norm = Norm(m, sem, io["norm_mix"][0], a.v_rows[:, 3, :], a.v_rows[:, 0:2, :], a.v_rows[:, 2, :], stat, acc, high, low)
        x_cleared, x_loaded, consts_loaded = sem("x_cleared"), [sem(f"x_loaded{t}") for t in range(NT)], sem("consts_loaded")
        w_loaded = [sem("w_loaded0"), sem("w_loaded1")]
        w_high_ready, w_low_ready = sem("w_high_ready"), sem("w_low_ready")
        small_loaded, cache_k_loaded = sem("small_loaded", kept=True), sem("cache_k_loaded", kept=True)
        small_high, small_low, rest_set = sem("small_high"), sem("small_low"), sem("rest_set")
        group_ready, group_stored = sem("group_ready"), sem("group_stored")
        k_ready, k_rows_ready, k_turned, kT_stored = sem("k_ready"), sem("k_rows_ready"), sem("k_turned"), sem("kT_stored")
        k_saved = [sem(f"k_saved{b}", kept=True) for b in range(4)]
        v_saved, cache_v_loaded, act_chain = sem("v_saved"), sem("cache_v_loaded", kept=True), sem("act_chain")
        f_ready, u_ready, soft_ready, logf_ready, f_turned, f_used, f_saved = (
            sem("f_ready"), sem("u_ready"), sem("soft_ready"), sem("logf_ready"), sem("f_turned"), sem("f_used"), sem("f_saved"))
        block = ctx.enter_context(nc.Block())
        out_k, out_v = [io["out_sb_k"], io["out_fox_k"]], [io["out_sb_v"], io["out_fox_v"]]
        w_view = io["w_in_ab"].rearrange("(c p) n -> p c n", p=P)

        def unit_done(eng, i):
            if i < 4:
                eng.wait_ge(k_ready, (i + 1) * NT)
            else:
                eng.wait_ge(group_ready, (i - 3) * NT if i < 8 else VG + (i - 7) * 4)

        @block.sync
        def _(sp):
            x_view = io["x_prompt"].rearrange("b (t p) d -> p (b t) d", p=P)
            for t in range(PT):
                sp.dma_start(m.x[:, t, :], x_view[:, t, :]).then_inc(x_loaded[t], 16)
            sp.wait_ge(x_cleared, 1)
            sp.dma_start(m.x[0:SAMPLE, PT, :], io["x_sample"].rearrange("b t d -> (b t) d")).then_inc(x_loaded[PT], 16)
            norm.load(sp)
            for i, (lo, what, kind, pair) in enumerate(UNITS):
                if i >= 2:
                    sp.wait_ge(w_low_ready, i - 1)
                sp.dma_start(w_raw[:, i % 2], w_view[:, :, lo:lo + COLS]).then_inc(w_loaded[i % 2], 16)
                if i == 4:
                    sp.wait_ge(logf_ready, 1)
                    sp.dma_start(io["out_fox_logf"][0].rearrange("b (t p) h -> p (b t) h", p=P), logf[:, 0:PT, :]).then_inc(f_saved, 16)
                    sp.dma_start(io["out_fox_logf"][1].rearrange("b t h -> (b t) h"), logf[0:SAMPLE, PT, :]).then_inc(f_saved, 16)
            for kind in range(2):
                for t in range(NT):
                    sp.wait_ge(group_stored, (2 * kind + 1) * NT + t + 1)
                    sp.dma_start(rows_of(out_v[kind], t), a.v_rows[0:width(t), t, kind * 512:(kind + 1) * 512]).then_inc(v_saved, 16)
            for b in range(4):
                sp.wait_ge(k_saved[b], 16 * KG // 4)
            sp.wait_ge(v_saved, 16 * 2 * NT)
            sp.wait_ge(f_saved, 32)
            sp.wait_ge(cache_v_loaded, 32)

        @block.gpsimd
        def _(pool):
            pool.dma_start(w_forget[:, :, :], w_view[:, :, 6 * 512:6 * 512 + H_FOX]).then_inc(small_loaded, 16)
            pool.dma_start(b_rows[:, :], io["b_forget"].partition_broadcast(P)).then_inc(small_loaded, 16)
            pool.dma_start(cache_f[:, :, :], io["cache_fox_logf"].rearrange("b (j p) h -> p (b j) h", p=P)).then_inc(small_loaded, 16)
            pool.wait_ge(norm.h_turned, 1)
            for kind, cache in enumerate((io["cache_sb_k"], io["cache_fox_k"])):
                pool.dma_start(cache_k[:, kind, :, :], cache.rearrange("b (j p) h d -> p (b j) (h d)", p=P)).then_inc(cache_k_loaded, 16)
            for kind, cache in enumerate((io["cache_sb_v"], io["cache_fox_v"])):
                pool.dma_start(a.cache_v[:, :, kind * 512:(kind + 1) * 512], cache.rearrange("b (j p) h d -> p (b j) (h d)", p=P)).then_inc(cache_v_loaded, 16)
            for g in range(KG):
                i, t = divmod(g, NT)
                _, _, kind, pair = UNITS[i]
                pool.wait_ge(k_rows_ready, g + 1)
                pool.dma_start(rows_of(out_k[kind], t)[:, pair * COLS:(pair + 1) * COLS], k_rows[0:width(t), g % 4, :]).then_inc(k_saved[g % 4], 16)

        @block.tensor
        def _(pe):
            def k_group(g):
                i, t = divmod(g, NT)
                if t == 0:
                    pe.wait_ge(w_low_ready, i + 1)
                if g < NT:
                    pe.wait_ge(norm.low_ready, t + 1)
                if g == NT - 1:
                    pe.wait_ge(rest_set, 1)
                if g >= 2:
                    pe.wait_ge(k_rows_ready, g - 1)
                norm.product(pe, acc_k[:, g % 2, 0:COLS], t, w_high[:, i % 2], w_low[:, i % 2]).then_inc(k_ready, 1)

            def turn_k(g):
                w = width(g % NT)
                pe.wait_ge(k_rows_ready, g + 1)
                if g >= 2:
                    pe.wait_ge(kT_stored, g - 1)
                for h in range(2):
                    last = pe.transpose(turned[:, g % 2, h * P:h * P + w], k_rows[0:w, g % 4, h * P:(h + 1) * P], m.ident[0:w, 0:w])
                last.then_inc(k_turned, 1)

            pe.wait_ge(consts_loaded, 32)
            norm.turn(pe, 0)
            for t in range(1, NT):
                norm.turn(pe, t)
                k_group(t - 1)
                if t >= 3:
                    turn_k(t - 3)
            for g in range(NT - 1, KG):
                k_group(g)
                turn_k(g - 2)
                if g == NT - 1:
                    pe.wait_ge(small_low, 1)
                    for t in range(NT):
                        last = norm.product(pe, acc[:, 0, t * H_FOX:(t + 1) * H_FOX], t, w_forget_high, w_forget_low)
                    last.then_inc(f_ready, 1)
            turn_k(KG - 2)
            turn_k(KG - 1)
            pe.wait_ge(cache_k_loaded, 32)
            for j in range(4):
                kind, kb = divmod(j, 2)
                pe.wait_ge(kT_stored, KG + j - 1)
                for h in range(4):
                    last = pe.transpose(turned[:, j % 2, h * P:(h + 1) * P], cache_k[:, kind, kb, h * P:(h + 1) * P], m.ident[:, :])
                last.then_inc(k_turned, 1)
            pe.wait_ge(kT_stored, KG + 4)
            pe.wait_ge(logf_ready, 1)
            for t in range(PT):
                pe.transpose(turned[0:H_FOX, 0, t * P:(t + 1) * P], logf[:, t, :], m.ident[:, :])
            for kb in range(2):
                pe.transpose(turned[0:H_FOX, 1, kb * P:(kb + 1) * P], cache_f[:, kb, :], m.ident[:, :])
            pe.transpose(turned[0:H_FOX, 1, PAST:LS], logf[0:SAMPLE, PT, :], m.ident[0:SAMPLE, 0:SAMPLE]).then_inc(f_turned, 1)
            for g in range(VG):
                i, t = divmod(g, NT)
                if t == 0:
                    pe.wait_ge(w_low_ready, 4 + i + 1)
                if g == 0:
                    pe.wait_ge(u_ready, 1)
                if g >= 4:
                    pe.wait_ge(group_stored, g - 3)
                norm.product(pe, acc[:, g % 4, 0:COLS], t, w_high[:, i % 2], w_low[:, i % 2]).then_inc(group_ready, 1)
            for j in range(QG):
                i, h, n = 8 + j // 4, (j // 2) % 2, j % 2
                g = VG + j
                if j % 4 == 0:
                    pe.wait_ge(w_low_ready, i + 1)
                pe.wait_ge(group_stored, g - 3)
                for c in range(DC):
                    for k, (w, x) in enumerate(((w_high, high), (w_low, high), (w_high, low))):
                        last = pe.matmul(acc[:, g % 4, 0:HALF_T], w[:, i % 2, c, h * P:(h + 1) * P],
                                         x[:, c * T + n * HALF_T:c * T + (n + 1) * HALF_T], start=(c == 0 and k == 0), stop=(c == DC - 1 and k == 2))
                last.then_inc(group_ready, 1)

        @block.scalar
        def _(act):
            act.dma_start(m.consts[:, :], io["consts"]).then_inc(consts_loaded, 16)
            act.dma_start(m.head_select[:, :], io["head_select"]).then_inc(consts_loaded, 16)
            act.preload_act_table_set("sqrt_and_others")
            for t in range(NT):
                act.wait_ge(x_loaded[t], 16)
                norm.square(act, t)
            norm.root(act, 0)

            def cut_high(i):
                act.wait_ge(w_loaded[i % 2], 16 * (i // 2 + 1))
                if i >= 2:
                    unit_done(act, i - 2)
                act.activation(w_high[:, i % 2], w_raw[:, i % 2], ACT.Copy).then_inc(w_high_ready, 1)

            cut_high(0)
            for t in range(NT):
                norm.store_high(act, t)
            cut_high(1)
            act.wait_ge(small_loaded, 48)
            act.activation(w_forget_high[:, :, :], w_forget[:, :, :], ACT.Copy).then_inc(small_high, 1)
            cut_high(2)
            act.wait_ge(u_ready, 1)
            act.activation(soft[:, :, :], u[:, :, :], ACT.Abs).then_inc(act_chain, 1)
            act.wait_ge(act_chain, 1)
            act.activation(soft[:, :, :], soft[:, :, :], ACT.Exp, scale=-1.0).then_inc(act_chain, 1)
            act.wait_ge(act_chain, 2)
            act.activation(soft[:, :, :], soft[:, :, :], ACT.Ln, bias=1.0).then_inc(soft_ready, 1)
            cut_high(3)
            cut_high(4)
            for g in range(VG):
                i, t = divmod(g, NT)
                w = width(t)
                if t == 0:
                    cut_high(5 + i)
                lo = UNITS[4 + i][2] * 512 + UNITS[4 + i][3] * COLS
                act.wait_ge(group_ready, g + 1)
                act.activation(a.v_rows[0:w, t, lo:lo + COLS], acc[0:w, g % 4, 0:COLS], ACT.Copy).then_inc(group_stored, 1)
            for j in range(QG):
                g, n = VG + j, j % 2
                _, _, kind, pair = UNITS[8 + j // 4]
                if j % 4 == 0 and j < 12:
                    cut_high(9 + j // 4)
                head = kind * 4 + pair * 2 + (j // 2) % 2
                act.wait_ge(group_ready, g + 1)
                act.activation(a.qT[:, head, n * HALF_T:(n + 1) * HALF_T], acc[:, g % 4, 0:HALF_T], ACT.Copy, scale=SCALE).then_inc(group_stored, 1)

        @block.vector
        def _(dve):
            dve.memset(m.x[:, PT, :], 0.0).then_inc(x_cleared, 1)
            dve.memset(m.ones[:, :], 1.0)
            dve.memset(m.ones16[:, :], 1.0)
            norm.clear_pad(dve)
            dve.wait_ge(consts_loaded, 32)
            dve.tensor_copy(m.masks[:, :], m.consts[:, 0:4 * P])
            dve.tensor_copy(m.before[:, :], m.consts[:, C_BEFORE:C_BEFORE + P]).then_inc(rest_set, 1)

            def cut_low(i):
                dve.wait_ge(w_high_ready, i + 1)
                dve.tensor_tensor(w_low[:, i % 2], w_raw[:, i % 2], w_high[:, i % 2].bitcast(F32), ALU.subtract).then_inc(w_low_ready, 1)

            def store_k(g):
                w = width(g % NT)
                dve.wait_ge(k_ready, g + 1)
                if g >= 4:
                    dve.wait_ge(k_turned, g - 3)
                    dve.wait_ge(k_saved[g % 4], 16 * (g // 4))
                dve.tensor_copy(k_rows[0:w, g % 4, :], acc_k[0:w, g % 2, 0:COLS]).then_inc(k_rows_ready, 1)

            def store_kT(g):
                i, t = divmod(g, NT)
                _, _, kind, pair = UNITS[i]
                heads = slice(kind * 4 + pair * 2, kind * 4 + pair * 2 + 2)
                dve.wait_ge(k_turned, g + 1)
                dst = a.kT[:, heads, t * P:(t + 1) * P] if t < PT else a.kT_sample[:, heads, PAST:LS]
                dve.tensor_copy(dst, turned[:, g % 2, 0:COLS].rearrange("p (h n) -> p h n", h=2)[:, :, 0:width(t)]).then_inc(kT_stored, 1)

            norm.inverse_root(dve, 0)
            norm.scale(dve, 0)
            cut_low(0)
            for t in range(1, NT):
                norm.scale(dve, t)
                norm.store_low(dve, t - 1)
                if t >= 2:
                    store_k(t - 2)
            norm.store_low(dve, NT - 1)
            cut_low(1)
            dve.wait_ge(small_high, 1)
            dve.tensor_tensor(w_forget_low[:, :, :], w_forget[:, :, :], w_forget_high[:, :, :].bitcast(F32), ALU.subtract).then_inc(small_low, 1)
            for g in range(NT - 2, KG):
                store_k(g)
                store_kT(g - 3)
                if g == NT:
                    dve.wait_ge(f_ready, 1)
                    dve.tensor_tensor(u[:, :, :], acc[:, 0, 0:NT * H_FOX].rearrange("p (t h) -> p t h", t=NT),
                                      b_rows[:, :].unsqueeze(1).broadcast_to([P, NT, H_FOX]), ALU.add).then_inc(u_ready, 1)
                if g == NT + 1:
                    dve.wait_ge(soft_ready, 1)
                    dve.scalar_tensor_tensor(out=logf[:, :, :], in0=u[:, :, :], scalar=0.0, in1=soft[:, :, :], op0=ALU.min, op1=ALU.subtract).then_inc(logf_ready, 1)
                if g % NT == 0:
                    cut_low(g // NT + 1)
            for g in range(KG - 3, KG):
                store_kT(g)
            for j in range(4):
                kind, kb = divmod(j, 2)
                dve.wait_ge(k_turned, KG + j + 1)
                dve.tensor_copy(a.kT_sample[:, kind * 4:kind * 4 + 4, kb * P:(kb + 1) * P],
                                turned[:, j % 2, :].rearrange("p (h n) -> p h n", h=4)).then_inc(kT_stored, 1)
            dve.wait_ge(f_turned, 1)
            dve.tensor_tensor_scan(a.forget[:, :], m.ones[0:4, :], turned[0:4, 0, :], 0.0, ALU.mult, ALU.add)
            dve.tensor_tensor_scan(a.forget_sample[:, :], m.ones[0:4, 0:LS], turned[0:4, 1, 0:LS], 0.0, ALU.mult, ALU.add)
            for i in range(5, 12):
                cut_low(i)


class Unit:

    def __init__(self, heads, t, stick=False):
        self.heads, self.t, self.sample, self.stick = heads, t, t == PT, stick
        self.n = LS if self.sample else (t + 1) * P
        self.blocks = 3 if self.sample else t + 1

    def rows_in(self, kb):
        return SAMPLE if self.sample and kb == 2 else P


def score_products(pe, m, a, unit, out, kv, mask, forget):
    for i, h in enumerate(unit.heads):
        q = a.qT[:, h, cols(unit.t)]
        k = a.kT_sample[:, kv(h), :] if unit.sample else a.kT[:, kv(h), :]
        rows = slice(32 * i, 32 * i + 32) if unit.sample else slice(0, P)
        nq = SAMPLE if unit.sample else P
        edge = PAST if unit.sample else unit.t * P
        spans = [(0, unit.n)] if mask is None else ([(0, edge)] if edge else []) + [(edge, unit.n)]
        for lo, hi in spans:
            masked = mask is None or lo == edge
            products = [(q, k[:, lo:hi])]
            if forget:
                f = a.forget_sample if unit.sample else a.forget
                products.append((m.head_select[:, (h - H_SB) * P:(h - H_SB) * P + nq], f[:, lo:hi]))
            if mask is not None and masked:
                products.append((m.ident16[0:nq, 0:nq], mask[0:nq, 0:hi - lo]))
            if mask is None:
                chosen = a.unchosen[unit.t]
                products.append((m.ident16[0:nq, 0:nq], chosen[0:nq, lo:hi]))
            for j, (left, right) in enumerate(products):
                last = pe.matmul(out[rows, lo:hi], left, right, start=(j == 0), stop=(j == len(products) - 1))
    return last


def value_products(pe, a, unit, out, pT, v_head):
    for i, h in enumerate(unit.heads):
        q = slice(32 * i, 32 * i + 32) if unit.sample else slice(0, P)
        vc = slice(v_head(h) * P, (v_head(h) + 1) * P)
        for kb in range(unit.blocks):
            n = unit.rows_in(kb)
            if unit.sample:
                v = a.cache_v[:, kb, vc] if kb < 2 else a.v_rows[0:SAMPLE, PT, vc]
            else:
                v = a.v_rows[:, kb, vc]
            last = pe.matmul(out[:, q], v, pT[0:n, kb, q], start=(kb == 0), stop=(kb == unit.blocks - 1))
    return last


def mixer_stage(nc, m, a, r, name, steps, kv, v_head, masks, forget, w_dram, g_dram, split):
    with ExitStack() as ctx:
        sb, ps, sem = tools(nc, ctx, name)
        order = [units[0].t for units, last in steps if last]
        last_step = [i for i, (_, last) in enumerate(steps) if last]
        base = []
        for end in last_step:
            base.append(max(end, base[-1] + 4) if base else end)
        units = [u for us, _ in steps for u in us]
        first_unit = [sum(len(us) for us, _ in steps[:i]) for i in range(len(steps))]
        kind_no = [sum(v.stick == u.stick for v in units[:i]) for i, u in enumerate(units)]
        sticks = any(u.stick for u in units)
        softs = sum(not u.stick for u in units)
        soft_banks = 1 if sticks else 3
        on_vector = set() if sticks else set(range(0, len(units), 2))
        PART = F32R if split else F32
        prob = sb("prob", [P, 4, 512])
        work = sb("work", [P, 2, 512]) if sticks else None
        pT = sb("pT", [P, 3, 4, P])
        row_stat = sb("row_stat", [P, 3, softs])
        oT = sb("oT", [P, 2, DC, P], PART)
        oT_rest = sb("oT_rest", [P, 2, DC, P], PART) if split else None
        g = sb("g", [P, D])
        h = sb("h", [P, 2, D])
        squares = sb("squares", [P, D])
        hT = sb("hT", [P, DC, P])
        stat = sb("stat", [P, 8, NT])
        w_route = sb("w_route", [P, DC, NG + NE])
        scores_soft = ps("scores_soft", [P, soft_banks, 512])
        scores_stick = ps("scores_stick", [P, 2, 512]) if sticks else None
        turned = ps("turned", [P, 2, 512])
        mixed = ps("mixed", [P, 2, 512])
        acc = ps("acc", [P, 512])
        scores_ready = {True: sem("stick_scores"), False: sem("soft_scores")}
        scores_used = {True: sem("stick_scores_used"), False: sem("soft_scores_used")}
        prob_ready = {True: sem("stick_prob"), False: sem("soft_prob")}
        prob_on_dve = sem("prob_on_dve")
        soft_ready, sum_ready, suffix_ready = sem("soft_ready"), sem("sum_ready"), sem("suffix_ready")
        exponent_ready, act_chain = sem("exponent_ready"), sem("act_chain")
        neg_max_ready, exp_ready, inverse_ready = sem("neg_max_ready"), sem("exp_ready"), sem("inverse_ready")
        turned_ready, turned_stored, mixed_ready, mixed_stored = (
            sem("turned_ready"), sem("turned_stored"), sem("mixed_ready"), sem("mixed_stored"))
        rest_stored, cleared = sem("rest_stored"), sem("cleared")
        w_loaded, small_loaded = [sem("w_loaded0"), sem("w_loaded1")], sem("small_loaded")
        w_rounded, w_split, first_loaded = sem("w_rounded"), sem("w_split"), sem("first_loaded")
        group_ready, added, squared, mean_ready, root_ready, newton = (
            sem("group_ready"), sem("added"), sem("squared"), sem("mean_ready"), sem("root_ready"), sem("newton"))
        h_ready, logits_ready, logits_stored = sem("h_ready"), sem("logits_ready"), sem("logits_stored")
        h_saved = [sem("h_saved0"), sem("h_saved1")]
        if split:
            w_raw = m.spare[:, 0:2 * DC * 256].rearrange("p (b c n) -> p b c n", b=2, c=DC)
            w_high = sb("w_high", [P, 4, DC, 256], F32R)
            w_low = sb("w_low", [P, 4, DC, 256], F32R)
        else:
            w_out = sb("w_out", [P, DC, D])

        turns = {}
        END = base[-1] + 10
        for s in range(END):
            for o, end in enumerate(base):
                if s == end + 9:
                    turns["norm", o, 0] = len(turns)
                    turns["norm", o, 1] = len(turns)
            if 1 <= s <= len(steps):
                for i in range(first_unit[s - 1], first_unit[s - 1] + len(steps[s - 1][0])):
                    turns["unit", i] = len(turns)
        block = ctx.enter_context(nc.Block())

        def units_of(s):
            return [(first_unit[s] + j, u) for j, u in enumerate(steps[s][0])] if 0 <= s < len(steps) else []

        def scores_of(i):
            u = units[i]
            return scores_stick[:, kind_no[i] % 2] if u.stick else scores_soft[:, kind_no[i] % soft_banks]

        def tiles_at(s, lag):
            return [(o, order[o]) for o, end in enumerate(base) if s == end + lag]

        @block.sync
        def _(sp):
            sp.dma_start(w_route[:, :, 0:NG], r.w_group.rearrange("(c p) g -> p c g", p=P)).then_inc(small_loaded, 16)
            sp.dma_start(w_route[:, :, NG:], r.w_router.rearrange("(c p) g e -> p c (g e)", p=P)).then_inc(small_loaded, 16)
            sp.dma_start(g[:, :], g_dram.partition_broadcast(P)).then_inc(small_loaded, 16)
            w_view = w_dram.rearrange("(c p) n -> p c n", p=P)
            if split:
                for q in range(4):
                    if q >= 2:
                        sp.wait_ge(w_split, q - 1)
                    sp.dma_start(w_raw[:, q % 2], w_view[:, :, q * 256:(q + 1) * 256]).then_inc(w_loaded[q % 2], 16)
            else:
                for n in range(2):
                    sp.dma_start(w_out[:, :, n * 512:(n + 1) * 512], w_view[:, :, n * 512:(n + 1) * 512]).then_inc(w_loaded[n], 16)
            if split:
                sp.wait_ge(w_split, 4)
            gate, up, down = r.first_weights
            for part, w in ((m.first_hidden[:, :, 0:FE], gate), (m.first_hidden[:, :, FE:], up), (m.first_down, down)):
                sp.dma_start(part, w.rearrange("(c p) n -> p c n", p=P)).then_inc(first_loaded, 16)
            for o, t in enumerate(order):
                w = width(t)
                sp.wait_ge(h_ready, o + 1)
                sp.dma_start(r.h_dram[t * P:t * P + w, :], h[0:w, o % 2, :]).then_inc(h_saved[o % 2], 16)
            sp.wait_ge(h_saved[0], 48)
            sp.wait_ge(h_saved[1], 32)
            sp.wait_ge(first_loaded, 48)

        @block.tensor
        def _(pe):
            def turn(i):
                pos, u = turns["unit", i], units[i]
                if i in on_vector:
                    pe.wait_ge(prob_on_dve, i // 2 + 1)
                else:
                    pe.wait_ge(prob_ready[u.stick], i // 2 + 1)
                if pos >= 2:
                    pe.wait_ge(turned_stored, pos - 1)
                for kb in range(u.blocks):
                    n = u.rows_in(kb)
                    last = pe.transpose(turned[0:n, pos % 2, kb * P:(kb + 1) * P], prob[:, i % 4, kb * P:kb * P + n], m.ident[:, :])
                last.then_inc(turned_ready, 1)

            def mix(i):
                pe.wait_ge(turned_stored, turns["unit", i] + 1)
                if i >= 2:
                    pe.wait_ge(mixed_stored, i - 1)
                    if split:
                        pe.wait_ge(rest_stored, i - 1)
                value_products(pe, a, units[i], mixed[:, i % 2, 0:P], pT[:, i % 3], v_head).then_inc(mixed_ready, 1)

            def output_part(o, q):
                n, first = divmod(q, 2)
                w = P if split else width(order[o])
                if q == 0:
                    done = first_unit[last_step[o]] + len(steps[last_step[o]][0])
                    pe.wait_ge(mixed_stored, done)
                    if split:
                        pe.wait_ge(rest_stored, done)
                if split and o == 0 and first == 0:
                    pe.wait_ge(w_split, 2 * n + 2)
                if o == 0 and not split and first == 0:
                    pe.wait_ge(w_loaded[n], 16)
                if first == 0 and 2 * o + n:
                    pe.wait_ge(added, 2 * o + n)
                if first == 0 and routed[0]:
                    pe.wait_ge(logits_stored, routed[0])
                for c in range(4 * first, 4 * first + 4):
                    if not split:
                        last = pe.matmul(acc[0:w, :], oT[:, o % 2, c, 0:w], w_out[:, c, n * 512:(n + 1) * 512], start=(c == 0), stop=(c == DC - 1))
                        continue
                    for half in range(2):
                        out, k = acc[:, half * 256:(half + 1) * 256], 2 * n + half
                        for j, (left, right) in enumerate(((oT, w_high), (oT, w_low), (oT_rest, w_high))):
                            last = pe.matmul(out, left[:, o % 2, c, :], right[:, k, c, :], start=(c == 0 and j == 0 and half == 0),
                                             stop=(c == DC - 1 and j == 2), skip_group_check=True)
                if first:
                    last.then_inc(group_ready, 1)

            def turn_norm(o, t):
                w = width(t)
                pe.wait_ge(h_ready, o + 1)
                for half in range(2):
                    pos = turns["norm", o, half]
                    pe.wait_ge(turned_stored, pos - 1)
                    for c in range(4):
                        last = pe.transpose(turned[:, pos % 2, c * P:c * P + w], h[0:w, o % 2, (4 * half + c) * P:(4 * half + c + 1) * P], m.ident[0:w, 0:w])
                    last.then_inc(turned_ready, 1)

            def route(o, t):
                w = width(t)
                if o == 0:
                    pe.wait_ge(small_loaded, 48)
                pe.wait_ge(added, min(2 * o + 3, 2 * NT))
                pe.wait_ge(turned_stored, turns["norm", o, 1] + 1)
                for c in range(DC):
                    last = pe.matmul(acc[0:w, 0:NG + NE], hT[:, c, 0:w], w_route[:, c, :], start=(c == 0), stop=(c == DC - 1))
                last.then_inc(logits_ready, 1)
                routed[0] = o + 1

            routed = [0]
            for s in range(END):
                for o, t in tiles_at(s, 9):
                    turn_norm(o, t)
                for i, u in units_of(s):
                    k, banks = kind_no[i], 2 if u.stick else soft_banks
                    if k >= banks:
                        pe.wait_ge(scores_used[u.stick], k - banks + 1)
                    score_products(pe, m, a, u, scores_of(i), kv, masks[u.stick], forget and not u.stick).then_inc(scores_ready[u.stick], 1)
                for o, t in tiles_at(s, 9):
                    route(o, t)
                for q in range(4):
                    for o, _ in tiles_at(s, 3 + q):
                        output_part(o, q)
                for i, _ in units_of(s - 1):
                    turn(i)
                for i, _ in units_of(s - 2):
                    mix(i)

        @block.scalar
        def _(act):
            act.preload_act_table_set("natural_log_exp_and_others")
            chained = 0
            for s in range(END + 1):
                for i, u in units_of(s):
                    if not u.stick:
                        continue
                    k, buf = kind_no[i], prob[:, i % 4, 0:u.n]
                    act.wait_ge(scores_ready[True], k + 1)
                    if i >= 4:
                        act.wait_ge(turned_ready, turns["unit", i - 4] + 1)
                    act.activation(buf, scores_of(i)[:, 0:u.n], ACT.Abs).then_inc(act_chain, 1)
                    act.wait_ge(act_chain, chained + 1)
                    act.activation(buf, buf, ACT.Exp, scale=-1.0).then_inc(act_chain, 1)
                    act.wait_ge(act_chain, chained + 2)
                    act.activation(buf, buf, ACT.Ln, bias=1.0).then_inc(soft_ready, 1)
                    chained += 2
                for i, u in units_of(s):
                    if u.stick:
                        continue
                    k = kind_no[i]
                    act.wait_ge(neg_max_ready, k + 1)
                    if i >= 4:
                        act.wait_ge(turned_ready, turns["unit", i - 4] + 1)
                    act.activation(prob[:, i % 4, 0:u.n], scores_of(i)[:, 0:u.n], ACT.Exp, bias=row_stat[:, 0, k:k + 1],
                                   accum_out=row_stat[:, 1, k:k + 1]).then_inc(exp_ready, 1)
                for i, u in units_of(s):
                    if u.stick:
                        k = kind_no[i]
                        act.wait_ge(exponent_ready, k + 1)
                        act.activation(prob[:, i % 4, 0:u.n], work[:, k % 2, 0:u.n], ACT.Exp).then_inc(prob_ready[True], 1)
                for o, t in tiles_at(s, 9):
                    w = width(t)
                    act.wait_ge(logits_ready, o + 1)
                    act.activation(r.logits[0:w, t, :], acc[0:w, 0:NG + NE], ACT.Copy).then_inc(logits_stored, 1)
                for i, u in units_of(s - 2):
                    o = sum(end < s - 2 for end in last_step)
                    h0, h1 = u.heads[0], u.heads[-1] + 1
                    act.wait_ge(mixed_ready, i + 1)
                    if i == 0:
                        act.wait_ge(cleared, 1)
                    if o >= 2:
                        act.wait_ge(group_ready, 2 * (o - 1))
                    act.activation(oT[:, o % 2, h0:h1, 0:width(u.t)], mixed[:, i % 2, 0:P].rearrange("p (h n) -> p h n", h=h1 - h0), ACT.Copy).then_inc(mixed_stored, 1)
                if split and 1 <= s < 5:
                    q = s - 1
                    act.wait_ge(w_loaded[q % 2], 16 * (q // 2 + 1))
                    act.activation(w_high[:, q], w_raw[:, q % 2], ACT.Copy).then_inc(w_rounded, 1)
                for o, t in tiles_at(s, 7):
                    act.wait_ge(added, 2 * o + 2)
                    if o:
                        act.wait_ge(squared, o)
                    act.activation(squares[:, :], m.x[:, t, :], ACT.Square, accum_out=stat[:, 0, o:o + 1]).then_inc(squared, 1)
                    act.wait_ge(mean_ready, o + 1)
                    act.activation(stat[:, 2, o:o + 1], stat[:, 1, o:o + 1], ACT.Ln).then_inc(act_chain, 1)
                    chained += 1
                    act.wait_ge(act_chain, chained)
                    act.activation(stat[:, 3, o:o + 1], stat[:, 2, o:o + 1], ACT.Exp, scale=-0.5).then_inc(root_ready, 1)

        @block.gpsimd
        def _(pool):
            for i, u in enumerate(units):
                if not u.stick and i not in on_vector:
                    k = kind_no[i]
                    p = prob[:, i % 4, 0:u.n]
                    pool.wait_ge(inverse_ready, k + 1)
                    pool.tensor_scalar(p, p, row_stat[:, 2, k:k + 1], None, ALU.mult).then_inc(prob_ready[False], 1)

        @block.vector
        def _(dve):
            if split:
                dve.memset(oT[:, 0].bitcast(F32), 0.0)
                dve.memset(oT_rest[:, 0].bitcast(F32), 0.0)
            dve.memset(r.logits[:, PT, :], 0.0).then_inc(cleared, 1)
            dve.wait_ge(cleared, 1)

            def store_turned(i):
                pos, u = turns["unit", i], units[i]
                dve.wait_ge(turned_ready, pos + 1)
                if i >= 3:
                    dve.wait_ge(mixed_ready, i - 2)
                full = 2 if u.sample else u.blocks
                done = dve.tensor_copy(pT[:, i % 3, 0:full, :], turned[:, pos % 2, 0:full * P].rearrange("p (k n) -> p k n", k=full))
                if u.sample:
                    done = dve.tensor_copy(pT[0:SAMPLE, i % 3, 2, :], turned[0:SAMPLE, pos % 2, 2 * P:3 * P])
                done.then_inc(turned_stored, 1)

            refined = 0
            for s in range(END):
                for o, t in tiles_at(s, 9):
                    w = width(t)
                    for half in range(2):
                        pos = turns["norm", o, half]
                        dve.wait_ge(turned_ready, pos + 1)
                        if o and half == 0:
                            dve.wait_ge(logits_ready, o)
                        dve.tensor_copy(hT[:, 4 * half:4 * half + 4, 0:w],
                                        turned[:, pos % 2, :].rearrange("p (c n) -> p c n", c=4)[:, :, 0:w]).then_inc(turned_stored, 1)
                for i, u in units_of(s):
                    if not u.stick:
                        k = kind_no[i]
                        dve.wait_ge(scores_ready[False], k + 1)
                        dve.tensor_reduce(row_stat[:, 0, k:k + 1], scores_of(i)[:, 0:u.n], AX.X, ALU.max, negate=True).then_inc(neg_max_ready, 1)
                for i, u in units_of(s):
                    if not u.stick:
                        continue
                    k = kind_no[i]
                    z, buf, out = scores_of(i)[:, 0:u.n], prob[:, i % 4, 0:u.n], work[:, k % 2, 0:u.n]
                    dve.wait_ge(soft_ready, k + 1)
                    dve.scalar_tensor_tensor(out=buf, in0=z, scalar=0.0, in1=buf, op0=ALU.max, op1=ALU.add).then_inc(sum_ready, 1)
                    dve.wait_ge(sum_ready, k + 1)
                    if k >= 2:
                        dve.wait_ge(prob_ready[True], k - 1)
                    dve.tensor_tensor_scan(out[:, ::-1], m.ones[:, 0:u.n], buf[:, ::-1], 0.0, ALU.mult, ALU.add).then_inc(suffix_ready, 1)
                    dve.wait_ge(suffix_ready, k + 1)
                    dve.tensor_tensor(out, z, out, ALU.subtract).then_inc(exponent_ready, 1)
                    dve.wait_ge(exponent_ready, k + 1)
                    dve.sem_inc(scores_used[True], 1)
                for i, u in units_of(s):
                    if not u.stick:
                        k = kind_no[i]
                        dve.wait_ge(exp_ready, k + 1)
                        dve.sem_inc(scores_used[False], 1)
                        dve.reciprocal(row_stat[:, 2, k:k + 1], row_stat[:, 1, k:k + 1]).then_inc(inverse_ready, 1)
                        if i in on_vector:
                            p = prob[:, i % 4, 0:u.n]
                            dve.wait_ge(inverse_ready, k + 1)
                            dve.tensor_scalar(p, p, row_stat[:, 2, k:k + 1], None, ALU.mult).then_inc(prob_on_dve, 1)
                for q in (1, 3):
                    for o, t in tiles_at(s, 3 + q):
                        n, w = q // 2, width(t)
                        x = m.x[0:w, t, n * 512:(n + 1) * 512]
                        dve.wait_ge(group_ready, 2 * o + n + 1)
                        dve.tensor_tensor(x, acc[0:w, :], x, ALU.add).then_inc(added, 1)
                for i, _ in units_of(s - 1):
                    store_turned(i)
                if split:
                    for i, u in units_of(s - 2):
                        o = sum(end < s - 2 for end in last_step)
                        h0, h1 = u.heads[0], u.heads[-1] + 1
                        w = width(u.t)
                        dve.wait_ge(mixed_stored, i + 1)
                        dve.tensor_tensor(oT_rest[:, o % 2, h0:h1, 0:w], mixed[:, i % 2, 0:P].rearrange("p (h n) -> p h n", h=h1 - h0),
                                          oT[:, o % 2, h0:h1, 0:w].bitcast(F32), ALU.subtract).then_inc(rest_stored, 1)
                if split and 1 <= s < 5:
                    q = s - 1
                    dve.wait_ge(w_rounded, q + 1)
                    dve.tensor_tensor(w_low[:, q], w_raw[:, q % 2], w_high[:, q].bitcast(F32), ALU.subtract).then_inc(w_split, 1)
                for o, t in tiles_at(s, 7):
                    dve.wait_ge(squared, o + 1)
                    v, y, tmp = stat[:, 1, o:o + 1], stat[:, 3, o:o + 1], stat[:, 4, o:o + 1]
                    dve.tensor_scalar(v, stat[:, 0, o:o + 1], 1.0 / D, EPS, ALU.mult, ALU.add).then_inc(mean_ready, 1)
                    dve.wait_ge(root_ready, o + 1)
                    dve.scalar_tensor_tensor(out=tmp, in0=y, scalar=v, in1=y, op0=ALU.mult, op1=ALU.mult).then_inc(newton, 1)
                    dve.wait_ge(newton, refined + 1)
                    dve.tensor_scalar(tmp, tmp, -0.5, 1.5, ALU.mult, ALU.add).then_inc(newton, 1)
                    dve.wait_ge(newton, refined + 2)
                    dve.tensor_tensor(stat[:, 5, o:o + 1], y, tmp, ALU.mult).then_inc(newton, 1)
                    dve.wait_ge(newton, refined + 3)
                    refined += 3
                    if o == 0:
                        dve.wait_ge(small_loaded, 48)
                    if o >= 2:
                        dve.wait_ge(h_saved[o % 2], 16 * (o // 2))
                        dve.wait_ge(turned_ready, turns["norm", o - 2, 1] + 1)
                    dve.scalar_tensor_tensor(out=h[:, o % 2, :], in0=m.x[:, t, :], scalar=stat[:, 5, o:o + 1], in1=g[:, :],
                                             op0=ALU.mult, op1=ALU.mult).then_inc(h_ready, 1)


class Router:

    def __init__(self, m, r, sb, sem, place):
        self.m, self.r, self.place = m, r, place
        self.col = sb("col", [P, 14, NT])
        self.quad = sb("quad", [P, 10, NT, NG])
        self.wide = sb("wide", [P, 2, NT, NE])
        self.sums = sb("sums", [P, 2, NT])
        self.chosen = sb("chosen", [P, NT, NE])
        self.chosen16 = sb("chosen16", [P, NT, NE], BF16)
        self.chosen_ready, self.place_ready = sem("chosen_ready"), sem("place_ready")
        self.chain_sem, self.for_act, self.from_act = sem("chain"), sem("for_act"), sem("from_act")

    def on_tensor(self, pe):
        m, place, chosen16, chosen_ready, place_ready = self.m, self.place, self.chosen16, self.chosen_ready, self.place_ready
        pe.wait_ge(chosen_ready, 1)
        for t in range(NT + 1):
            for s in range(min(t, PT) + 1):
                left = m.before[:, :] if s == t else m.ones16[:, :]
                last = pe.matmul(place[:, t, :], left, chosen16[:, s, :], start=(s == 0), stop=(s == min(t, PT)))
        last.then_inc(place_ready, 1)

    def on_scalar(self, act):
        col, quad, for_act, from_act = self.col, self.quad, self.for_act, self.from_act
        act.wait_ge(for_act, 1)
        act.activation(quad[:, 1], quad[:, 0], ACT.Exp).then_inc(from_act, 1)
        act.wait_ge(for_act, 2)
        act.activation(col[:, 5, :], col[:, 4, :], ACT.Exp).then_inc(from_act, 1)

    def on_vector(self, dve):
        m, r, place, logits, col, quad, wide, sums = self.m, self.r, self.place, self.r.logits, self.col, self.quad, self.wide, self.sums
        chosen, chosen16, chosen_ready, place_ready = self.chosen, self.chosen16, self.chosen_ready, self.place_ready
        for_act, from_act = self.for_act, self.from_act
        step = Chain(dve, self.chain_sem)

        def over(x, n):
            return x.unsqueeze(2).broadcast_to([P, NT, n])

        first = m.consts[:, C_FIRST:C_FIRST + 4].unsqueeze(1).broadcast_to([P, NT, 4])

        def first_max(out, best, values, tmp):
            step(dve.tensor_tensor(tmp, values, over(best, 4), ALU.is_equal))
            step.wait()
            step(dve.tensor_tensor(tmp, tmp, first, ALU.mult))
            step.wait()
            step(dve.tensor_reduce(col[:, 13, :], tmp, AX.X, ALU.max))
            step.wait()
            step(dve.tensor_tensor(out, tmp, over(col[:, 13, :], 4), ALU.is_equal))
            step.wait()

        groups = logits[:, :, 0:NG]
        step(dve.tensor_reduce(col[:, 0, :], groups, AX.X, ALU.max))
        step.wait()
        dve.tensor_tensor(quad[:, 0], groups, over(col[:, 0, :], 4), ALU.subtract).then_inc(for_act, 1)
        first_max(quad[:, 2], col[:, 0, :], groups, quad[:, 3])
        experts = logits[:, :, NG:].rearrange("p t (g e) -> p t g e", g=NG)
        group_of = quad[:, 2].unsqueeze(3).broadcast_to([P, NT, NG, EPG])
        wide4 = wide[:, 0].rearrange("p t (g e) -> p t g e", g=NG)
        step(dve.tensor_tensor(wide4, experts, group_of, ALU.mult))
        step.wait()
        step(dve.tensor_reduce(quad[:, 4], wide[:, 0].rearrange("p t (g e) -> p t e g", g=NG), AX.X, ALU.add))
        step.wait()
        step(dve.tensor_reduce(col[:, 1, :], quad[:, 4], AX.X, ALU.max))
        step.wait()
        first_max(quad[:, 5], col[:, 1, :], quad[:, 4], quad[:, 3])
        step(dve.tensor_scalar(quad[:, 7], quad[:, 5], -1.0, 1.0, ALU.mult, ALU.add))
        step.wait()
        step(dve.tensor_tensor(quad[:, 7], quad[:, 7], quad[:, 4], ALU.mult))
        step.wait()
        step(dve.scalar_tensor_tensor(out=quad[:, 6], in0=quad[:, 5], scalar=TAKEN, in1=quad[:, 7], op0=ALU.mult, op1=ALU.add))
        step.wait()
        step(dve.tensor_reduce(col[:, 2, :], quad[:, 6], AX.X, ALU.max))
        step.wait()
        first_max(quad[:, 8], col[:, 2, :], quad[:, 6], quad[:, 3])
        dve.tensor_tensor(col[:, 4, :], col[:, 2, :], col[:, 1, :], ALU.subtract).then_inc(for_act, 1)
        step(dve.tensor_tensor(quad[:, 9], quad[:, 2], over(m.consts[:, C_VALID:C_VALID + NT], NG), ALU.mult))
        step.wait()
        group_of = quad[:, 9].unsqueeze(3).broadcast_to([P, NT, NG, EPG])
        for j, q in enumerate((5, 8)):
            step(dve.tensor_tensor(r.pick[:, j].rearrange("p t (g e) -> p t g e", g=NG), group_of,
                                   quad[:, q].unsqueeze(2).broadcast_to([P, NT, NG, EPG]), ALU.mult))
        step.wait()
        step(dve.tensor_tensor(chosen[:, :, :], r.pick[:, 0], r.pick[:, 1], ALU.add))
        step.wait()
        dve.tensor_copy(chosen16[:, :, :], chosen[:, :, :]).then_inc(chosen_ready, 1)
        dve.wait_ge(from_act, 2)
        step(dve.tensor_reduce(col[:, 3, :], quad[:, 1], AX.X, ALU.add))
        step(dve.tensor_scalar(col[:, 6, :], col[:, 5, :], 1.0, None, ALU.add))
        step.wait()
        step(dve.tensor_tensor(col[:, 7, :], col[:, 3, :], col[:, 6, :], ALU.mult))
        step.wait()
        step(dve.reciprocal(r.gate[:, 0, :], col[:, 7, :]))
        step.wait()
        step(dve.tensor_tensor(r.gate[:, 1, :], r.gate[:, 0, :], col[:, 5, :], ALU.mult))
        experts = m.consts[:, C_EXPERT:C_EXPERT + NE]
        step(dve.tensor_tensor(wide[:, :, :, :], r.pick[:, :, :, :], experts.unsqueeze(1).unsqueeze(1).broadcast_to([P, 2, NT, NE]), ALU.mult))
        step.wait()
        step(dve.tensor_reduce(sums[:, :, :], wide[:, :, :, :], AX.X, ALU.add))
        step.wait()
        step(dve.tensor_scalar(r.expert_row[:, :, :], sums[:, :, :], float(P), None, ALU.mult))
        dve.wait_ge(place_ready, 1)
        step(dve.tensor_tensor(wide[:, :, :, :], r.pick[:, :, :, :], place[:, 0:NT, :].unsqueeze(1).broadcast_to([P, 2, NT, NE]), ALU.mult))
        step(dve.tensor_reduce(col[:, 10, 0:1], place[:, NT, :], AX.X, ALU.max))
        step.wait()
        step(dve.tensor_reduce(r.place[:, :, :], wide[:, :, :, :], AX.X, ALU.add))
        step(dve.tensor_copy(r.most[0:1, 0:1], col[0:1, 10, 0:1]))
        step.wait()


def expert_stage(nc, m, r, name, layer, io):
    with ExitStack() as ctx:
        sb, ps, sem = tools(nc, ctx, name)
        PICKS = 2 * NT
        take = sb("take", [P, PICKS, P])
        value = sb("value", [P, PICKS, NE])
        slots = sb("slots", [P, NE], U32)
        slot_col = sb("slot_col", [P, 2], U32)
        xg = sb("xg", [P, 2, D])
        xT = sb("xT", [P, 2, DC, P])
        silu = sb("silu", [P, 2, FE])
        act_rows = sb("act_rows", [P, 2, FE])
        actT_high = sb("actT_high", [P, 2, 2, P], F32R)
        actT_low = sb("actT_low", [P, 2, 2, P], F32R)
        w_down_high = sb("w_down_high", [P, 2, D], F32R)
        w_down_low = sb("w_down_low", [P, 2, D], F32R)
        y = sb("y", [P, 2, D])
        got = [xg[:, 0], xg[:, 1], y[:, 0], y[:, 1]]
        served = sb("served", [P, 2, NT])
        pass_gate = sb("pass_gate", [P, 2, NT])
        row = sb("row", [P, 2, NT])
        result_row = sb("result_row", [P, 2, NT], U32)
        turned = ps("turned", [P, 2, 512])
        hidden = ps("hidden", [P, 2, 2 * FE])
        act_turned_ps = ps("act_turned_ps", [P, 2, 2, P])
        down = ps("down", [P, 2, 512])
        table = ps("table", [P, 512])
        place = table[:, NE:(NT + 2) * NE].rearrange("p (t e) -> p t e", e=NE)
        router = Router(m, r, sb, sem, place)
        w_hidden = sb("w_hidden", [P, 4, DC, 2 * FE])
        w_down = sb("w_down", [P, 4, 2, D])
        hidden_loaded = [sem(f"hidden_loaded{b}") for b in range(4)]
        down_loaded = [sem(f"down_loaded{b}") for b in range(4)]
        gathered = [sem("gathered0", kept=True), sem("gathered1", kept=True)]
        saved = [sem("saved0"), sem("saved1")]
        take_ready, take_used, table_ready, slots_ready = sem("take_ready"), sem("take_used"), sem("table_ready"), sem("slots_ready")
        col_ready, x_turned, xT_low, xT_high = sem("col_ready"), sem("x_turned"), sem("xT_low"), sem("xT_high")
        hidden_ready, silu_ready, act_ready = sem("hidden_ready"), sem("silu_ready"), sem("act_ready")
        act_turned, actT_ready, down_ready, y_low, y_high = sem("act_turned"), sem("actT_ready"), sem("down_ready"), sem("y_low"), sem("y_high")
        moved, passed, prepared, added = sem("moved"), sem("passed"), sem("prepared"), sem("added")
        got_ready = [sem(f"got_ready{b}", kept=True) for b in range(4)]
        down_high_ready, down_low_ready, actT_high_ready = sem("down_high_ready"), sem("down_low_ready"), sem("actT_high_ready")
        block = ctx.enter_context(nc.Block())
        USES = [len(range(b, PICKS, 4)) for b in range(4)]

        def wait_count(eng, signal, count):
            if not isinstance(count, int) or count > 0:
                eng.wait_ge(signal, count)

        def first_wait(eng, signal, count):
            if not isinstance(count, int) or count > 0:
                eng.wait_ge(signal, count)
                eng.sem_inc(passed, 1)

        def all_passes(eng, one_pass):
            one_pass(0)
            most = eng.value_load(r.most[0:1, 0:1], min_val=0, max_val=T)
            with eng.If(most > SLOTS):
                with eng.Fori(1, PASSES) as c:
                    one_pass(c)

        def steps(eng, c, step):
            with eng.Fori(0, 6) as i:
                for j in range(2):
                    step(i * 2 + 3 + j, c * NE + i * 2 + (3 + j), c * (NE // 2) + i + (1 + j), 1 - j)

        def fixed(c, e, step):
            step(e, c * NE + e, c * (NE // 2) + e // 2, e % 2)

        def weight_steps(eng, c, first, rounds, step):
            with eng.Fori(0, rounds) as i:
                for j in range(first, first + 4):
                    step(i * 4 + j, c * NE + i * 4 + j, c * (NE // 2) + i * 2 + j // 2, j % 2, (c * (NE // 4) + i + j // 4, j % 4))

        def y_of(c):
            return r.y_dram if isinstance(c, int) else r.y_more

        def loaded_ahead(weights):
            use, slot = weights
            return isinstance(use, int) and use == 0 and slot == 0

        def expert_before(weights):
            use, slot = weights
            return (use, slot - 1) if slot else (use - 1, 3)

        def raw_down(weights):
            return m.first_down if loaded_ahead(weights) else w_down[:, weights[1]]

        def weight_fixed(c, e, step):
            step(e, c * NE + e, c * (NE // 2) + e // 2, e % 2, (c * (NE // 4) + e // 4, e % 4))

        @block.sync
        def _(sp):
            def load_hidden(e, n, slot):
                first_wait(sp, hidden_ready, n - 3)
                for j, w in enumerate((io["moe_w_gate"], io["moe_w_up"])):
                    sp.dma_start(w_hidden[:, slot, :, j * FE:(j + 1) * FE],
                                 w[layer, bass.ds(e, 1)].rearrange("a (c p) f -> p (a c) f", p=P)).then_inc(hidden_loaded[slot], 16)

            def load_down(e, n, slot):
                first_wait(sp, down_ready, n - 3)
                sp.dma_start(w_down[:, slot], io["moe_w_down"][layer, bass.ds(e, 1)].rearrange("a (c p) d -> p (a c) d", p=P)).then_inc(down_loaded[slot], 16)

            def save(e, n, b, y_dram):
                sp.wait_ge(y_low, n + 1)
                first_wait(sp, y_high, n + 1)
                sp.dma_start(y_dram.rearrange("(e p) d -> e p d", p=P)[bass.ds(e, 1)].rearrange("a p d -> (a p) d"),
                             y[:, b, :]).then_inc(saved[b], 16)

            def one_pass(c):
                y_dram = y_of(c)

                def step(e, n, k, b, weights):
                    load_hidden(e, n, weights[1])
                    save(e - 5, n - 5, 1 - b, y_dram)
                    load_down(e, n, weights[1])

                first_wait(sp, added, c * PICKS)
                for e in range(5):
                    if isinstance(c, int) and e == 0:
                        sp.sem_inc(hidden_loaded[0], 32)
                        sp.sem_inc(down_loaded[0], 16)
                        continue
                    if e in (2, 3):
                        first_wait(sp, col_ready, c * NE + e)
                    load_hidden(e, c * NE + e, e % 4)
                    load_down(e, c * NE + e, e % 4)
                weight_steps(sp, c, 5, 2, step)
                for e in range(13, NE):
                    weight_fixed(c, e, step)
                for e in range(NE - 5, NE):
                    save(e, c * NE + e, e % 2, y_dram)

            all_passes(sp, one_pass)
            for b in range(2):
                sp.wait_ge(saved[b], 16 * NE // 2)

        @block.gpsimd
        def _(pool):
            def gather(e, n, k, b):
                first_wait(pool, x_turned, n - 1)
                pool.tensor_copy(slot_col[:, b:b + 1], slots[:, bass.ds(e, 1)]).then_inc(col_ready, 1)
                first_wait(pool, col_ready, n + 1)
                pool.indirect_dma_start(xg[:, b, :], None, r.h_dram, bass.IndirectOffsetOnAxis(slot_col[:, b:b + 1], 0)).then_inc(gathered[b], 16)

            def one_pass(c):
                pool.wait_ge(slots_ready, c + 1)
                for e in range(3):
                    fixed(c, e, gather)
                steps(pool, c, gather)
                fixed(c, NE - 1, gather)
                if isinstance(c, int):
                    return
                for b in range(2):
                    first_wait(pool, saved[b], (c + 1) * (16 * NE // 2))
                for i in range(PICKS):
                    t, j = divmod(i, 2)
                    w = width(t)
                    first_wait(pool, added, c * PICKS + max(i - 3, 0))
                    pool.indirect_dma_start(got[i % 4][0:w, :], None, y_of(c),
                                            bass.IndirectOffsetOnAxis(result_row[0:w, j, t:t + 1], 0)).then_inc(got_ready[i % 4], 16)

            all_passes(pool, one_pass)

        @block.tensor
        def _(pe):
            def turn_x(e, n, k, b):
                pe.wait_ge(gathered[b], (k + 1) * 16)
                wait_count(pe, xT_low, n)
                wait_count(pe, xT_high, n)
                for c in range(DC):
                    last = pe.transpose(turned[:, c // 4, (c % 4) * P:(c % 4 + 1) * P], xg[:, b, c * P:(c + 1) * P], m.ident[:, :])
                last.then_inc(x_turned, 1)

            def make_hidden(e, n, b, weights):
                use, slot = weights
                w = m.first_hidden if loaded_ahead(weights) else w_hidden[:, slot]
                pe.wait_ge(xT_low, n + 1)
                pe.wait_ge(xT_high, n + 1)
                pe.wait_ge(hidden_loaded[slot], (use + 1) * 32)
                wait_count(pe, act_ready, n - 1)
                for c in range(DC):
                    last = pe.matmul(hidden[:, b, :], xT[:, b, c, :], w[:, c, :], start=(c == 0), stop=(c == DC - 1))
                last.then_inc(hidden_ready, 1)

            def turn_act(e, n, k, b):
                pe.wait_ge(act_ready, n + 1)
                for c in range(2):
                    last = pe.transpose(act_turned_ps[:, b, c, :], act_rows[:, b, c * P:(c + 1) * P], m.ident[:, :])
                last.then_inc(act_turned, 1)

            def make_down(e, n, b):
                pe.wait_ge(actT_ready, n + 1)
                pe.wait_ge(down_low_ready, n + 1)
                wait_count(pe, y_low, n)
                wait_count(pe, y_high, n)
                for half in range(2):
                    for c in range(2):
                        for j, (left, right) in enumerate(((actT_high, w_down_high), (actT_high, w_down_low), (actT_low, w_down_high))):
                            last = pe.matmul(down[:, half, :], left[:, b, c, :], right[:, c, half * 512:(half + 1) * 512],
                                             start=(c == 0 and j == 0), stop=(c == 1 and j == 2))
                last.then_inc(down_ready, 1)

            def one_pass(c):
                for i in range(PICKS):
                    pe.wait_ge(take_ready, c * PICKS + i + 1)
                    rows = width(i // 2)
                    pe.matmul(table[:, 0:NE], take[0:rows, i, :], value[0:rows, i, :], start=(i == 0), stop=(i == PICKS - 1)).then_inc(take_used, 1)
                def step(e, n, k, b, weights, more=True):
                    half = k - 1 + b
                    make_hidden(e, n, b, weights)
                    turn_act(e - 1, n - 1, half, 1 - b)
                    if more:
                        turn_x(e + 1, n + 1, k + b, 1 - b)
                    make_down(e - 1, n - 1, 1 - b)

                fixed(c, 0, turn_x)
                weight_fixed(c, 0, lambda e, n, k, b, weights: make_hidden(e, n, b, weights))
                fixed(c, 1, turn_x)
                weight_fixed(c, 1, step)
                weight_fixed(c, 2, step)
                weight_steps(pe, c, 3, 3, step)
                weight_fixed(c, NE - 1, lambda e, n, k, b, weights: step(e, n, k, b, weights, more=False))
                fixed(c, NE - 1, turn_act)
                fixed(c, NE - 1, lambda e, n, k, b: make_down(e, n, b))

            router.on_tensor(pe)
            all_passes(pe, one_pass)

        @block.scalar
        def _(act):
            def store_xT(e, n, k, b):
                act.wait_ge(x_turned, n + 1)
                act.activation(xT[:, b, 0:4, :], turned[:, 0, :].rearrange("p (c n) -> p c n", c=4), ACT.Copy).then_inc(xT_low, 1)

            def gate(e, n, k, b):
                act.wait_ge(hidden_ready, n + 1)
                wait_count(act, act_ready, n - 1)
                act.activation(silu[:, b, :], hidden[:, b, 0:FE], ACT.Silu).then_inc(silu_ready, 1)

            def cut_high(n, weights):
                use, slot = weights
                act.wait_ge(down_loaded[slot], (use + 1) * 16)
                wait_count(act, down_ready, n)
                act.activation(w_down_high[:, :, :], raw_down(weights), ACT.Copy).then_inc(down_high_ready, 1)

            def store_y(e, n, k, b):
                act.wait_ge(down_ready, n + 1)
                if not isinstance(k, int) or k > 0:
                    act.wait_ge(saved[b], k * 16)
                act.activation(y[:, b, 0:512], down[:, 0, :], ACT.Copy).then_inc(y_low, 1)

            def one_pass(c):
                def step(e, n, k, b, weights, more=True):
                    half = k - 1 + b
                    gate(e - 1, n - 1, half, 1 - b)
                    cut_high(n - 1, expert_before(weights))
                    if more:
                        store_xT(e + 1, n + 1, k + b, 1 - b)
                    store_y(e - 1, n - 1, half, 1 - b)

                fixed(c, 0, store_xT)
                fixed(c, 1, store_xT)
                weight_fixed(c, 1, step)
                weight_fixed(c, 2, step)
                weight_steps(act, c, 3, 3, step)
                weight_fixed(c, NE - 1, lambda e, n, k, b, weights: step(e, n, k, b, weights, more=False))
                fixed(c, NE - 1, gate)
                weight_fixed(c, NE - 1, lambda e, n, k, b, weights: cut_high(n, weights))
                fixed(c, NE - 1, store_y)

            router.on_scalar(act)
            all_passes(act, one_pass)

        @block.vector
        def _(dve):
            def store_xT(e, n, k, b):
                dve.wait_ge(x_turned, n + 1)
                dve.tensor_copy(xT[:, b, 4:8, :], turned[:, 1, :].rearrange("p (c n) -> p c n", c=4)).then_inc(xT_high, 1)

            def multiply(e, n, k, b):
                dve.wait_ge(silu_ready, n + 1)
                wait_count(dve, act_turned, n - 1)
                dve.tensor_tensor(act_rows[:, b, :], hidden[:, b, FE:2 * FE], silu[:, b, :], ALU.mult).then_inc(act_ready, 1)

            def cut_low(n, weights):
                dve.wait_ge(down_high_ready, n + 1)
                dve.tensor_tensor(w_down_low[:, :, :], raw_down(weights), w_down_high[:, :, :].bitcast(F32), ALU.subtract).then_inc(down_low_ready, 1)

            def store_actT(e, n, k, b):
                dve.wait_ge(act_turned, n + 1)
                wait_count(dve, down_ready, n - 1)
                dve.tensor_copy(actT_high[:, b, :, :], act_turned_ps[:, b, :, :]).then_inc(actT_high_ready, 1)
                dve.wait_ge(actT_high_ready, n + 1)
                dve.tensor_tensor(actT_low[:, b, :, :], act_turned_ps[:, b, :, :], actT_high[:, b, :, :].bitcast(F32), ALU.subtract).then_inc(actT_ready, 1)

            def store_y(e, n, k, b):
                dve.wait_ge(down_ready, n + 1)
                if not isinstance(k, int) or k > 0:
                    dve.wait_ge(saved[b], k * 16)
                dve.tensor_copy(y[:, b, 512:1024], down[:, 1, :]).then_inc(y_high, 1)

            def one_pass(c):
                if not isinstance(c, int):
                    dve.tensor_scalar(r.place[:, :, :], r.place[:, :, :], float(-SLOTS), None, ALU.add).then_inc(moved, 1)
                    dve.wait_ge(moved, c)
                p0 = c * 4
                dve.tensor_scalar(served[:, :, :], r.place[:, :, :], 0.0, None, ALU.is_ge).then_inc(prepared, 1)
                dve.wait_ge(prepared, p0 + 1)
                dve.scalar_tensor_tensor(out=served[:, :, :], in0=r.place[:, :, :], scalar=float(SLOTS), in1=served[:, :, :], op0=ALU.is_lt, op1=ALU.mult)
                dve.tensor_tensor(row[:, :, :], r.place[:, :, :], r.expert_row[:, :, :], ALU.add).then_inc(prepared, 1)
                dve.wait_ge(prepared, p0 + 2)
                gates, rows = (r.pass_gate, r.result_row) if isinstance(c, int) else (pass_gate, result_row)
                dve.tensor_tensor(gates[:, :, :], r.gate[:, :, :], served[:, :, :], ALU.mult)
                dve.tensor_tensor(row[:, :, :], row[:, :, :], served[:, :, :], ALU.mult).then_inc(prepared, 1)
                dve.wait_ge(prepared, p0 + 3)
                dve.tensor_copy(rows[:, :, :], row[:, :, :]).then_inc(prepared, 1)
                dve.wait_ge(prepared, p0 + 4)
                for i in range(PICKS):
                    t, j = divmod(i, 2)
                    if not isinstance(c, int):
                        dve.wait_ge(take_used, (c - 1) * PICKS + (i + 1))
                    dve.tensor_scalar(take[:, i, :], m.consts[:, C_SLOT:C_SLOT + P], r.place[:, j, t:t + 1], None, ALU.is_equal)
                    dve.tensor_scalar(value[:, i, :], r.pick[:, j, t, :], m.consts[:, C_TOKEN + t:C_TOKEN + t + 1], None, ALU.mult).then_inc(take_ready, 1)
                dve.wait_ge(take_used, c * PICKS + PICKS)
                if not isinstance(c, int):
                    dve.wait_ge(x_turned, c * NE)
                dve.tensor_copy(slots[:, :], table[:, 0:NE]).then_inc(slots_ready, 1)
                fixed(c, 0, store_xT)
                fixed(c, 1, store_xT)

                def step(e, n, k, b, weights, more=True):
                    half = k - 1 + b
                    multiply(e - 1, n - 1, half, 1 - b)
                    cut_low(n - 1, expert_before(weights))
                    store_actT(e - 1, n - 1, half, 1 - b)
                    if more:
                        store_xT(e + 1, n + 1, k + b, 1 - b)
                    store_y(e - 1, n - 1, half, 1 - b)

                weight_fixed(c, 1, step)
                weight_fixed(c, 2, step)
                weight_steps(dve, c, 3, 3, step)
                weight_fixed(c, NE - 1, lambda e, n, k, b, weights: step(e, n, k, b, weights, more=False))
                fixed(c, NE - 1, multiply)
                weight_fixed(c, NE - 1, lambda e, n, k, b, weights: cut_low(n, weights))
                fixed(c, NE - 1, store_actT)
                fixed(c, NE - 1, store_y)
                if isinstance(c, int):
                    dve.sem_inc(added, PICKS)
                    return
                for i in range(PICKS):
                    t, j = divmod(i, 2)
                    w = width(t)
                    x = m.x[0:w, t, :]
                    dve.wait_ge(got_ready[i % 4], ((c - 1) * USES[i % 4] + (i // 4 + 1)) * 16)
                    if j:
                        dve.wait_ge(added, c * PICKS + i)
                    dve.scalar_tensor_tensor(out=x, in0=got[i % 4][0:w, :], scalar=pass_gate[0:w, j, t:t + 1], in1=x,
                                             op0=ALU.mult, op1=ALU.add).then_inc(added, 1)

            router.on_vector(dve)
            all_passes(dve, one_pass)


def project_dsa_stage(nc, m, a, r, high, low, io):
    with ExitStack() as ctx:
        sb, ps, sem = tools(nc, ctx, "dsa")
        rope = sb("rope", [P, R_COLS])
        idx_rows = sb("idx_rows", [P, 2, IDX_COLS])
        idx_rot = sb("idx_rot", [P, 2, 6, D_IDX])
        idx_tmp = sb("idx_tmp", [P, 2, 5, D_IDX])
        idx_w = sb("idx_w", [P, NT, H_IDX])
        cache_i = sb("cache_i", [P, 2, 2, D_IDX])
        cache_k = sb("cache_k", [P, 2, KV_DSA * HEAD])
        qiT = sb("qiT", [P, 2, T])
        kiT = sb("kiT", [P, PROMPT])
        kiT_sample = sb("kiT_sample", [P, LS])
        relu = sb("relu", [P, 2, 512])
        COLS = 2 * HEAD
        turning = sb("turning", [P, 3, 2, COLS])
        rows, rot, tmp = (turning[:, k] for k in range(3))
        stat = sb("stat", [P, 6, NT])
        w_raw = m.spare[:, 0:2 * DC * IDX_COLS].rearrange("p (b c n) -> p b c n", b=2, c=DC)
        w_high = sb("w_high", [P, 2, DC, IDX_COLS], F32R)
        w_low = sb("w_low", [P, 2, DC, IDX_COLS], F32R)
        acc = ps("acc", [P, 4, 512])
        turned = ps("turned", [P, 2, 512])
        logit = ps("logit", [P, 2, 512])
        w_loaded = [sem("w_loaded0"), sem("w_loaded1")]
        w_high_ready, w_low_ready = sem("w_high_ready"), sem("w_low_ready")
        small_loaded, cache_v_loaded = sem("small_loaded"), sem("cache_v_loaded")
        group_ready, group_stored = sem("group_ready"), sem("group_stored")
        idx_chain, idx_rot_ready, pool_chain, rot_ready = sem("idx_chain"), sem("idx_rot_ready"), sem("pool_chain"), sem("rot_ready")
        idx_turned, idx_T_stored = sem("idx_turned"), sem("idx_T_stored")
        logit_ready, relu_ready, score_step = sem("logit_ready"), sem("relu_ready"), sem("score_step")
        rows_turned, rows_T_stored = sem("rows_turned"), sem("rows_T_stored")
        best_found, best_taken, barred = sem("best_found"), sem("best_taken"), sem("barred")
        idx_saved = [sem("idx_saved0"), sem("idx_saved1")]
        k_saved = [sem("k_saved0"), sem("k_saved1")]
        v_saved = sem("v_saved")
        free = a.qT[:, :, :].rearrange("p h n -> p (h n)")
        norm = Norm(m, sem, io["norm_mix"][1], free[:, 3 * D:4 * D], free[:, 0:2 * D].rearrange("p (b n) -> p b n", b=2),
                    free[:, 2 * D:3 * D], stat, acc, high, low)
        combine = Combine(m, r, sem, [a.kT[:, :, :].rearrange("p h n -> p (h n)"), a.v_rows[:, 0:D // COLS, :].rearrange("p t n -> p (t n)"),
                                      relu[:, :, :].rearrange("p b n -> p (b n)"), turning[:, 0:2].rearrange("p k b n -> p (k b n)")])
        block = ctx.enter_context(nc.Block())

        UNITS = [(1536, IDX_COLS), (1024, COLS)] + [(pair * COLS, COLS) for pair in range(4)] + [(1280, COLS)]
        NI = NT
        EARLY = 4
        NR = 5 * NT
        TILES = [3, PT, 2, 1]
        SCORES = [(t, h) for t in TILES for h in range(H_IDX)]
        SIZE = {t: (LS if t == PT else (t + 1) * P) for t in TILES}
        ROUNDS = {t: (K_SAMPLE if t == PT else K_PROMPT) // 8 for t in TILES}
        best = {t: sb(f"best{t}", [P, 8]) for t in TILES}
        score = {t: sb(f"score{t}", [P, SIZE[t]]) for t in TILES}

        def idx_acc(t):
            return logit[:, t % 2, 0:IDX_COLS]

        @block.sync
        def _(sp):
            w_view = io["w_in_dsa"].rearrange("(c p) n -> p c n", p=P)

            def load_unit(i):
                lo, n = UNITS[i]
                if i >= 2:
                    sp.wait_ge(w_low_ready, i - 1)
                sp.dma_start(w_raw[:, i % 2, :, 0:n], w_view[:, :, lo:lo + n]).then_inc(w_loaded[i % 2], 16)

            norm.load(sp)
            load_unit(0)
            sp.wait_ge(combine.added, 2 * NT - 3)
            sp.dma_start(rope[:, :], io["rope"]).then_inc(small_loaded, 16)
            for twice in range(2):
                sp.dma_start(cache_i[:, :, twice, :], io["cache_dsa_idx_k"].rearrange("b (j p) e -> p (b j) e", p=P)).then_inc(small_loaded, 16)
            sp.dma_start(cache_k[:, :, :], io["cache_dsa_k"].rearrange("b (j p) h d -> p (b j) (h d)", p=P)).then_inc(small_loaded, 16)
            load_unit(1)
            sp.dma_start(a.cache_v[:, :, :], io["cache_dsa_v"].rearrange("b (j p) h d -> p (b j) (h d)", p=P)).then_inc(cache_v_loaded, 16)
            load_unit(2)
            for t in range(NT):
                w = width(t)
                sp.wait_ge(idx_rot_ready, t + 1)
                dst = io["out_dsa_idx"][0].rearrange("b t e -> (b t) e")[t * P:(t + 1) * P, :] if t < PT else io["out_dsa_idx"][1].rearrange("b t e -> (b t) e")
                sp.dma_start(dst, idx_rot[0:w, t % 2, 4, :]).then_inc(idx_saved[t % 2], 16)
            load_unit(3)
            for t in range(NT):
                sp.wait_ge(rot_ready, t + 1)
                sp.dma_start(rows_of(io["out_dsa_k"], t), rot[0:width(t), t % 2, :]).then_inc(k_saved[t % 2], 16)
            for i in range(4, len(UNITS)):
                load_unit(i)
            for t in range(NT):
                sp.wait_ge(group_stored, NI + NR + t + 1)
                sp.dma_start(rows_of(io["out_dsa_v"], t), a.v_rows[0:width(t), t, :]).then_inc(v_saved, 16)
            sp.wait_ge(idx_saved[0], 48)
            sp.wait_ge(idx_saved[1], 32)
            sp.wait_ge(k_saved[0], 48)
            sp.wait_ge(k_saved[1], 32)
            sp.wait_ge(v_saved, 16 * NT)
            sp.wait_ge(cache_v_loaded, 16)

        @block.tensor
        def _(pe):
            def group(g):
                i, t = divmod(g, NT)
                n = UNITS[i][1]
                if t == 0:
                    pe.wait_ge(w_low_ready, i + 1)
                if g < NI:
                    pe.wait_ge(norm.low_ready, t + 1)
                    if g >= 2:
                        pe.wait_ge(group_stored, g - 1)
                else:
                    pe.wait_ge(group_stored, g - 3)
                out = idx_acc(t) if g < NI else acc[:, g % 4, 0:n]
                norm.product(pe, out, t, w_high[:, i % 2, :, 0:n], w_low[:, i % 2, :, 0:n]).then_inc(group_ready, 1)

            def turn_idx(t):
                w = width(t)
                pe.wait_ge(idx_rot_ready, t + 1)
                pe.wait_ge(idx_T_stored, t + 1)
                for j in range(3):
                    last = pe.transpose(turned[:, t % 2, j * P:j * P + w], idx_rot[0:w, t % 2, 2 * j:2 * j + 2, :].rearrange("p h e -> p (h e)"), m.ident[0:w, 0:w])
                last.then_inc(idx_turned, 1)

            norm.turn(pe, 0)
            for t in range(1, NT):
                norm.turn(pe, t)
                group(t - 1)
            pe.wait_ge(small_loaded, 64)
            for kb in range(2):
                for h in range(2):
                    last = pe.transpose(turned[:, 0, (2 * h + kb) * P:(2 * h + kb + 1) * P], cache_k[:, kb, h * P:(h + 1) * P], m.ident[:, :])
            last.then_inc(idx_turned, 1)
            for kb in range(2):
                last = pe.transpose(turned[:, 1, kb * P:(kb + 1) * P], cache_i[:, kb, :, :].rearrange("p a e -> p (a e)"), m.ident[:, :])
            last.then_inc(idx_turned, 1)
            group(NI - 1)
            for t in range(EARLY):
                group(NI + t)
                turn_idx(t)
            turn_idx(NT - 1)
            pe.wait_ge(idx_T_stored, 2 + NT)
            for i, (t, h) in enumerate(SCORES):
                half = slice((h % 2) * 64, (h % 2) * 64 + 64)
                w = width(t)
                if i >= 2:
                    pe.wait_ge(relu_ready, i - 1)
                keys = kiT_sample[half, :] if t == PT else kiT[half, 0:SIZE[t]]
                pe.matmul(logit[0:w, i % 2, 0:SIZE[t]], qiT[half, h // 2, cols(t)], keys, start=True, stop=True).then_inc(logit_ready, 1)

            def turn_rows(i):
                w = width(i % NT)
                pe.wait_ge(rot_ready, i + 1)
                if i >= 2:
                    pe.wait_ge(rows_T_stored, i - 1)
                for h in range(2):
                    last = pe.transpose(turned[:, i % 2, h * P:h * P + w], rot[0:w, i % 2, h * P:(h + 1) * P], m.ident[0:w, 0:w])
                last.then_inc(rows_turned, 1)

            for i in range(NR + NT):
                if i >= EARLY:
                    group(NI + i)
                if 2 <= i < NR + 2:
                    turn_rows(i - 2)

        @block.scalar
        def _(act):
            def cut_high(i):
                n = UNITS[i][1]
                act.wait_ge(w_loaded[i % 2], 16 * (i // 2 + 1))
                if i >= 2:
                    act.wait_ge(group_ready, (i - 1) * NT)
                act.activation(w_high[:, i % 2, :, 0:n], w_raw[:, i % 2, :, 0:n], ACT.Copy).then_inc(w_high_ready, 1)

            def store_idx_rows(t):
                w = width(t)
                act.wait_ge(group_ready, t + 1)
                if t >= 2:
                    act.wait_ge(idx_rot_ready, t - 1)
                act.activation(idx_rows[0:w, t % 2, :], idx_acc(t)[0:w, :], ACT.Copy).then_inc(group_stored, 1)

            act.preload_act_table_set("sqrt_and_others")
            cut_high(0)
            for t in range(NT):
                act.wait_ge(combine.added, 2 * t + 2)
                norm.square(act, t)
            norm.root(act, 0)
            for t in range(NT):
                norm.store_high(act, t)
                if t in (2, 3):
                    store_idx_rows(t - 2)
            cut_high(1)
            for t in range(2, NT):
                store_idx_rows(t)
            cut_high(2)
            for i, (t, h) in enumerate(SCORES):
                w = width(t)
                act.wait_ge(logit_ready, i + 1)
                if i >= 2:
                    act.wait_ge(score_step, i - 1)
                act.activation(relu[0:w, i % 2, 0:SIZE[t]], logit[0:w, i % 2, 0:SIZE[t]], ACT.Relu, scale=D_IDX ** -0.5).then_inc(relu_ready, 1)

            def store_T(i):
                unit, t = divmod(i, NT)
                w = width(t)
                act.wait_ge(rows_turned, i + 1)
                if unit:
                    dst = a.qT[:, 2 * unit - 2:2 * unit, cols(t)]
                else:
                    dst = a.kT[:, :, t * P:(t + 1) * P] if t < PT else a.kT_sample[:, :, PAST:LS]
                act.activation(dst, turned[:, i % 2, 0:COLS].rearrange("p (h n) -> p h n", h=2)[:, :, 0:w], ACT.Copy).then_inc(rows_T_stored, 1)

            for i in range(NR + NT):
                unit, t = divmod(i, NT)
                w = width(t)
                g = NI + i
                act.wait_ge(group_ready, g + 1)
                if i < NR:
                    if i >= 2:
                        act.wait_ge(rot_ready, i - 1)
                    act.activation(rows[0:w, i % 2, :], acc[0:w, g % 4, 0:COLS], ACT.Copy, scale=SCALE if unit else 1.0).then_inc(group_stored, 1)
                else:
                    act.activation(a.v_rows[0:w, t, :], acc[0:w, g % 4, 0:COLS], ACT.Copy).then_inc(group_stored, 1)
                if 2 <= i < NR + 2:
                    store_T(i - 2)
                if t == NT - 1 and unit + 3 < len(UNITS):
                    cut_high(unit + 3)

        def rotate(eng, chain, out, x, tmp_a, tmp_b, cos, sin, heads):
            w, half = x.shape[0], x.shape[2] // 2
            swapped = x.rearrange("p h (s e) -> p h s e", s=2)[:, :, ::-1, :]
            chain(eng.tensor_tensor(tmp_a, x, cos.unsqueeze(1).broadcast_to([w, heads, 2 * half]), ALU.mult))
            chain(eng.tensor_tensor(tmp_b.rearrange("p h (s e) -> p h s e", s=2), swapped,
                                    sin.rearrange("p (s e) -> p s e", s=2).unsqueeze(1).broadcast_to([w, heads, 2, half]), ALU.mult))
            chain.wait()
            return eng.tensor_tensor(out, tmp_a, tmp_b, ALU.add)

        @block.gpsimd
        def _(pool):
            for t in range(NT):
                combine.gather(pool, t)
            chain = Chain(pool, pool_chain)
            pool.wait_ge(small_loaded, 64)
            for i in range(NR):
                t = i % NT
                w = width(t)
                pool.wait_ge(group_stored, NI + i + 1)
                if i >= 2:
                    pool.wait_ge(rows_turned, i - 1)
                    if i < NT + 2:
                        pool.wait_ge(k_saved[i % 2], 16 * (i // 2))

                def view(x):
                    return x.rearrange("p (h d) -> p h d", d=HEAD)

                rotate(pool, chain, view(rot[0:w, i % 2, :]), view(rows[0:w, i % 2, :]), view(tmp[0:w, 0, :]), view(tmp[0:w, 1, :]),
                       rope[0:w, R_COS + t * HEAD:R_COS + (t + 1) * HEAD], rope[0:w, R_SIN + t * HEAD:R_SIN + (t + 1) * HEAD], 2).then_inc(rot_ready, 1)
                pool.wait_ge(rot_ready, i + 1)

        @block.vector
        def _(dve):
            chain = Chain(dve, idx_chain)

            def cut_low(i):
                n = UNITS[i][1]
                dve.wait_ge(w_high_ready, i + 1)
                dve.tensor_tensor(w_low[:, i % 2, :, 0:n], w_raw[:, i % 2, :, 0:n], w_high[:, i % 2, :, 0:n].bitcast(F32),
                                  ALU.subtract).then_inc(w_low_ready, 1)

            norm.clear_pad(dve)
            for t in range(NT):
                combine.add(dve, t)
            cut_low(0)
            norm.inverse_root(dve, 0)
            norm.scale(dve, 0)
            for t in range(1, NT):
                norm.scale(dve, t)
                norm.store_low(dve, t - 1)
            norm.store_low(dve, NT - 1)
            cut_low(1)
            dve.wait_ge(idx_turned, 1)
            dve.tensor_copy(a.kT_sample[:, :, 0:PAST], turned[:, 0, :].rearrange("p (h n) -> p h n", h=2)).then_inc(idx_T_stored, 1)
            dve.wait_ge(idx_turned, 2)
            dve.tensor_copy(kiT_sample[:, 0:PAST], turned[:, 1, 0:PAST]).then_inc(idx_T_stored, 1)

            def store_idx_T(t):
                w = width(t)
                dve.wait_ge(idx_turned, 3 + t)
                dve.tensor_copy(qiT[:, :, cols(t)], turned[:, t % 2, 0:2 * P].rearrange("p (h n) -> p h n", h=2)[:, :, 0:w])
                dst = kiT[:, t * P:(t + 1) * P] if t < PT else kiT_sample[:, PAST:LS]
                dve.tensor_copy(dst, turned[:, t % 2, 2 * P:2 * P + w]).then_inc(idx_T_stored, 1)

            dve.wait_ge(small_loaded, 64)
            for t in range(NT):
                w = width(t)
                dve.wait_ge(group_stored, t + 1)
                if t >= 2:
                    dve.wait_ge(idx_turned, 2 + t - 1)
                    dve.wait_ge(idx_saved[t % 2], 16 * (t // 2))
                x = idx_rows[0:w, t % 2, 0:5 * D_IDX].rearrange("p (h e) -> p h e", h=5)
                chain(rotate(dve, chain, idx_rot[0:w, t % 2, 0:5, :], x, idx_tmp[0:w, 0], idx_tmp[0:w, 1],
                             rope[0:w, R_ICOS + t * D_IDX:R_ICOS + (t + 1) * D_IDX], rope[0:w, R_ISIN + t * D_IDX:R_ISIN + (t + 1) * D_IDX], 5))
                chain(dve.tensor_scalar(idx_w[0:w, t, :], idx_rows[0:w, t % 2, 5 * D_IDX:IDX_COLS], H_IDX ** -0.5, None, ALU.mult))
                chain.wait()
                dve.tensor_copy(idx_rot[0:w, t % 2, 5, :], idx_rot[0:w, t % 2, 4, :]).then_inc(idx_rot_ready, 1)
                if t >= 1:
                    store_idx_T(t - 1)
            store_idx_T(NT - 1)
            cut_low(2)
            for i, (t, h) in enumerate(SCORES):
                w = width(t)
                s = score[t][0:w, :]
                dve.wait_ge(relu_ready, i + 1)
                if h == 0:
                    dve.tensor_scalar(s, relu[0:w, i % 2, 0:SIZE[t]], idx_w[0:w, t, 0:1], None, ALU.mult).then_inc(score_step, 1)
                else:
                    dve.wait_ge(score_step, i)
                    dve.scalar_tensor_tensor(out=s, in0=relu[0:w, i % 2, 0:SIZE[t]], scalar=idx_w[0:w, t, h:h + 1], in1=s,
                                             op0=ALU.mult, op1=ALU.add).then_inc(score_step, 1)
            dve.wait_ge(score_step, len(SCORES))
            for t in (3, 2, 1):
                last = dve.memset(score[t][0:CHUNK, SIZE[t] - CHUNK:SIZE[t]], BARRED)
            last.then_inc(barred, 1)
            dve.wait_ge(barred, 1)
            found = taken = 0
            for k in range(max(ROUNDS.values())):
                live = [t for t in TILES if k < ROUNDS[t]]
                if k:
                    dve.wait_ge(best_taken, taken)
                for t in live:
                    dve.max(best[t][0:width(t), :], score[t][0:width(t), :]).then_inc(best_found, 1)
                for j, t in enumerate(live):
                    dve.wait_ge(best_found, found + j + 1)
                    dve.match_replace(score[t][0:width(t), :], best[t][0:width(t), :], score[t][0:width(t), :], TAKEN).then_inc(best_taken, 1)
                found += len(live)
                taken += len(live)
                if k % 4 == 3 and 3 + k // 4 < len(UNITS):
                    cut_low(3 + k // 4)
            dve.wait_ge(best_taken, taken)
            for t in TILES:
                dve.tensor_scalar(a.unchosen[t][0:width(t), :], score[t][0:width(t), :], UNTAKEN_FROM, NEG, ALU.is_gt, ALU.mult)


def trunk_program(nc, io):
    with ExitStack() as ctx:
        def sb(name, shape, dtype=F32):
            return ctx.enter_context(nc.sbuf_tensor(name, shape, dtype))

        m = Main()
        m.x = sb("x", [P, NT, D])
        m.spare = sb("spare", [P, DC * 2 * FE + 2 * D])
        m.first_hidden = m.spare[:, 0:DC * 2 * FE].rearrange("p (c n) -> p c n", c=DC)
        m.first_down = m.spare[:, DC * 2 * FE:].rearrange("p (c n) -> p c n", c=2)
        m.consts = sb("consts", [P, C_COLS])
        m.masks = sb("masks", [P, 4 * P], BF16)
        m.before = sb("before", [P, P], BF16)
        m.ones16 = sb("ones16", [P, P], BF16)
        m.ones = sb("ones", [P, 512])
        m.head_select = sb("head_select", [H_FOX, H_FOX * P])
        m.ident = m.consts[:, C_IDENT:C_IDENT + P]
        m.ident16 = m.masks[:, C_IDENT:C_IDENT + P]
        neg_sb, neg_fox, neg_chunk = (m.masks[:, c:c + P] for c in (C_NEG_SB, C_NEG_FOX, C_NEG_CHUNK))

        def routing(layer, scope):
            def sb(name, shape, dtype=F32):
                return scope.enter_context(nc.sbuf_tensor(f"moe{layer}_{name}", shape, dtype))

            r = Routing()
            r.w_group, r.w_router = io["moe_w_group"][layer], io["moe_w_router"][layer]
            r.first_weights = [io[name][layer, 0] for name in ("moe_w_gate", "moe_w_up", "moe_w_down")]
            r.logits = sb("logits", [P, NT, NG + NE])
            r.pick = sb("pick", [P, 2, NT, NE])
            r.place = sb("place", [P, 2, NT])
            r.gate = sb("gate", [P, 2, NT])
            r.expert_row = sb("expert_row", [P, 2, NT])
            r.most = sb("most", [P, 1], U32)
            r.result_row = sb("result_row", [P, 2, NT], U32)
            r.pass_gate = sb("pass_gate", [P, 2, NT])
            r.h_dram = nc.dram_tensor(f"h_dram{layer}", (T, D), F32, kind="Internal").ap()
            r.y_dram = nc.dram_tensor(f"y_dram{layer}", (NE * P, D), F32, kind="Internal").ap()
            r.y_more = nc.dram_tensor(f"y_more{layer}", (NE * P, D), F32, kind="Internal").ap()
            return r

        def tile_steps(pairs, sample):
            steps = [(sample, True)]
            for t in reversed(range(PT)):
                steps += [([Unit([h], t, stick) for h, stick in pair], j == len(pairs) - 1) for j, pair in enumerate(pairs)]
            return steps

        r0, r1 = routing(0, ctx), routing(1, ctx)
        with ExitStack() as inner:
            def sb(name, shape, dtype=F32):
                return inner.enter_context(nc.sbuf_tensor(f"ab_{name}", shape, dtype))

            a = Attention()
            a.qT = sb("qT", [P, 8, T])
            a.kT = sb("kT", [P, 8, PROMPT])
            a.kT_sample = sb("kT_sample", [P, 8, LS])
            a.v_rows = sb("v_rows", [P, NT, D])
            a.cache_v = sb("cache_v", [P, 2, D])
            a.forget = sb("forget", [4, PROMPT])
            a.forget_sample = sb("forget_sample", [4, LS])
            with ExitStack() as parts:
                high, low = (parts.enter_context(nc.sbuf_tensor(f"ab_hT_{part}", [P, DC * T + P - SAMPLE], F32R)) for part in ("high", "low"))
                project_ab_stage(nc, m, a, high, low, io)
            pairs = [((h, True), (h + H_SB, False)) for h in range(H_SB)]
            sample = [Unit(list(range(h0, h0 + 4)), PT, h0 == 0) for h0 in (0, H_SB)]
            mixer_stage(nc, m, a, r0, "mixer0", tile_steps(pairs, sample), lambda h: h, lambda h: h, {True: neg_sb, False: neg_fox}, True,
                        io["w_out_ab"], io["norm_ffn"][0], split=False)
        expert_stage(nc, m, r0, "experts0", 0, io)

        with ExitStack() as inner:
            def sb(name, shape, dtype=F32):
                return inner.enter_context(nc.sbuf_tensor(f"dsa_{name}", shape, dtype))

            a = Attention()
            a.qT = sb("qT", [P, H_DSA, T])
            a.kT = sb("kT", [P, KV_DSA, PROMPT])
            a.kT_sample = sb("kT_sample", [P, KV_DSA, LS])
            a.v_rows = sb("v_rows", [P, NT, KV_DSA * HEAD])
            a.cache_v = sb("cache_v", [P, 2, KV_DSA * HEAD])
            a.unchosen = {t: sb(f"unchosen{t}", [P, LS if t == PT else (t + 1) * P], BF16) for t in range(1, NT)}
            a.unchosen[0] = neg_chunk
            with ExitStack() as parts:
                high, low = (parts.enter_context(nc.sbuf_tensor(f"dsa_hT_{part}", [P, DC * T + P - SAMPLE], F32R)) for part in ("high", "low"))
                project_dsa_stage(nc, m, a, r0, high, low, io)
            kv = lambda h: h // (H_DSA // KV_DSA)
            pairs = [((h, False), (h + 1, False)) for h in range(0, H_DSA, 2)]
            sample = [Unit(list(range(h0, h0 + 4)), PT) for h0 in (0, 4)]
            mixer_stage(nc, m, a, r1, "mixer1", tile_steps(pairs, sample), kv, kv, {False: None}, False,
                        io["w_out_dsa"], io["norm_ffn"][1], split=True)
        expert_stage(nc, m, r1, "experts1", 1, io)
        y = [io["y_prompt"].rearrange("b t d -> (b t) d"), io["y_sample"].rearrange("b t d -> (b t) d")]
        final_stage(nc, m, r1, io["norm_final"], y)


_INS = ["x_prompt", "x_sample", "cache_sb_k", "cache_sb_v", "cache_fox_k", "cache_fox_v", "cache_fox_logf",
        "cache_dsa_k", "cache_dsa_v", "cache_dsa_idx_k", "norm_mix", "norm_ffn", "norm_final",
        "w_in_ab", "b_forget", "w_out_ab", "w_in_dsa", "w_out_dsa",
        "moe_w_group", "moe_w_router", "moe_w_gate", "moe_w_up", "moe_w_down"]


def _row_shapes(n):
    return [(1, n, H_SB, HEAD), (1, n, H_SB, HEAD), (1, n, H_FOX, HEAD), (1, n, H_FOX, HEAD), (1, n, H_FOX),
            (1, n, KV_DSA, HEAD), (1, n, KV_DSA, HEAD), (1, n, D_IDX)]


def _constants():
    import numpy as np

    p, j = np.arange(P)[:, None], np.arange(P)[None, :]
    consts = np.zeros((P, C_COLS), np.float32)
    consts[:, C_IDENT:C_IDENT + P] = p == j
    consts[:, C_NEG_SB:C_NEG_SB + P] = np.where(j >= p, NEG, 0)
    consts[:, C_NEG_FOX:C_NEG_FOX + P] = np.where(j > p, NEG, 0)
    consts[:, C_NEG_CHUNK:C_NEG_CHUNK + P] = np.where(j // CHUNK > p // CHUNK, NEG, 0)
    consts[:, C_BEFORE:C_BEFORE + P] = p < j
    consts[:, C_SLOT:C_SLOT + P] = j
    tile = np.arange(NT)[None, :]
    consts[:, C_TOKEN:C_TOKEN + NT] = np.minimum(tile * P + p, T - 1)
    consts[:, C_VALID:C_VALID + NT] = tile * P + p < T
    consts[:, C_FIRST:C_FIRST + 4] = 4 - np.arange(4)
    consts[:, C_EXPERT:C_EXPERT + NE] = np.arange(NE)
    select = np.zeros((H_FOX, H_FOX, P), np.float32)
    for h in range(H_FOX):
        select[h, h] = -1.0
    pos = np.where(tile < PT, tile * P + p, PAST + p).astype(np.float32)
    tables = []
    for size in (HEAD, D_IDX):
        half = size // 2
        inv = (10000.0 ** (-np.arange(half, dtype=np.float32) / np.float32(half)).astype(np.float64)).astype(np.float32)
        ang = (pos[:, :, None] * inv[None, None, :]).astype(np.float32).astype(np.float64)
        cos, sin = np.cos(ang).astype(np.float32), np.sin(ang).astype(np.float32)
        tables += [np.concatenate([cos, cos], 2).reshape(P, -1), np.concatenate([-sin, sin], 2).reshape(P, -1)]
    return {"consts": consts, "head_select": select.reshape(H_FOX, -1), "rope": np.concatenate(tables, 1).astype(np.float32)}


def kernel(**inputs):
    import numpy as np
    import concourse.bacc as bacc
    from concourse.bass_utils import run_bass_kernel_spmd

    nc = bacc.Bacc("TRN2", target_bir_lowering=False, num_devices=1)
    arrays = {name: np.ascontiguousarray(inputs[name]) for name in _INS}
    arrays.update(_constants())
    io = {}
    feed = {}
    for name, value in arrays.items():
        feed[f"in_{name}"] = value
        io[name] = nc.dram_tensor(f"in_{name}", value.shape, F32, kind="ExternalInput").ap()
    shapes = [(1, PROMPT, D), (1, SAMPLE, D)] + _row_shapes(PROMPT) + _row_shapes(SAMPLE)
    outs = [nc.dram_tensor(f"out_{i}", shape, F32, kind="ExternalOutput").ap() for i, shape in enumerate(shapes)]
    io["y_prompt"], io["y_sample"] = outs[0:2]
    (io["out_sb_k"], io["out_sb_v"], io["out_fox_k"], io["out_fox_v"], io["out_fox_logf"],
     io["out_dsa_k"], io["out_dsa_v"], io["out_dsa_idx"]) = [(outs[2 + i], outs[10 + i]) for i in range(8)]
    trunk_program(nc, io)
    r = run_bass_kernel_spmd(nc, [feed], core_ids=[0])
    return tuple(r.results[0][f"out_{i}"] for i in range(len(outs)))
```
